# Optimizing a Trainium2 kernel written in Bass

```python
import jax, jax.numpy as jnp
from jax import lax
import numpy as np

D_MODEL = 1024
BATCH = 1
SEQ = 512
DEPTH = 2

A_HEADS = 4
A_DK = 128
A_DV = 128
A_KD = A_HEADS * A_DK
A_WIDTH = A_HEADS * A_DV
A_CHUNK = 64
B_Q_HEADS = 8
B_KV_HEADS = 2
B_HEAD_DIM = 64
B_WIDTH = B_Q_HEADS * B_HEAD_DIM
B_KV_WIDTH = B_KV_HEADS * B_HEAD_DIM
WINDOW = 128
ROPE_DIM = B_HEAD_DIM // 4
ROPE_THETA = 500000.0
AB_IN_WIDTH = 2 * A_KD + 2 * A_WIDTH + B_WIDTH + 2 * B_KV_WIDTH
AB_OUT_WIDTH = A_WIDTH + B_WIDTH
POOL_WINDOWS = (2, 4, 8, 16)
POOL_GROUPS = 4
POOL_GROUP = D_MODEL // POOL_GROUPS
D_FF = 2816
CONV_WIDTH = 3
N_EVEN = (DEPTH + 1) // 2
N_ODD = DEPTH // 2
ALPHA = (2.0 * DEPTH) ** 0.25
BETA = (8.0 * DEPTH) ** -0.25
LN_EPS = 1e-5
RMS_EPS = 1e-6


F32 = jnp.float32

def _layer_norm(x, g, b):
    xf = x.astype(F32)
    mu = xf.mean(-1, keepdims=True)
    var = jnp.mean(jnp.square(xf - mu), -1, keepdims=True)
    return ((xf - mu) * lax.rsqrt(var + LN_EPS) * g + b).astype(x.dtype)

def _rope(x, cos, sin):
    half = ROPE_DIM // 2
    x1 = x[..., :half].astype(F32)
    x2 = x[..., half:ROPE_DIM].astype(F32)
    r1 = x1 * cos - x2 * sin
    r2 = x2 * cos + x1 * sin
    return jnp.concatenate([r1.astype(x.dtype), r2.astype(x.dtype), x[..., ROPE_DIM:]], -1)

def _hgrn2(q, fz, i, lb):
    Bn, T = q.shape[:2]
    fzf = fz.astype(F32)
    f = lb + (1.0 - lb) * jax.nn.sigmoid(fzf)
    logf = jnp.log(f)
    k = (1.0 - lb) * jax.nn.sigmoid(-fzf)
    nc = T // A_CHUNK

    def to_chunks(a):
        a = a.reshape(Bn, nc, A_CHUNK, A_HEADS, a.shape[-1])
        return a.transpose(1, 0, 3, 2, 4)

    qc, kc, vc, gc = (to_chunks(a) for a in (q.astype(F32), k, i.astype(F32), logf))
    causal = jnp.tril(jnp.ones((A_CHUNK, A_CHUNK), bool))[:, :, None]

    def step(S, inp):
        qb, kb, vb, gb = inp
        b = jnp.cumsum(gb, axis=2)
        o_inter = jnp.einsum('bhtk,bhkv->bhtv', qb * jnp.exp(b), S)
        diff = b[:, :, :, None, :] - b[:, :, None, :, :]
        decay = jnp.exp(jnp.where(causal, diff, -jnp.inf))
        att = jnp.einsum('bhtk,bhsk,bhtsk->bhts', qb, kb, decay)
        o = o_inter + jnp.einsum('bhts,bhsv->bhtv', att, vb)
        b_last = b[:, :, -1:, :]
        S = jnp.exp(b_last[:, :, 0])[..., None] * S + jnp.einsum(
            'bhsk,bhsv->bhkv', kb * jnp.exp(b_last - b), vb)
        return S, o

    S0 = jnp.zeros((Bn, A_HEADS, A_DK, A_DV), F32)
    _, o = lax.scan(step, S0, (qc, kc, vc, gc))
    return o.transpose(1, 0, 3, 2, 4).reshape(Bn, T, A_HEADS, A_DV)

def _swa(q, k, v, sinks):
    Bn, T = q.shape[:2]
    nb = T // WINDOW
    G = B_Q_HEADS // B_KV_HEADS
    qb = q.reshape(Bn, nb, WINDOW, B_KV_HEADS, G, B_HEAD_DIM)

    def band(a):
        a = a.reshape(Bn, nb, WINDOW, B_KV_HEADS, B_HEAD_DIM)
        prev = jnp.pad(a, ((0, 0), (1, 0), (0, 0), (0, 0), (0, 0)))[:, :-1]
        return jnp.concatenate([prev, a], axis=2)

    kb, vb = band(k), band(v)
    s = jnp.einsum('bnqhgd,bnkhd->bnhgqk', qb, kb).astype(F32) * (B_HEAD_DIM ** -0.5)
    qi = jnp.arange(WINDOW)[:, None] + WINDOW
    ki = jnp.arange(2 * WINDOW)[None, :]
    rel = qi - ki
    allowed = (rel >= 0) & (rel < WINDOW)
    blk = jnp.arange(nb)[:, None, None]
    valid = allowed[None] & ((blk > 0) | (ki[None] >= WINDOW))
    s = jnp.where(valid[None, :, None, None], s, -jnp.inf)
    sink = sinks.astype(F32).reshape(B_KV_HEADS, G)[None, None, :, :, None, None]
    m = jnp.maximum(s.max(-1, keepdims=True), sink)
    p = jnp.exp(s - m)
    p = p / (p.sum(-1, keepdims=True) + jnp.exp(sink - m))
    o = jnp.einsum('bnhgqk,bnkhd->bnqhgd', p.astype(v.dtype), vb)
    return o.reshape(Bn, T, B_WIDTH)

def _even_mixer(h, w_in, w_out, lb, norm_g, sinks, cos, sin):
    Bn, T, _ = h.shape
    z = h @ w_in
    widths = [A_KD, A_KD, A_WIDTH, A_WIDTH, B_WIDTH, B_KV_WIDTH, B_KV_WIDTH]
    idx = np.cumsum(widths)[:-1].tolist()
    aq, af, ai, ag, bq, bk, bv = jnp.split(z, idx, axis=-1)
    oa = _hgrn2(aq.reshape(Bn, T, A_HEADS, A_DK), af.reshape(Bn, T, A_HEADS, A_DK),
                ai.reshape(Bn, T, A_HEADS, A_DV), lb.reshape(A_HEADS, A_DK))
    oa = oa * lax.rsqrt(jnp.mean(oa * oa, -1, keepdims=True) + RMS_EPS) * norm_g
    oa = oa.reshape(Bn, T, A_WIDTH).astype(h.dtype) * jax.nn.silu(ag)
    q = _rope(bq.reshape(Bn, T, B_Q_HEADS, B_HEAD_DIM), cos, sin)
    k = _rope(bk.reshape(Bn, T, B_KV_HEADS, B_HEAD_DIM), cos, sin)
    v = bv.reshape(Bn, T, B_KV_HEADS, B_HEAD_DIM)
    ob = _swa(q, k, v, sinks).astype(h.dtype)
    return jnp.concatenate([oa, ob], axis=-1) @ w_out

def _pool_mixer(h, w_grp, scale):
    Bn, T, D = h.shape
    hf = h.astype(F32).reshape(Bn, T, POOL_GROUPS, POOL_GROUP)
    t = jnp.arange(T)
    outs = []
    for gi, w in enumerate(POOL_WINDOWS):
        xg = hf[:, :, gi]
        cs = jnp.cumsum(jnp.pad(xg, ((0, 0), (w, 0), (0, 0))), axis=1)
        win_sum = cs[:, w:] - cs[:, :T]
        cnt = jnp.minimum(t + 1, w).astype(F32)[None, :, None]
        outs.append(win_sum / cnt - xg)
    pooled = jnp.stack(outs, axis=2).astype(h.dtype)
    y = jnp.einsum('btgc,gcd->btgd', pooled, w_grp)
    return y.reshape(Bn, T, D) * scale

def _conv_ffn(h, w_up, conv_w, conv_b, w_down):
    T = h.shape[1]
    u, v = jnp.split(h @ w_up, 2, axis=-1)
    up = jnp.pad(u, ((0, 0), (CONV_WIDTH - 1, 0), (0, 0)))
    uc = conv_b
    for j in range(CONV_WIDTH):
        uc = uc + up[:, j:j + T] * conv_w[j]
    return (jax.nn.silu(uc) * v) @ w_down

def first_inputs(seed: int = 0) -> dict:
    key = jax.random.key(seed)
    ks = jax.random.split(key, 20)
    n = jax.random.normal
    D = D_MODEL
    x = n(ks[0], (BATCH, SEQ, D), F32)
    c = n(ks[1], (BATCH, D), F32)
    offs = jax.random.randint(ks[2], (BATCH, 1), 0, 4096, dtype=jnp.int32)
    positions = offs + jnp.arange(SEQ, dtype=jnp.int32)[None, :]
    ada_w = n(ks[3], (DEPTH, D, 6 * D), F32) * D ** -0.5
    ada_b = 0.02 * n(ks[4], (DEPTH, 6 * D), F32)
    ln_g = 1.0 + 0.02 * n(ks[5], (DEPTH, 2, D), F32)
    ln_b = 0.02 * n(ks[6], (DEPTH, 2, D), F32)
    ab_w_in = n(ks[7], (N_EVEN, D, AB_IN_WIDTH), F32) * D ** -0.5
    ab_w_out = n(ks[8], (N_EVEN, AB_OUT_WIDTH, D), F32) * (AB_OUT_WIDTH ** -0.5 * BETA)
    hgrn_lb_raw = 0.5 * n(ks[9], (N_EVEN, A_KD), F32)
    hgrn_norm_g = 1.0 + 0.02 * n(ks[10], (N_EVEN, A_DV), F32)
    attn_sinks = 0.5 * n(ks[11], (N_EVEN, B_Q_HEADS), F32)
    pool_w = n(ks[12], (N_ODD, POOL_GROUPS, POOL_GROUP, POOL_GROUP), F32) * (POOL_GROUP ** -0.5 * BETA)
    pool_scale = 1.0 + 0.02 * n(ks[13], (N_ODD, D), F32)
    ffn_w_up = n(ks[14], (DEPTH, D, 2 * D_FF), F32) * D ** -0.5
    ffn_conv_w = n(ks[15], (DEPTH, CONV_WIDTH, D_FF), F32) * CONV_WIDTH ** -0.5
    ffn_conv_b = 0.02 * n(ks[16], (DEPTH, D_FF), F32)
    ffn_w_down = n(ks[17], (DEPTH, D_FF, D), F32) * (D_FF ** -0.5 * BETA)
    return {"x": x, "c": c, "positions": positions, "ada_w": ada_w, "ada_b": ada_b,
            "ln_g": ln_g, "ln_b": ln_b, "ab_w_in": ab_w_in, "ab_w_out": ab_w_out,
            "hgrn_lb_raw": hgrn_lb_raw, "hgrn_norm_g": hgrn_norm_g, "attn_sinks": attn_sinks,
            "pool_w": pool_w, "pool_scale": pool_scale, "ffn_w_up": ffn_w_up,
            "ffn_conv_w": ffn_conv_w, "ffn_conv_b": ffn_conv_b, "ffn_w_down": ffn_w_down}

def first_block(x, c, positions, ada_w, ada_b, ln_g, ln_b, ab_w_in, ab_w_out,
              hgrn_lb_raw, hgrn_norm_g, attn_sinks, pool_w, pool_scale,
              ffn_w_up, ffn_conv_w, ffn_conv_b, ffn_w_down):
    lb_p = jax.nn.softmax(hgrn_lb_raw.astype(F32), axis=0)
    lower_bounds = jnp.cumsum(lb_p, axis=0) - lb_p[0]
    inv_freq = ROPE_THETA ** (-jnp.arange(0, ROPE_DIM, 2, dtype=F32) / ROPE_DIM)
    ang = positions.astype(F32)[..., None] * inv_freq
    cos = jnp.cos(ang)[:, :, None, :]
    sin = jnp.sin(ang)[:, :, None, :]
    c_act = jax.nn.silu(c)
    for l in range(DEPTH):
        mod = c_act @ ada_w[l] + ada_b[l]
        sh1, sc1, g1, sh2, sc2, g2 = [m[:, None, :] for m in jnp.split(mod, 6, axis=-1)]
        h = x * (1.0 + sc1) + sh1
        if l % 2 == 0:
            e = l // 2
            y = _even_mixer(h, ab_w_in[e], ab_w_out[e], lower_bounds[e], hgrn_norm_g[e],
                            attn_sinks[e], cos, sin)
        else:
            o = l // 2
            y = _pool_mixer(h, pool_w[o], pool_scale[o])
        x = _layer_norm(ALPHA * x + g1 * y, ln_g[l, 0], ln_b[l, 0])
        h = x * (1.0 + sc2) + sh2
        y = _conv_ffn(h, ffn_w_up[l], ffn_conv_w[l], ffn_conv_b[l], ffn_w_down[l])
        x = _layer_norm(ALPHA * x + g2 * y, ln_g[l, 1], ln_b[l, 1])
    return x


CTX_LEN = 256
GRID_W = 64
N_EVEN_2 = (DEPTH + 1) // 2
N_ODD_2 = DEPTH // 2
N_MOD = 6
EPS = 1e-6

MIX_WIDTH = D_MODEL
FOURIER_WIDTH = MIX_WIDTH // 2
FOURIER_GROUPS = 4
FOURIER_GROUP_DIM = FOURIER_WIDTH // FOURIER_GROUPS
GLA_HEADS = 4
GLA_VAL_WIDTH = MIX_WIDTH - FOURIER_WIDTH
GLA_DV = GLA_VAL_WIDTH // GLA_HEADS
GLA_DK = GLA_DV // 2
GLA_KEY_WIDTH = GLA_HEADS * GLA_DK
GLA_GATE_RANK = 16
GLA_GATE_TEMP = 16.0
GLA_CHUNK = 64
EVEN_SPLITS = [FOURIER_WIDTH,
               FOURIER_WIDTH + GLA_KEY_WIDTH,
               FOURIER_WIDTH + 2 * GLA_KEY_WIDTH,
               FOURIER_WIDTH + 2 * GLA_KEY_WIDTH + GLA_VAL_WIDTH,
               FOURIER_WIDTH + 2 * GLA_KEY_WIDTH + 2 * GLA_VAL_WIDTH]
EVEN_IN_WIDTH = EVEN_SPLITS[-1] + GLA_GATE_RANK

HEAD_DIM = 128
ATT_HEADS = D_MODEL // HEAD_DIM
ATT_KV_HEADS = 2
ATT_GROUP = ATT_HEADS // ATT_KV_HEADS
Q_WIDTH = ATT_HEADS * HEAD_DIM
QKV_WIDTH = (ATT_HEADS + 2 * ATT_KV_HEADS) * HEAD_DIM
Q_BLOCK = 128
ROPE_THETA_2 = 10000.0
ROPE_AXIS_DIM = HEAD_DIM // 2

D_FF_2 = ((8 * D_MODEL // 3 + 255) // 256) * 256
CONV_W = 3


def rms_norm(x, g):
    xf = x.astype(jnp.float32)
    y = xf * lax.rsqrt(jnp.mean(xf * xf, axis=-1, keepdims=True) + EPS)
    return (y * g.astype(jnp.float32)).astype(x.dtype)

def adaln(cv, w, b):
    m = jax.nn.silu(cv) @ w + b
    m = m.reshape(cv.shape[:-1] + (1, N_MOD, D_MODEL))
    return [m[..., k, :] for k in range(N_MOD)]

def dwconv_centred(x, w, b):
    L = x.shape[1]
    pad = CONV_W // 2
    xp = jnp.pad(x, ((0, 0), (pad, CONV_W - 1 - pad), (0, 0)))
    out = b
    for k in range(CONV_W):
        out = out + xp[:, k:k + L] * w[k]
    return out

def conv_ffn(h, w_up, w_conv, b_conv, w_down):
    u = dwconv_centred(h @ w_up, w_conv, b_conv)
    g, v = jnp.split(u, 2, axis=-1)
    return (jax.nn.silu(g) * v) @ w_down

def fourier_mix(u):
    B_, L, _ = u.shape
    ug = u.reshape(B_, L, FOURIER_GROUPS, FOURIER_GROUP_DIM).astype(jnp.float32)
    f = jnp.fft.fft2(ug, axes=(1, 3), norm='ortho').real
    return f.reshape(B_, L, FOURIER_WIDTH).astype(u.dtype)

def gla_scan(q, k, v, loga, s0):
    q, k, v = (t.astype(jnp.float32) for t in (q, k, v))
    B_, H, L, _ = q.shape
    n = L // GLA_CHUNK

    def to_chunks(t):
        return jnp.moveaxis(t.reshape(B_, H, n, GLA_CHUNK, t.shape[-1]), 2, 0)

    mask = jnp.tril(jnp.ones((GLA_CHUNK, GLA_CHUNK), bool))[:, :, None]

    def step(S, inp):
        qc, kc, vc, ac = inp
        b = jnp.cumsum(ac, axis=2)
        diff = b[:, :, :, None, :] - b[:, :, None, :, :]
        decay = jnp.exp(jnp.where(mask, diff, -jnp.inf))
        attn = jnp.einsum('bhid,bhjd,bhijd->bhij', qc, kc, decay)
        o = attn @ vc + jnp.einsum('bhid,bhde->bhie', qc * jnp.exp(b), S)
        b_last = b[:, :, -1:, :]
        S_new = (jnp.exp(b_last[:, :, 0, :, None]) * S
                 + jnp.einsum('bhjd,bhje->bhde', kc * jnp.exp(b_last - b), vc))
        return S_new, o

    s_fin, o = lax.scan(step, s0, (to_chunks(q), to_chunks(k), to_chunks(v), to_chunks(loga)))
    o = jnp.moveaxis(o, 0, 2).reshape(B_, H, L, v.shape[-1])
    return o, s_fin

def even_mix(h, s_f, s_b, w_in, w_gate, b_gate, g_gla, w_out):
    B_, L, _ = h.shape
    p = h @ w_in
    u_f, q, k, v, r, z = jnp.split(p, EVEN_SPLITS, axis=-1)

    def heads(t, d):
        return t.reshape(B_, L, GLA_HEADS, d).transpose(0, 2, 1, 3)

    q = heads(q, GLA_DK) * (GLA_DK ** -0.5)
    k = heads(k, GLA_DK)
    v = heads(v, GLA_DV)
    zf = z.astype(jnp.float32)
    loga = [heads(jax.nn.log_sigmoid(zf @ w_gate[d].astype(jnp.float32) + b_gate[d].astype(jnp.float32))
                  / GLA_GATE_TEMP, GLA_DK) for d in range(2)]

    def flip(t):
        return jnp.flip(t, axis=2)

    o_f, s_f = gla_scan(q, k, v, loga[0], s_f)
    o_b, s_b = gla_scan(flip(q), flip(k), flip(v), flip(loga[1]), s_b)
    o = o_f + flip(o_b)
    o = o * lax.rsqrt(jnp.mean(o * o, axis=-1, keepdims=True) + EPS)
    o = o.transpose(0, 2, 1, 3).reshape(B_, L, GLA_VAL_WIDTH) * g_gla.astype(jnp.float32)
    o = (o * jax.nn.silu(r.astype(jnp.float32))).astype(h.dtype)
    y = jnp.concatenate([fourier_mix(u_f), o], axis=-1) @ w_out
    return y, s_f, s_b

def axial_rope_tables(n_tokens):
    rows = n_tokens // GRID_W
    r, c = jnp.meshgrid(jnp.arange(rows), jnp.arange(GRID_W), indexing='ij')
    inv = ROPE_THETA_2 ** (-jnp.arange(0, ROPE_AXIS_DIM, 2, dtype=jnp.float32) / ROPE_AXIS_DIM)
    ang = jnp.concatenate([r.reshape(-1, 1).astype(jnp.float32) * inv,
                           c.reshape(-1, 1).astype(jnp.float32) * inv], axis=-1)
    return jnp.cos(ang), jnp.sin(ang)

def apply_rope(t, cos, sin):
    tf = t.astype(jnp.float32)
    t1, t2 = jnp.split(tf, 2, axis=-1)
    return jnp.concatenate([t1 * cos - t2 * sin, t1 * sin + t2 * cos], axis=-1).astype(t.dtype)

def attn_q(h, w_q, g_q):
    B_, L, _ = h.shape
    q = rms_norm((h @ w_q).reshape(B_, L, ATT_HEADS, HEAD_DIM), g_q)
    return q.transpose(0, 2, 1, 3)

def attn_kv(h, w_kv, g_k):
    B_, L, _ = h.shape
    kv = (h @ w_kv).reshape(B_, L, 2, ATT_KV_HEADS, HEAD_DIM)
    k = rms_norm(kv[:, :, 0], g_k).transpose(0, 2, 1, 3)
    v = kv[:, :, 1].transpose(0, 2, 1, 3)
    return k, v

def grouped_attend(q, k, v):
    s = jnp.einsum('bkgqd,bksd->bkgqs', q, k).astype(jnp.float32) * (HEAD_DIM ** -0.5)
    p = jax.nn.softmax(s, axis=-1).astype(v.dtype)
    return jnp.einsum('bkgqs,bksd->bkgqd', p, v)

def second_inputs(seed: int = 0) -> dict:
    key = jax.random.key(seed)
    ks = jax.random.split(key, 22)
    f32 = jnp.float32

    def nrm(k, shape, scale):
        return jax.random.normal(k, shape, f32) * scale

    def gain(k, shape):
        return 1.0 + 0.02 * jax.random.normal(k, shape, f32)

    return {
        'x': nrm(ks[0], (BATCH, SEQ, D_MODEL), 1.0),
        'c': nrm(ks[1], (BATCH, D_MODEL), 1.0),
        'ctx': nrm(ks[2], (BATCH, CTX_LEN, D_MODEL), 1.0),
        'c_ctx': nrm(ks[3], (D_MODEL,), 1.0),
        'w_mod': nrm(ks[4], (DEPTH, D_MODEL, N_MOD * D_MODEL), D_MODEL ** -0.5),
        'b_mod': nrm(ks[5], (DEPTH, N_MOD * D_MODEL), 0.02),
        'g_norm_mix': gain(ks[6], (DEPTH, D_MODEL)),
        'g_norm_ffn': gain(ks[7], (DEPTH, D_MODEL)),
        'g_norm_final': gain(ks[8], (D_MODEL,)),
        'w_even_in': nrm(ks[9], (N_EVEN_2, D_MODEL, EVEN_IN_WIDTH), D_MODEL ** -0.5),
        'w_gla_gate': nrm(ks[10], (N_EVEN_2, 2, GLA_GATE_RANK, GLA_KEY_WIDTH), GLA_GATE_RANK ** -0.5),
        'b_gla_gate': nrm(ks[11], (N_EVEN_2, 2, GLA_KEY_WIDTH), 0.1),
        'g_gla_out': gain(ks[12], (N_EVEN_2, GLA_VAL_WIDTH)),
        'w_even_out': nrm(ks[13], (N_EVEN_2, MIX_WIDTH, D_MODEL), MIX_WIDTH ** -0.5),
        'w_qkv': nrm(ks[14], (N_ODD_2, D_MODEL, QKV_WIDTH), D_MODEL ** -0.5),
        'g_q': gain(ks[15], (N_ODD_2, HEAD_DIM)),
        'g_k': gain(ks[16], (N_ODD_2, HEAD_DIM)),
        'w_att_out': nrm(ks[17], (N_ODD_2, Q_WIDTH, D_MODEL), Q_WIDTH ** -0.5),
        'w_ffn_up': nrm(ks[18], (DEPTH, D_MODEL, 2 * D_FF_2), D_MODEL ** -0.5),
        'w_ffn_conv': nrm(ks[19], (DEPTH, CONV_W, 2 * D_FF_2), CONV_W ** -0.5),
        'b_ffn_conv': nrm(ks[20], (DEPTH, 2 * D_FF_2), 0.02),
        'w_ffn_down': nrm(ks[21], (DEPTH, D_FF_2, D_MODEL), D_FF_2 ** -0.5),
    }

def second_block(x, c, ctx, c_ctx, w_mod, b_mod, g_norm_mix, g_norm_ffn, g_norm_final,
              w_even_in, w_gla_gate, b_gla_gate, g_gla_out, w_even_out,
              w_qkv, g_q, g_k, w_att_out,
              w_ffn_up, w_ffn_conv, b_ffn_conv, w_ffn_down):
    B_, S, _ = x.shape
    cos, sin = axial_rope_tables(S)
    h_lat, h_ctx = x, ctx
    for i in range(DEPTH):
        last = i == DEPTH - 1
        j = i // 2
        sh1, sc1, ga1, sh2, sc2, ga2 = adaln(c, w_mod[i], b_mod[i])
        csh1, csc1, cga1, csh2, csc2, cga2 = adaln(c_ctx, w_mod[i], b_mod[i])
        a_lat = rms_norm(h_lat, g_norm_mix[i]) * (1 + sc1) + sh1
        a_ctx = rms_norm(h_ctx, g_norm_mix[i]) * (1 + csc1) + csh1
        if i % 2 == 0:
            zero = jnp.zeros((B_, GLA_HEADS, GLA_DK, GLA_DV), jnp.float32)
            o_ctx, s_f, s_b = even_mix(a_ctx, zero, zero, w_even_in[j], w_gla_gate[j],
                                       b_gla_gate[j], g_gla_out[j], w_even_out[j])
            o_lat, _, _ = even_mix(a_lat, s_f, s_b, w_even_in[j], w_gla_gate[j],
                                   b_gla_gate[j], g_gla_out[j], w_even_out[j])
        else:
            w_q = w_qkv[j][:, :Q_WIDTH]
            w_kv = w_qkv[j][:, Q_WIDTH:]
            q_l = apply_rope(attn_q(a_lat, w_q, g_q[j]), cos, sin)
            k_l, v_l = attn_kv(a_lat, w_kv, g_k[j])
            k_l = apply_rope(k_l, cos, sin)
            k_c, v_c = attn_kv(a_ctx, w_kv, g_k[j])
            k_all = jnp.concatenate([k_c, k_l], axis=2)
            v_all = jnp.concatenate([v_c, v_l], axis=2)
            nb = S // Q_BLOCK
            qb = jnp.moveaxis(q_l.reshape(B_, ATT_KV_HEADS, ATT_GROUP, nb, Q_BLOCK, HEAD_DIM), 3, 0)
            ob = lax.map(lambda blk: grouped_attend(blk, k_all, v_all), qb)
            o_lat = ob.transpose(1, 0, 4, 2, 3, 5).reshape(B_, S, Q_WIDTH) @ w_att_out[j]
            if not last:
                Lc = a_ctx.shape[1]
                q_c = attn_q(a_ctx, w_q, g_q[j]).reshape(B_, ATT_KV_HEADS, ATT_GROUP, Lc, HEAD_DIM)
                o_c = grouped_attend(q_c, k_c, v_c)
                o_ctx = o_c.transpose(0, 3, 1, 2, 4).reshape(B_, Lc, Q_WIDTH) @ w_att_out[j]
        h_lat = h_lat + ga1 * o_lat
        f_lat = rms_norm(h_lat, g_norm_ffn[i]) * (1 + sc2) + sh2
        h_lat = h_lat + ga2 * conv_ffn(f_lat, w_ffn_up[i], w_ffn_conv[i], b_ffn_conv[i], w_ffn_down[i])
        if not last:
            h_ctx = h_ctx + cga1 * o_ctx
            f_ctx = rms_norm(h_ctx, g_norm_ffn[i]) * (1 + csc2) + csh2
            h_ctx = h_ctx + cga2 * conv_ffn(f_ctx, w_ffn_up[i], w_ffn_conv[i], b_ffn_conv[i], w_ffn_down[i])
    return rms_norm(h_lat, g_norm_final)


def setup_inputs(seed=0):
    out = dict(first_inputs(seed))
    for name, value in second_inputs(seed + 1).items():
        if name != "x":
            out[name + "_2"] = value
    return out


def reference(
    x, c, positions, ada_w, ada_b, ln_g, ln_b, ab_w_in, ab_w_out, hgrn_lb_raw, hgrn_norm_g,
    attn_sinks, pool_w, pool_scale, ffn_w_up, ffn_conv_w, ffn_conv_b, ffn_w_down, c_2, ctx_2,
    c_ctx_2, w_mod_2, b_mod_2, g_norm_mix_2, g_norm_ffn_2, g_norm_final_2, w_even_in_2,
    w_gla_gate_2, b_gla_gate_2, g_gla_out_2, w_even_out_2, w_qkv_2, g_q_2, g_k_2, w_att_out_2,
    w_ffn_up_2, w_ffn_conv_2, b_ffn_conv_2, w_ffn_down_2,
):
    x = first_block(
        x, c, positions, ada_w, ada_b, ln_g, ln_b, ab_w_in, ab_w_out, hgrn_lb_raw, hgrn_norm_g,
        attn_sinks, pool_w, pool_scale, ffn_w_up, ffn_conv_w, ffn_conv_b, ffn_w_down,
    )
    return second_block(
        x, c_2, ctx_2, c_ctx_2, w_mod_2, b_mod_2, g_norm_mix_2, g_norm_ffn_2, g_norm_final_2,
        w_even_in_2, w_gla_gate_2, b_gla_gate_2, g_gla_out_2, w_even_out_2, w_qkv_2, g_q_2,
        g_k_2, w_att_out_2, w_ffn_up_2, w_ffn_conv_2, b_ffn_conv_2, w_ffn_down_2,
    )


_drawn_inputs = setup_inputs


def setup_inputs(seed=0):
    import zlib

    import numpy as np

    out = dict(_drawn_inputs(seed))
    spreads = {}
    factors = {'hgrn_norm_g': 8.0,
     'attn_sinks': 8.0,
     'pool_scale': 8.0,
     'ffn_conv_b': 8.0,
     'g_norm_mix_2': 3.739,
     'g_norm_ffn_2': 3.175,
     'g_norm_final_2': 2.723,
     'g_gla_out_2': 7.183,
     'g_q_2': 8.0,
     'g_k_2': 8.0,
     'b_ffn_conv_2': 3.739}
    for name, (base, spread) in spreads.items():
        noise = np.random.default_rng([zlib.crc32(name.encode()), seed]).standard_normal(out[name].shape)
        drawn = base * np.exp(spread * noise) if base else spread * noise
        out[name] = __import__('jax').numpy.asarray(drawn.astype(out[name].dtype))
    for name, factor in factors.items():
        out[name] = (out[name] * factor).astype(out[name].dtype)
    return out
```

```python
from contextlib import ExitStack, contextmanager

import numpy as np

import concourse.bass as bass
from concourse import mybir

F32 = mybir.dt.float32
F32R = mybir.dt.float32r
I32 = mybir.dt.int32
U8 = mybir.dt.uint8
ALU = mybir.AluOpType
ACT = mybir.ActivationFunctionType
AX = mybir.AxisListType

P = 128
D = 1024
KD = D // P
CTX, LAT = 256, 512
TALL = CTX + LAT
CHUNK = 128
LEVELS = 7
F_FF = 2816
FT = F_FF // P
FG = FT // 2
NMOD = 6 * KD
JW = 192
JOBS = 6 * D // JW
SEG_OF = {1: 0, 2: 1}
BANK = 512
ALPHA = 4.0 ** 0.25
LN_EPS, RMS_EPS, EPS = 1e-5, 1e-6, 1e-6
NEG = -1.0e30
TWO_PI = 2.0 * np.pi
LATS = slice(CTX, TALL)
HEAD_ORDER = [0, 2, 4, 6, 1, 3, 5, 7]


class Ticket:

    def __init__(self, counter, value, loop):
        self.counter, self.value, self.loop = counter, value, loop


class Counter:
    def __init__(self, name, sem):
        self.name, self.sem, self.value = name, sem, 0


class Loop:
    def __init__(self, index, count, strides):
        self.index, self.count, self.strides, self.closed = index, count, strides, False


class Program:

    def __init__(self, nc, ctx):
        self.nc, self.loop, self.waited = nc, None, {}
        self.engines = {"pe": nc.tensor, "act": nc.scalar, "dve": nc.vector, "pool": nc.gpsimd, "sp": nc.sync}
        self.counters = {}
        for name in ("pe", "act", "dve", "pool", "w0", "w1", "m0", "m1", "load", "store", "r0", "r1", "turn"):
            self.counters[name] = Counter(name, ctx.enter_context(nc.semaphore(f"done_{name}")))

    def wait(self, engine, *tickets):
        due = []
        for t in tickets:
            if t is None:
                continue
            value = t.value
            if t.loop is not None and t.loop.closed:
                value += (t.loop.count - 1) * t.loop.strides.get(t.counter.name, 0)
            inside = t.loop is not None and not t.loop.closed
            key = (engine, t.counter.name, inside)
            if self.waited.get(key, -1) >= value:
                continue
            self.waited[key] = value
            if inside:
                value = self.engines[engine].snap(value + t.loop.index * t.loop.strides.get(t.counter.name, 0))
            due.append((t.counter.sem, value))
        for sem, value in due:
            self.engines[engine].wait_ge(sem, value)

    def previous(self, t):
        return Ticket(t.counter, t.value - t.loop.strides[t.counter.name], t.loop)

    def done(self, name, instruction, step=1):
        c = self.counters[name]
        instruction.then_inc(c.sem, step)
        c.value += step
        return Ticket(c, c.value, self.loop)

    def at(self, name):
        return Ticket(self.counters[name], self.counters[name].value, self.loop)

    def pe(self, instruction):
        return self.done("pe", instruction)

    def act(self, instruction):
        return self.done("act", instruction)

    def dve(self, instruction):
        return self.done("dve", instruction)

    def pool(self, instruction):
        return self.done("pool", instruction)

    @contextmanager
    def repeat(self, count, **strides):
        start = {k: c.value for k, c in self.counters.items()}
        self.waited = {}
        with self.nc.Fori(0, count) as i:
            loop = self.loop = Loop(i, count, strides)
            yield i
        made = {k: c.value - start[k] for k, c in self.counters.items() if c.value != start[k]}
        assert made == strides, f"a pass of this loop adds {made}"
        loop.closed, self.loop, self.waited = True, None, {}
        for k, n in strides.items():
            self.counters[k].value += (count - 1) * n


class Kernel:
    def __init__(self, nc, ctx, ins, out):
        self.nc, self.ins, self.out = nc, ins, out
        self.p = Program(nc, ctx)
        self.slot = 0
        self.free_w = [None, None]
        self.free_hl = [None, None]
        self.free_ps = [[], []]
        sb = lambda name, shape, dt=F32: ctx.enter_context(nc.sbuf_tensor(name, shape, dt))
        self.x = sb("x", [P, KD, TALL])
        self.h_hi = sb("h_hi", [P, KD, TALL], F32R)
        self.h_lo = sb("h_lo", [P, KD, TALL], F32R)
        self.w_raw = [sb(f"w_raw{i}", [P, FG * P]) for i in range(2)]
        self.w_hi = [sb(f"w_hi{i}", [P, FG * P], F32R) for i in range(2)]
        self.w_lo = [sb(f"w_lo{i}", [P, FG * P], F32R) for i in range(2)]
        self.ones = sb("ones", [P, P])
        self.ident = sb("ident", [P, P])
        self.mods1 = sb("mods1", [P, 2, NMOD])
        self.mods2 = sb("mods2", [P, 2, NMOD, 2])
        self.small = sb("small", [P, SMALL_COLS])
        self.mean = sb("mean", [P, LAT])
        self.rstd = sb("rstd", [P, TALL])
        self.gain = sb("gain", [P, 2, KD])
        self.c_act = sb("c_act", [P, 3 * KD])
        self.turn = sb("turn", [NMOD, 2, P])
        self.rows = nc.dram_tensor("mod_rows", (4, 2, 6 * D), F32, kind="Internal").ap()
        self.modulations_done = []
        self.turn_read = self.columns_read = None
        self.tmp = [sb(f"tmp{i}", [P, LAT]) for i in range(2)]
        self.ps = ctx.enter_context(nc.psum_tensor("ps", [P, 8, BANK], F32))
        self.x_done = self.h_done = self.gain_read = self.bank_free = self.mods_made = None
        self.x_tile, self.sq_free, self.tmp_free = [None] * KD, [None, None], [None, None]

    def col(self, name, i=0, n=1):
        at = SMALL[name][0] + i
        return self.small[:, at:at + n]

    def load(self, dst, src, *after):
        p = self.p
        p.wait("sp", *after)
        return p.done("load", self.nc.sync.dma_start(dst, src), 16)


def _small_table():
    sizes = [("c1", 8), ("cc2", 8), ("c2", 8), ("ada_b", 96), ("mod_b", 96), ("ln_g", 32), ("ln_b", 32),
             ("lb_raw", 4), ("norm_g", 1), ("pool_scale", 8), ("fcw", 2 * 3 * FT), ("fcb", 2 * FT),
             ("gmix", 16), ("gffn", 16), ("gfin", 8), ("bgate", 4), ("ggla", 4), ("gq", 1), ("gk", 1),
             ("cw2", 2 * 3 * 2 * FT), ("cb2", 2 * 2 * FT), ("inv_freq", 1), ("sinks", 8)]
    table, at = {}, 0
    for name, n in sizes:
        table[name] = (at, n)
        at += n
    return table, at


SMALL, SMALL_COLS = _small_table()


def segments(tokens):
    both = [(0, CTX, 0), (CTX, LAT, 1)]
    return both if tokens == TALL else both[1:]


class Stream:

    def __init__(self, k, name, first, count, kt, hi, lo, tokens, token_major=False):
        self.k, self.source, self.first, self.count, self.kt = k, k.ins[name], first, count, kt
        self.hi, self.lo, self.tokens, self.token_major = hi, lo, tokens, token_major
        self.kept = {}
        self.jobs = None

    def dram(self, n):
        if isinstance(n, int):
            return self.source[n + self.first, :, :]
        return self.source[bass.ds(n, 1), :, :].rearrange("o p c -> (o p) c")

    def host(self, jobs):
        self.jobs, self.job0, self.pending = jobs, 1 if self.count > KD else 0, False
        jobs.start(self.k.slot if self.job0 == 0 else 1 - self.k.slot)
        return self

    def hosted(self, n):
        return not isinstance(n, int) or self.job0 <= n < self.job0 + self.jobs.count

    def fetch(self, n, where):
        k, p = self.k, self.k.p
        s = where
        tile = n if isinstance(n, int) else k.nc.sync.snap(n + self.first)
        p.wait("sp", k.free_w[s])
        cols = self.kt * P
        return p.done(f"w{s}", k.nc.sync.dma_start(k.w_raw[s][:, 0:cols], self.dram(tile)), 16)

    def split(self, s, loaded):
        k, p = self.k, self.k.p
        cols = self.kt * P
        raw, hi, lo = (t[s][:, 0:cols] for t in (k.w_raw, k.w_hi, k.w_lo))
        p.wait("act", loaded, k.free_hl[s])
        high = p.act(k.nc.scalar.activation(hi, raw, ACT.Copy))
        p.wait("dve", high)
        low = p.dve(k.nc.vector.tensor_tensor(lo, raw, hi.bitcast(F32), ALU.subtract))
        k.free_w[s] = low
        return low

    def product(self, s, low, ps):
        k, p, nc = self.k, self.k.p, self.k.nc
        p.wait("pe", low, *k.free_ps[s], *self.ready)
        wh = k.w_hi[s][:, 0:self.kt * P].rearrange("p (k n) -> p k n", n=P)
        wl = k.w_lo[s][:, 0:self.kt * P].rearrange("p (k n) -> p k n", n=P)
        if self.token_major:
            first = 0 if self.tokens == TALL else CTX
            for t in range(self.tokens // P):
                out = ps[:, t // 4, (t % 4) * P:(t % 4 + 1) * P]
                at = slice(first + t * P, first + (t + 1) * P)
                for c in range(self.kt):
                    for n, (a, b) in enumerate(((self.hi, wh), (self.lo, wh), (self.hi, wl))):
                        last = nc.tensor.matmul(out, a[:, c, at], b[:, c, :], start=c == 0 and n == 0,
                                                stop=c == self.kt - 1 and n == 2)
        else:
            for c in range(self.kt):
                for n, (a, b) in enumerate(((wh, self.hi), (wh, self.lo), (wl, self.hi))):
                    for t0, tn, bank in segments(self.tokens):
                        t0 -= TALL - b.shape[2]
                        last = nc.tensor.matmul(ps[:, bank, 0:tn], a[:, c, :], b[:, c, t0:t0 + tn],
                                                start=c == 0 and n == 0, stop=c == self.kt - 1 and n == 2)
        product = p.pe(last)
        k.free_hl[s] = product
        return product

    def step(self, n, s, consume, has_next, has_fetch):
        k, p = self.k, self.k.p
        ps = k.ps[:, 2 * s:2 * s + 2, :]
        product = self.product(s, self.low[s], ps)
        if has_next:
            self.low[1 - s] = self.split(1 - s, self.loaded[1 - s])
        if has_fetch:
            self.loaded[1 - s] = self.fetch(n + 3, 1 - s)
        k.free_ps[s] = list(consume(n, s, ps, product))
        self.ready = ()
        if self.jobs is not None:
            j = n - self.job0
            if self.pending:
                self.jobs.reduce(j - 1, 1 - s)
            self.pending = self.hosted(n)
            if self.pending:
                self.jobs.compute(j, s)

    def start(self, *ready):
        k = self.k
        self.ready = ready
        self.loaded, self.low = [None, None], [None, None]
        s = self.s0 = k.slot
        self.loaded[s] = self.fetch(0, s)
        self.loaded[1 - s] = self.fetch(1, 1 - s) if self.count > 1 else None
        self.low[s] = self.split(s, self.loaded[s])
        self.loaded[s] = self.fetch(2, s) if self.count > 2 else None

    def run(self, consume, **strides):
        k, p = self.k, self.k.p
        s0, count = self.s0, self.count
        total = {"pe": 2, "act": 2, "dve": 2, "w0": 16, "w1": 16}
        if self.jobs is not None:
            nv = len(self.jobs.vectors)
            for name, n in (("pe", 2), ("act", 2), ("dve", 2 * nv * KD), ("m0", 16), ("m1", 16), ("r0", 16), ("r1", 16)):
                total[name] = total.get(name, 0) + n
        for name, n in strides.items():
            total[name] = total.get(name, 0) + n

        def tiles(ns):
            for n in ns:
                self.step(n, s0 if n % 2 == 0 else 1 - s0, consume, n + 1 < count, n + 3 < count)

        passes = (count - 2 - 3) // 2
        if passes < 2:
            tiles(range(count))
        else:
            tiles(range(2))
            with p.repeat(passes, **total) as i:
                carry = lambda t: t and Ticket(t.counter, t.value, p.loop)
                k.free_hl = [carry(t) for t in k.free_hl]
                k.free_w = [carry(t) for t in k.free_w]
                k.free_ps = [[carry(t) for t in ts] for ts in k.free_ps]
                self.low = [carry(t) for t in self.low]
                self.loaded = [carry(t) for t in self.loaded]
                self.kept = {name: carry(t) for name, t in self.kept.items()}
                if self.jobs is not None:
                    self.jobs.kept = {name: carry(t) for name, t in self.jobs.kept.items()}
                    self.jobs.made = carry(self.jobs.made)
                for u in range(2):
                    self.step(i * 2 + (2 + u), s0 if u == 0 else 1 - s0, consume, True, True)
            tiles(range(2 + 2 * passes, count))
        if self.jobs is not None:
            if self.pending:
                self.jobs.reduce(count - 1 - self.job0, s0 if count % 2 else 1 - s0)
            k.modulations_done = self.jobs.read_all()
        k.slot = s0 if count % 2 == 0 else 1 - s0


class Space:

    def __init__(self, k, ctx, name):
        sb = lambda n, shape: ctx.enter_context(k.nc.sbuf_tensor(f"{n}_{name}", shape, F32))
        self.k = k
        self.raw = [sb(f"m_raw{s}", [P, KD, JW]) for s in range(2)]
        self.acc = [sb(f"m_acc{s}", [P, 2, JW]) for s in range(2)]
        self.row = [sb(f"m_row{s}", [1, 2, JW]) for s in range(2)]


class Modulations:

    def __init__(self, space, block, layer, first, count, vectors):
        k = space.k
        self.k, self.block, self.layer, self.first, self.count, self.vectors = k, block, layer, first, count, vectors
        nv = len(vectors)
        self.raw = space.raw
        self.acc, self.row = ([t[:, 0:nv, :] for t in ts] for ts in (space.acc, space.row))
        self.kept = {"stored0": k.p.at("r0"), "stored1": k.p.at("r1")}
        self.after = list(k.modulations_done)

    def fetch(self, j, s, *after):
        k, p = self.k, self.k.p
        first = (self.layer * JOBS) + self.first
        src = k.ins["ada_w" if self.block == 0 else "w_mod"]
        if isinstance(j, int):
            at = src[first + j, :, :]
        else:
            at = src[bass.ds(k.nc.sync.snap(j + first), 1), :, :].rearrange("o p c -> (o p) c")
        p.wait("sp", *after)
        self.kept[f"loaded{s}"] = p.done(f"m{s}", k.nc.sync.dma_start(
            self.raw[s][:, :, :].rearrange("p k n -> p (k n)"), at), 16)

    def start(self, s0, *after):
        self.fetch(0, s0, *self.after, *after)
        self.fetch(1, 1 - s0)

    def compute(self, j, s):
        k, p, nc = self.k, self.k.p, self.k.nc
        static = isinstance(j, int)
        p.wait("dve", self.kept[f"loaded{s}"], self.kept[f"stored{s}"], k.c_done if static else None)
        made = [None] * len(self.vectors)
        for kk in range(KD):
            for i, v in enumerate(self.vectors):
                c = k.c_act[:, v * KD + kk:v * KD + kk + 1]
                w, acc = self.raw[s][:, kk, :], self.acc[s][:, i, :]
                if kk == 0:
                    made[i] = p.dve(nc.vector.tensor_scalar(acc, w, c, None, ALU.mult))
                else:
                    p.wait("dve", made[i])
                    made[i] = p.dve(nc.vector.scalar_tensor_tensor(acc, w, c, acc, ALU.mult, ALU.add))
        self.made = made[-1]
        if not static or j + 2 < self.count:
            self.fetch(j + 2, s, self.made)

    def reduce(self, j, s):
        k, p, nc = self.k, self.k.p, self.k.nc
        p.wait("pe", self.made, self.kept[f"stored{s}"], k.ones_set if isinstance(j, int) else None)
        for i in range(len(self.vectors)):
            last = nc.tensor.matmul(k.ps[0:1, 4 + s, i * JW:(i + 1) * JW], k.ones[:, 0:1], self.acc[s][:, i, :],
                                    start=True, stop=True)
        summed = p.pe(last)
        p.wait("act", summed, self.kept[f"stored{s}"])
        n = len(self.vectors) * JW
        row = self.row[s][:, :, :].rearrange("p v n -> p (v n)")
        read = p.act(nc.scalar.activation(row, k.ps[0:1, 4 + s, 0:n], ACT.Copy))
        rows = k.rows[self.block * 2 + self.layer, :, :].rearrange("v (j n) -> v j n", n=JW)[0:len(self.vectors)]
        if isinstance(j, int):
            out = rows[:, self.first + j, :]
        else:
            out = rows[:, bass.ds(nc.gpsimd.snap(j + self.first), 1), :].rearrange("v o n -> v (o n)")
        p.wait("pool", read)
        self.kept[f"stored{s}"] = p.done(
            f"r{s}", nc.gpsimd.dma_start(out.unsqueeze(0), self.row[s][:, :, :]), 16)
        self.stores = [self.kept["stored0"], self.kept["stored1"]]

    def read_all(self):
        return [self.made, *self.stores]


class Stages(Kernel):
    def constants(self):
        p, nc, ins = self.p, self.nc, self.ins
        self.load(self.small[:, :], ins["small"])
        self.load(self.ident[:, :], ins["ident"])
        self.load(self.x[:, :, LATS], ins["x"])
        self.consts = self.load(self.x[:, :, 0:CTX], ins["ctx"])
        self.ones_set = p.pool(nc.gpsimd.memset(self.ones[:, :], 1.0))

    def condition_start(self):
        p, nc = self.p, self.nc
        p.wait("act", self.consts)
        self.c_done = p.act(nc.scalar.activation(self.c_act[:, :], self.col("c1", 0, 3 * KD), ACT.Silu))
        with ExitStack() as ctx:
            jobs = Modulations(Space(self, ctx, "start"), 0, 0, 0, JOBS // 2 - 1, [0])
            jobs.start(0)
            for n in range(jobs.count):
                jobs.compute(n, n % 2)
                jobs.reduce(n, n % 2)
            self.modulations_done = jobs.read_all()
        self.columns_of(0, 0, [0], 0, 2 * KD)

    def columns_of(self, block, layer, vectors, f0, f1):
        p, nc = self.p, self.nc
        n, nv = f1 - f0, len(vectors)
        turn, mods = self.turn, self.mods1 if block == 0 else self.mods2
        rows = self.rows[block * 2 + layer, :, :].rearrange("v (f c) -> v f c", c=P)
        for v in range(nv):
            p.wait("sp", *self.modulations_done, self.turn_read)
            loaded = p.done("turn", nc.sync.dma_start(turn[0:n, v, :], rows[v, f0:f1, :]), 16)
        p.wait("pe", loaded, self.columns_read)
        for v in range(nv):
            last = nc.tensor.matmul(self.ps[:, 7, v * n:(v + 1) * n], turn[0:n, v, :], self.ident[0:n, 0:n],
                                    is_transpose=True, start=True, stop=True)
        self.turn_read = p.pe(last)
        p.wait("dve", self.turn_read, self.consts)
        bias = self.col("ada_b" if block == 0 else "mod_b", layer * NMOD + f0, n)
        for v in range(nv):
            out = mods[:, layer, f0:f1] if block == 0 else mods[:, layer, f0:f1, SEG_OF[vectors[v]]]
            made = p.dve(nc.vector.tensor_tensor(out, self.ps[:, 7, v * n:(v + 1) * n], bias, ALU.add))
        self.columns_read = self.mods_made = made
        p.wait("dve", made)
        for m in (KD, 4 * KD):
            if f0 <= m < f1:
                for v in range(nv):
                    out = mods[:, layer, m:m + KD] if block == 0 else mods[:, layer, m:m + KD, SEG_OF[vectors[v]]]
                    self.mods_made = p.dve(nc.vector.tensor_scalar(out, out, 1.0, None, ALU.add))

    def mod(self, block, layer, m, f, seg=1):
        at = m * KD + f if isinstance(f, int) else f + m * KD
        at = slice(at, at + 1) if isinstance(at, int) else bass.ds(at, 1)
        if block == 0:
            return self.mods1[:, layer, at]
        return self.mods2[:, layer, at, seg]

    def split(self, f, t0, tn, value, made):
        p, nc = self.p, self.nc
        hi, lo = self.h_hi[:, f, t0:t0 + tn], self.h_lo[:, f, t0:t0 + tn]
        p.wait("act", made)
        high = p.act(nc.scalar.activation(hi, value, ACT.Copy))
        p.wait("dve", high)
        return p.dve(nc.vector.tensor_tensor(lo, value, hi.bitcast(F32), ALU.subtract))

    def residual(self, block, layer, m, tokens, gate=None):
        x_ready = self.x_done

        def consume(n, s, ps, product):
            p, nc = self.p, self.nc
            p.wait("dve", product, x_ready if isinstance(n, int) else None)
            for t0, tn, bank in segments(tokens):
                g = self.mod(block, layer, m, n, seg=bank) if gate is None else gate(n)
                x = self.x[:, n if isinstance(n, int) else bass.ds(n, 1), t0:t0 + tn]
                if not isinstance(n, int):
                    x = x.rearrange("p o t -> p (o t)")
                done = p.dve(nc.vector.scalar_tensor_tensor(x, ps[:, bank, 0:tn], g, x, ALU.mult, ALU.add))
            self.x_done = done
            return (done,)
        return consume

    def column_sum(self, src, t0, tn, bank, square):
        p, nc = self.p, self.nc
        p.wait("pe", self.ones_set, self.bank_free)
        for f in range(KD):
            value = src[:, f, t0:t0 + tn]
            if square:
                p.wait("act", self.x_done, self.sq_free[f % 2], self.tmp_free[f % 2])
                squared = p.act(nc.scalar.activation(self.tmp[f % 2][:, 0:tn], value, ACT.Square))
                p.wait("pe", squared)
                value = self.tmp[f % 2][:, 0:tn]
            else:
                p.wait("pe", self.x_done)
            last = nc.tensor.matmul(self.ps[:, bank, 0:tn], self.ones[:, :], value, start=f == 0, stop=f == KD - 1)
            if square or f == KD - 1:
                last = p.pe(last)
                self.sq_free[f % 2] = last if square else self.sq_free[f % 2]
        return last

    def reciprocal_root(self, t0, tn, bank, summed, width, eps):
        p, nc = self.p, self.nc
        r = self.rstd[:, t0:t0 + tn]
        p.wait("dve", summed)
        scaled = p.dve(nc.vector.tensor_scalar(r, self.ps[:, bank, 0:tn], 1.0 / width, eps, ALU.mult, ALU.add))
        self.bank_free = scaled
        p.wait("act", scaled)
        root = p.act(nc.scalar.activation(r, r, ACT.Sqrt))
        p.wait("dve", root)
        return p.dve(nc.vector.reciprocal(r, r))

    def layer_norm(self, which):
        p, nc = self.p, self.nc
        t0, tn = CTX, LAT
        mean = self.mean[:, 0:tn]
        summed = self.column_sum(self.x, t0, tn, 6, False)
        p.wait("dve", summed)
        p.wait("act", summed)
        made = self.bank_free = p.dve(nc.vector.tensor_scalar(mean, self.ps[:, 6, 0:tn], 1.0 / D, None, ALU.mult))
        for f in range(KD):
            x = self.x[:, f, t0:t0 + tn]
            p.wait("dve", made)
            self.x_done = p.dve(nc.vector.tensor_tensor(x, x, mean, ALU.subtract))
        summed = self.column_sum(self.x, t0, tn, 7, True)
        rstd = self.reciprocal_root(t0, tn, 7, summed, D, LN_EPS)
        for f in range(KD):
            x = self.x[:, f, t0:t0 + tn]
            p.wait("dve", rstd)
            scaled = p.dve(nc.vector.tensor_tensor(x, x, self.rstd[:, t0:t0 + tn], ALU.mult))
            p.wait("act", scaled)
            self.x_tile[f] = p.act(nc.scalar.activation(x, x, ACT.Identity, scale=self.col("ln_g", which * KD + f),
                                                        bias=self.col("ln_b", which * KD + f)))
        self.x_done = self.x_tile[KD - 1]

    def modulate1(self, layer, m, plain=None):
        p, nc = self.p, self.nc
        for f in range(KD):
            x = self.x[:, f, LATS]
            h = self.tmp[f % 2][:, 0:LAT] if plain is None else plain[:, f, :]
            p.wait("act", self.x_tile[f], self.mods_made, self.tmp_free[f % 2], self.sq_free[f % 2])
            made = p.act(nc.scalar.activation(h, x, ACT.Identity, scale=self.mod(0, layer, m + 1, f),
                                              bias=self.mod(0, layer, m, f)))
            if plain is None:
                self.h_done = self.tmp_free[f % 2] = self.split(f, CTX, LAT, h, made)
            else:
                self.h_done = made
            p.wait("pool", made)
            self.x_tile[f] = p.pool(nc.gpsimd.tensor_scalar(x, x, ALPHA, None, ALU.mult))
        self.x_done = self.x_tile[KD - 1]

    def rms_modulate(self, layer, m, gain, tokens):
        p, nc = self.p, self.nc
        for t0, tn, bank in segments(tokens):
            gains = self.gain[:, bank, :]
            p.wait("dve", self.mods_made, self.gain_read)
            gained = p.dve(nc.vector.tensor_tensor(gains, self.mods2[:, layer, (m + 1) * KD:(m + 2) * KD, bank],
                                                   self.col(gain, layer * KD, KD), ALU.mult))
            summed = self.column_sum(self.x, t0, tn, 6 + bank, True)
            rstd = self.reciprocal_root(t0, tn, 6 + bank, summed, D, EPS)
            for f in range(KD):
                x, h = self.x[:, f, t0:t0 + tn], self.tmp[f % 2][:, 0:tn]
                p.wait("dve", rstd, self.tmp_free[f % 2], self.sq_free[f % 2])
                scaled = p.dve(nc.vector.tensor_tensor(h, x, self.rstd[:, t0:t0 + tn], ALU.mult))
                p.wait("act", gained, scaled)
                made = p.act(nc.scalar.activation(h, h, ACT.Identity, scale=self.gain[:, bank, f:f + 1],
                                                  bias=self.mod(1, layer, m, f, seg=bank)))
                self.h_done = self.tmp_free[f % 2] = self.split(f, t0, tn, h, made)
        self.gain_read = made

    def ffn(self, block, layer, tokens, hosting=None):
        p, nc = self.p, self.nc
        with ExitStack() as ctx:
            sb = lambda name, shape, dt=F32: ctx.enter_context(nc.sbuf_tensor(f"{name}_{block}{layer}", shape, dt))
            t_first = TALL - tokens
            g_hi, g_lo = sb("g_hi", [P, FG, tokens], F32R), sb("g_lo", [P, FG, tokens], F32R)
            conv = [sb("conv_u", [P, TALL]), sb("conv_v", [P, TALL])]
            act = sb("silu_u", [P, TALL])
            g = sb("gated", [P, TALL])
            self.job_space = Space(self, ctx, f"{block}{layer}") if hosting else None
            cw, cb, parts = ("fcw", "fcb", 1) if block == 0 else ("cw2", "cb2", 2)
            base_w, base_b = SMALL[cw][0], SMALL[cb][0]
            down_done = self.h_done
            for half in range(2):
                up = Stream(self, f"up{block}{layer}", half * 2 * FG, 2 * FG, KD, self.h_hi, self.h_lo, tokens)
                up.start(self.h_done)
                if hosting:
                    up.host(hosting.pop(0)(self.job_space))

                def taps(j, part, tap):
                    width = parts * 3 * FT
                    at = base_w + layer * width + (part * 3 + tap) * FT + half * FG
                    return self.small[:, at + j:at + j + 1] if isinstance(j, int) else self.small[:, bass.ds(j + at, 1)]

                def bias(j, part):
                    at = base_b + layer * parts * FT + part * FT + half * FG
                    return self.small[:, at + j:at + j + 1] if isinstance(j, int) else self.small[:, bass.ds(j + at, 1)]

                def convolve(j, part, ps, product, kept):
                    out = conv[part]
                    shifts = ((2, 0), (1, 1), (0, 2)) if block == 0 else ((1, 0), (0, 1), (-1, 2))
                    p.wait("act", product, kept)
                    for t0, tn, bank in segments(tokens):
                        centre = next(tap for d, tap in shifts if d == 0)
                        first = p.act(nc.scalar.activation(out[:, t0:t0 + tn], ps[:, bank, 0:tn], ACT.Identity,
                                                           scale=taps(j, part, centre), bias=bias(j, part)))
                    last = first
                    for d, tap in shifts:
                        if d == 0:
                            continue
                        p.wait("dve", last)
                        for t0, tn, bank in segments(tokens):
                            lo, hi = max(d, 0), tn + min(d, 0)
                            o = out[:, t0 + lo:t0 + hi]
                            last = p.dve(nc.vector.scalar_tensor_tensor(o, ps[:, bank, lo - d:hi - d], taps(j, part, tap),
                                                                        o, ALU.mult, ALU.add))
                    return last

                tall = slice(t_first, TALL)

                def consume(n, s, ps, product):
                    if isinstance(n, int):
                        is_u, j = n % 2 == 0, n // 2
                    else:
                        is_u, j = s == up.s0, consume.pair
                    if is_u:
                        made = convolve(j, 0, ps, product, up.kept.get("silu"))
                        p.wait("act", made, up.kept.get("gated"))
                        up.kept["silu"] = p.act(nc.scalar.activation(act[:, tall], conv[0][:, tall], ACT.Silu))
                        return (made,)
                    where = j if isinstance(j, int) else bass.ds(j, 1)
                    hi, lo = g_hi[:, where, :], g_lo[:, where, :]
                    if not isinstance(j, int):
                        hi, lo = hi.rearrange("p o t -> p (o t)"), lo.rearrange("p o t -> p (o t)")
                    if block == 1:
                        made = convolve(j, 1, ps, product, up.kept.get("gated"))
                        p.wait("dve", made, up.kept["silu"], up.kept.get("low"))
                        gated = p.dve(nc.vector.tensor_tensor(g[:, tall], act[:, tall], conv[1][:, tall], ALU.mult))
                        read = made
                    else:
                        p.wait("dve", product, up.kept["silu"], up.kept.get("low"))
                        read = gated = p.dve(nc.vector.tensor_tensor(g[:, tall], act[:, tall], ps[:, 1, 0:LAT], ALU.mult))
                    up.kept["gated"] = gated
                    p.wait("act", gated, down_done)
                    high = p.act(nc.scalar.activation(hi, g[:, tall], ACT.Copy))
                    p.wait("dve", high)
                    low = up.kept["low"] = p.dve(nc.vector.tensor_tensor(lo, g[:, tall], hi.bitcast(F32), ALU.subtract))
                    self.g_done = low
                    return (read,)

                self.run_pairs(up, consume, block, tokens)
                down = Stream(self, f"down{block}{layer}", half * KD, KD, FG, g_hi, g_lo, tokens)
                down.start(self.g_done)
                if hosting:
                    down.host(hosting.pop(0)(self.job_space))
                down.run(self.residual(block, layer, 5, tokens))
                down_done = self.free_hl[1 - self.slot]
                if half == 1 and hosting:
                    hosting.pop(0)()

    def run_pairs(self, up, consume, block, tokens):
        n_seg = len(segments(tokens))
        conv = n_seg * (1 if block == 0 else 2)
        orig = up.step

        def step(n, s, c, has_next, has_fetch):
            if not isinstance(n, int):
                consume.pair = self.p.loop.index + 1
            orig(n, s, c, has_next, has_fetch)

        up.step = step
        up.run(consume, act=conv + 2, dve=2 * conv + 2)

    def keep(self, dst, tokens, scale=1.0, func=ACT.Copy):
        t_first = TALL - tokens

        def consume(n, s, ps, product):
            p, nc = self.p, self.nc
            p.wait("act", product, self.z_free if isinstance(n, int) else None)
            for t0, tn, bank in segments(tokens):
                at = dst[:, n if isinstance(n, int) else bass.ds(n, 1), t0 - t_first:t0 - t_first + tn]
                if not isinstance(n, int):
                    at = at.rearrange("p o t -> p (o t)")
                self.z_done = p.act(nc.scalar.activation(at, ps[:, bank, 0:tn], func, scale=scale))
            return (self.z_done,)
        return consume

    def keep_token_major(self, dst, tokens, n0=0):
        tiles = tokens // P

        def consume(n, s, ps, product):
            p, nc = self.p, self.nc
            p.wait("act", product, self.z_free)
            for b in range((tiles + 3) // 4):
                m = min(4, tiles - 4 * b)
                self.z_done = p.act(nc.scalar.activation(
                    dst[:, 4 * b:4 * b + m, (n0 + n) * P:(n0 + n + 1) * P],
                    ps[:, b, 0:m * P].rearrange("p (t f) -> p t f", f=P), ACT.Copy))
            return (self.z_done,)
        return consume

    def straight(self, name, first, count, kt, hi, lo, tokens, consume, token_major=False, **strides):
        st = Stream(self, name, first, count, kt, hi, lo, tokens, token_major)
        st.start(self.h_done)
        st.run(consume, **strides)

    def decayed_products(self, levels, att, masks, q, k, b, comb, width, heads_of, ready, backward, first_mask):
        p, nc = self.p, self.nc
        n_tok = width
        read = ready
        for level in range(levels):
            half = 1 << level
            v = lambda a: a.rearrange("p (n c) -> p n c", c=2 * half)
            bb, cc, qq, kk = v(b), v(comb), v(q), v(k)
            left, right = slice(0, half), slice(half, 2 * half)
            shape = [P, n_tok // (2 * half), half]
            p.wait("dve", read)
            if not backward:
                mid = bb[:, :, half - 1:half].to_broadcast(shape)
                p.dve(nc.vector.tensor_tensor(cc[:, :, left], mid, bb[:, :, left], ALU.subtract))
                made = p.dve(nc.vector.tensor_tensor(cc[:, :, right], bb[:, :, right], mid, ALU.subtract))
                sides = ((left, kk), (right, qq))
            else:
                mid = bb[:, :, half:half + 1].to_broadcast(shape)
                p.dve(nc.vector.tensor_tensor(cc[:, :, left], mid, bb[:, :, left], ALU.subtract))
                made = p.dve(nc.vector.tensor_tensor(cc[:, :, right], bb[:, :, right], mid, ALU.subtract))
                sides = ((left, qq), (right, kk))
            p.wait("act", made)
            decays = p.act(nc.scalar.activation(comb, comb, ACT.Exp))
            p.wait("dve", decays)
            for side, factor in sides:
                made = p.dve(nc.vector.tensor_tensor(cc[:, :, side], cc[:, :, side], factor[:, :, side], ALU.mult))
            read = self.products_to(att, [(comb, comb)], heads_of, made, masks[:, first_mask + level, :])
        return read

    def load_masks(self, masks, name, att, after):
        p, nc = self.p, self.nc
        n = masks.shape[1]
        wide = att[:, 0:n, :].bitcast(I32)
        loaded = self.load(wide, self.ins[name], after)
        p.wait("pool", loaded)
        packed = p.pool(nc.gpsimd.tensor_copy(masks[:, :, :], wide))
        p.wait("pool", packed)
        return packed, p.pool(nc.gpsimd.memset(att[:, :, :], 0.0))

    def products_to(self, att, pairs, units, made, mask):
        p, nc = self.p, self.nc
        lhs, rhs = pairs[0]
        last = None
        for b0 in range(0, len(units), 8):
            pair = (b0 // 8) % 2
            group = units[b0:b0 + 8]
            p.wait("pe", made, self.att_free[pair])
            for i, (rows, cols) in enumerate(group):
                out = self.ps[:, 4 + 2 * pair + i // 4, (i % 4) * P:(i % 4 + 1) * P]
                last = nc.tensor.matmul(out, lhs[rows, cols], rhs[rows, cols], start=True, stop=True)
            last = p.pe(last)
            p.wait("dve", last)
            n = len(group)
            got = self.ps[:, 4 + 2 * pair:6 + 2 * pair, :].rearrange("p b (i t) -> p (b i) t", t=P)[:, 0:n, :]
            self.att_free[pair] = self.att_done = p.dve(nc.vector.copy_predicated(
                att[:, b0:b0 + n, :], mask.unsqueeze(1).to_broadcast([P, n, P]), got))
        return last

    def even_mixer1(self):
        p, nc, ins = self.p, self.nc, self.ins
        self.z_free = None
        NC = LAT // CHUNK
        with ExitStack() as ctx:
            sb = lambda name, shape, dt=F32: ctx.enter_context(nc.sbuf_tensor(name, shape, dt))
            z = sb("z1", [P, 22, LAT])
            v = sb("v1", [P, NC, 5 * P])
            with ExitStack() as inner:
                st = Stream(self, "in1", 0, 22, KD, self.h_hi, self.h_lo, LAT)
                st.start(self.h_done)
                st.host(Modulations(Space(self, inner, "in1"), 0, 0, JOBS // 2 - 1, JOBS // 2 + 1, [0]))
                st.run(self.keep(z, LAT), act=2)
                self.columns_of(0, 0, [0], 2 * KD, NMOD)
            for f in range(5):
                units = [(slice(0, P), slice(t * P, (t + 1) * P)) for t in range(NC)]
                self.transposes(v[:, :, f * P:(f + 1) * P], z[:, 17 + f, :], units, self.z_done)
            self.z_done = self.evicted
            zk = z[:, 16:17, :]
            z_done = self.z_done
            self.hgrn(ins, z, v, z_done)
            self.window_attention(ins, z, zk, v, z_done)
            self.straight("out1", 0, KD, KD, self.h_hi, self.h_lo, LAT, self.residual(0, 0, 2, LAT), dve=2)

    def hgrn(self, ins, z, v, z_done):
        p, nc = self.p, self.nc
        H, NC = 4, LAT // CHUNK
        W = H * LAT
        with ExitStack() as ctx:
            sb = lambda name, shape, dt=F32: ctx.enter_context(nc.sbuf_tensor(name, shape, dt))
            flat = lambda a, i: a[:, i:i + H, :].rearrange("p h t -> p (h t)")
            q, f, gate = flat(z, 0), flat(z, 4), flat(z, 8)
            k = sb("hk", [P, W])
            b = sb("hb", [P, W])
            comb = sb("hcomb", [P, W])
            att = sb("hatt", [P, H * NC, P])
            kd_t = flat(z, 18).rearrange("p (n c) -> p n c", c=P)
            state = f.rearrange("p (h c v) -> p h c v", h=H, c=NC)
            reset = self.mean
            masks = sb("hmasks", [P, LEVELS + 1, P], U8)
            lb = sb("hlb", [P, 4 * H])
            loaded = self.load(reset[:, :], ins["reset1"])
            loaded, zeroed = self.load_masks(masks, "masks1", att, None)
            raw, e, prob, one_less = (lb[:, i * H:(i + 1) * H] for i in range(4))
            p.wait("dve", self.consts)
            made = p.dve(nc.vector.tensor_tensor(e, self.col("lb_raw", 0, H), self.col("lb_raw", 0, H), ALU.subtract))
            p.wait("act", made, z_done)
            made = p.act(nc.scalar.activation(e, e, ACT.Exp))
            p.wait("dve", made)
            made = p.dve(nc.vector.reciprocal(raw, e))
            p.wait("dve", made)
            made = p.dve(nc.vector.tensor_tensor(prob, e, raw, ALU.mult))
            p.wait("dve", made)
            made = p.dve(nc.vector.tensor_tensor(raw, prob, prob, ALU.subtract))
            p.wait("dve", made)
            lower = p.dve(nc.vector.tensor_scalar(one_less, raw, -1.0, 1.0, ALU.mult, ALU.add))
            p.wait("dve", z_done)
            made = p.dve(nc.vector.tensor_scalar(f, f, -1.0, 80.0, ALU.mult, ALU.min))
            p.wait("act", made)
            made = p.act(nc.scalar.activation(k[:, :], f, ACT.Exp))
            p.wait("dve", made)
            made = p.dve(nc.vector.tensor_scalar(f, k[:, :], 1.0, None, ALU.add))
            p.wait("dve", made)
            made = p.dve(nc.vector.reciprocal(f, f))
            p.wait("dve", made, lower)
            made = p.dve(nc.vector.tensor_tensor(k[:, :], k[:, :], f, ALU.mult))
            p.wait("dve", made)
            for h in range(H):
                at = slice(h * LAT, (h + 1) * LAT)
                p.dve(nc.vector.tensor_scalar(k[:, at], k[:, at], one_less[:, h:h + 1], None, ALU.mult))
                gates = p.dve(nc.vector.tensor_scalar(f[:, at], f[:, at], one_less[:, h:h + 1], raw[:, h:h + 1],
                                                      ALU.mult, ALU.add))
            p.wait("act", gates)
            logs = p.act(nc.scalar.activation(f, f, ACT.Ln))
            p.wait("dve", logs, loaded)
            for h in range(H):
                at = slice(h * LAT, (h + 1) * LAT)
                summed = p.dve(nc.vector.tensor_tensor_scan(b[:, at], reset[:, :], f[:, at], 0.0, ALU.mult, ALU.add))
            units = [(slice(0, P), slice(h * LAT + c * CHUNK, h * LAT + (c + 1) * CHUNK))
                     for h in range(H) for c in range(NC)]
            p.wait("dve", zeroed)
            self.products_to(att, [(k, q)], units, summed, masks[:, LEVELS, :])
            read = self.decayed_products(LEVELS, att, masks, q, k[:, :], b[:, :], comb[:, :], W, units, summed, False, 0)
            v3 = lambda a: a.rearrange("p (n c) -> p n c", c=CHUNK)
            ends = v3(b[:, :])[:, :, CHUNK - 1:CHUNK]
            p.wait("dve", read, summed)
            made = p.dve(nc.vector.tensor_tensor(v3(comb[:, :]), ends.to_broadcast([P, H * NC, CHUNK]), v3(b[:, :]), ALU.subtract))
            p.wait("act", made)
            made = p.act(nc.scalar.activation(comb[:, :], comb[:, :], ACT.Exp))
            p.wait("dve", made)
            made = p.dve(nc.vector.tensor_tensor(comb[:, :], comb[:, :], k[:, :], ALU.mult))
            kd_read = self.transposes(kd_t, comb, units, made)
            p.wait("act", self.att_done, read)
            qd = k
            p.wait("act", made)
            e2 = p.act(nc.scalar.activation(qd[:, :], b[:, :], ACT.Exp))
            ends_e = reset
            made_e = p.act(nc.scalar.activation(ends_e[:, 0:H * NC].unsqueeze(2), ends, ACT.Exp))
            p.wait("dve", e2)
            q_done = p.dve(nc.vector.tensor_tensor(qd[:, :], qd[:, :], q, ALU.mult))
            p.wait("pe", self.evicted, self.att_free[0], self.att_free[1])
            p.wait("dve", made_e)
            zero = p.dve(nc.vector.memset(state[:, :, 0, :], 0.0))
            for c in range(NC - 1):
                for h in range(H):
                    last = nc.tensor.matmul(self.ps[:, 4 + c, h * P:(h + 1) * P], kd_t[:, h * NC + c, :],
                                            v[:, c, (1 + h) * P:(2 + h) * P], start=True, stop=True)
                got = p.pe(last)
                p.wait("dve", got, zero)
                for h in range(H):
                    zero_next = p.dve(nc.vector.scalar_tensor_tensor(
                        state[:, h, c + 1, :], state[:, h, c, :], ends_e[:, h * NC + c:h * NC + c + 1],
                        self.ps[:, 4 + c, h * P:(h + 1) * P], ALU.mult, ALU.add))
                zero = zero_next
            p.wait("pe", self.att_done, q_done, zero)
            outs = []
            for h in range(H):
                for c in range(NC):
                    out = self.ps[:, 4 + h, c * P:(c + 1) * P]
                    nc.tensor.matmul(out, v[:, c, (1 + h) * P:(2 + h) * P], att[:, h * NC + c, :], start=True, stop=False)
                    last = nc.tensor.matmul(out, state[:, h, c, :], qd[:, h * LAT + c * CHUNK:h * LAT + (c + 1) * CHUNK],
                                            start=False, stop=True)
                outs.append(p.pe(last))
            for h in range(H):
                at = slice(h * LAT, (h + 1) * LAT)
                o = comb[:, at]
                p.wait("act", outs[h], kd_read)
                copied = p.act(nc.scalar.activation(o, self.ps[:, 4 + h, :], ACT.Copy))
                squared = self.head_norm(o, h, 4 + h, P, RMS_EPS, copied, LAT)
                p.wait("dve", squared, copied)
                made = p.dve(nc.vector.scalar_tensor_tensor(o, o, self.col("norm_g"), self.rstd[:, 0:LAT], ALU.mult, ALU.mult))
                p.wait("act", made)
                silu = p.act(nc.scalar.activation(gate[:, at], gate[:, at], ACT.Silu))
                p.wait("dve", silu)
                made = p.dve(nc.vector.tensor_tensor(o, o, gate[:, at], ALU.mult))
                self.rstd_free = made
                self.h_done = self.split(h, CTX, LAT, o, made)
            self.att_free = [self.h_done, self.h_done]

    def head_norm(self, value, n, bank, width, eps, made, tn):
        p, nc = self.p, self.nc
        t = self.tmp[n % 2][:, 0:tn]
        p.wait("act", made, self.tmp_free[n % 2], self.sq_free[n % 2])
        squared = p.act(nc.scalar.activation(t, value, ACT.Square))
        p.wait("pe", squared, made)
        summed = self.sq_free[n % 2] = p.pe(nc.tensor.matmul(self.ps[:, bank, 0:tn], self.ones[:, :], t, start=True, stop=True))
        r = self.rstd[:, 0:tn]
        p.wait("dve", summed, self.rstd_free)
        scaled = p.dve(nc.vector.tensor_scalar(r, self.ps[:, bank, 0:tn], 1.0 / width, eps, ALU.mult, ALU.add))
        self.head_bank_read = scaled
        p.wait("act", scaled)
        root = p.act(nc.scalar.activation(r, r, ACT.Sqrt))
        p.wait("dve", root)
        return p.dve(nc.vector.reciprocal(r, r))

    def transposes(self, dst, src, units, made):
        p, nc = self.p, self.nc
        for b0 in range(0, len(units), 8):
            pair = (b0 // 8) % 2
            group = units[b0:b0 + 8]
            p.wait("pe", made, self.att_free[pair])
            rows_n = group[0][0].stop - group[0][0].start
            for i, (rows, cols) in enumerate(group):
                last = nc.tensor.matmul(self.ps[:, 4 + 2 * pair + i // 4, (i % 4) * P:(i % 4) * P + rows_n], src[rows, cols],
                                        self.ident[rows, rows], is_transpose=True, start=True, stop=True)
            last = p.pe(last)
            p.wait("act", last)
            n = len(group)
            got = self.ps[:, 4 + 2 * pair:6 + 2 * pair, :].rearrange("p b (i t) -> p (b i) t", t=P)[:, 0:n, 0:rows_n]
            self.att_free[pair] = self.evicted = p.act(nc.scalar.activation(dst[:, b0:b0 + n, 0:rows_n], got, ACT.Copy))
        return last

    def window_attention(self, ins, z, zk, v, z_done):
        p, nc = self.p, self.nc
        NB, QT, NQ = LAT // P, 4, 8
        with ExitStack() as ctx:
            sb = lambda name, shape, dt=F32: ctx.enter_context(nc.sbuf_tensor(name, shape, dt))
            pos_i = sb("pos_i", [P, LAT], I32)
            ang, turns = sb("ang", [P, LAT]), sb("turns", [P, LAT])
            sin, cos = sb("sin1", [P, LAT]), sb("cos1", [P, LAT])
            rot = sb("rot1", [P, 3, P])
            kk = sb("kk1", [P, 2, LAT])
            mask = sb("wmask", [P, 2 * P])
            s = sb("scores1", [P, NQ, 2 * P])
            pt = sb("probs1t", [P, 2 * NQ, P])
            m, rs, es = sb("wm", [P, NQ]), sb("wrs", [P, NQ]), sb("wes", [P, NQ])
            o = z[:, 8:12, :]
            self.load(rot[:, :, :], ins["rot1"], self.h_done)
            self.load(mask[:, :], ins["wmask"])
            loaded = self.load(pos_i[:, :], ins["positions"].to_broadcast([P, LAT]))
            p.wait("dve", loaded, self.h_done)
            made = p.dve(nc.vector.tensor_copy(ang[:, :], pos_i[:, :]))
            p.wait("dve", made)
            angles = p.dve(nc.vector.tensor_scalar(ang[:, :], ang[:, :], self.col("inv_freq"), None, ALU.mult))
            parts = [6.28125, 0.0019350051879882812, 3.0199159819e-07]
            for dst, quarter in ((sin, 0.0), (cos, 0.25)):
                p.wait("dve", angles)
                made = p.dve(nc.vector.tensor_scalar(turns[:, :], ang[:, :], float(1.0 / TWO_PI), quarter, ALU.mult, ALU.add))
                p.wait("dve", made)
                made = p.dve(nc.vector.tensor_scalar(turns[:, :], turns[:, :], 12582912.0, -12582912.0, ALU.add, ALU.add))
                src = ang
                for part in parts:
                    p.wait("dve", made)
                    made = p.dve(nc.vector.scalar_tensor_tensor(dst[:, :], turns[:, :], -part, src[:, :], ALU.mult, ALU.add))
                    src = dst
                p.wait("dve", made)
                made = p.dve(nc.vector.tensor_scalar(dst[:, :], dst[:, :], quarter * TWO_PI, 3.1415925, ALU.add, ALU.min))
                p.wait("dve", made)
                angles = made = p.dve(nc.vector.tensor_scalar(dst[:, :], dst[:, :], -3.1415925, None, ALU.max))
                p.wait("act", made)
                tables = p.act(nc.scalar.activation(dst[:, :], dst[:, :], ACT.Sin))
            rotated, roped = [], None
            for j in range(QT + 1):
                x = z[:, 12 + j, :] if j < QT else zk[:, 0, :]
                bank = 4 + j % 2
                p.wait("pe", loaded, z_done, rotated[j - 2] if j > 1 else self.h_done)
                got = p.pe(nc.tensor.matmul(self.ps[:, bank, :], rot[:, 0, :], x, start=True, stop=True))
                p.wait("dve", got, tables, roped)
                made = p.dve(nc.vector.tensor_tensor(turns[:, :], self.ps[:, bank, :], sin[:, :], ALU.mult))
                rotated.append(made)
                made2 = p.dve(nc.vector.tensor_tensor(x, x, cos[:, :], ALU.mult))
                p.wait("dve", made2, made)
                roped = p.dve(nc.vector.tensor_tensor(x, x, turns[:, :], ALU.add))
            for g in range(2):
                p.wait("pe", roped, *rotated)
                got = p.pe(nc.tensor.matmul(self.ps[:, 4 + g, :], rot[:, 1 + g, :], zk[:, 0, :], start=True, stop=True))
                p.wait("act", got)
                keys = p.act(nc.scalar.activation(kk[:, g, :], self.ps[:, 4 + g, :], ACT.Copy))
            free = keys
            order = HEAD_ORDER
            for n in range(NB):
                k0 = max(n - 1, 0) * P
                nk = (n + 1) * P - k0
                m0 = 2 * P - nk
                p.wait("pe", roped, free)
                for i, h in enumerate(order):
                    rows = slice((h % 2) * 64, (h % 2) * 64 + 64)
                    last = nc.tensor.matmul(self.ps[:, 4 + i // 2, (i % 2) * 256:(i % 2) * 256 + nk],
                                            z[rows, 12 + h // 2, n * P:(n + 1) * P], kk[rows, h // 4, k0:k0 + nk],
                                            start=True, stop=True)
                scored = p.pe(last)
                got = self.ps[:, 4:8, :].rearrange("p b (i k) -> p (b i) k", k=256)[:, :, 0:nk]
                sn = s[:, :, 0:nk]
                p.wait("dve", scored, free)
                made = p.dve(nc.vector.scalar_tensor_tensor(sn, got, 64 ** -0.5,
                             mask[:, m0:2 * P].unsqueeze(1).to_broadcast([P, NQ, nk]), ALU.mult, ALU.add))
                p.wait("dve", made)
                made = p.dve(nc.vector.tensor_reduce(m[:, :], sn, AX.X, ALU.max))
                p.wait("dve", made)
                made = p.dve(nc.vector.tensor_tensor(m[:, :], m[:, :], self.col("sinks", 0, NQ), ALU.max))
                p.wait("dve", made)
                p.dve(nc.vector.tensor_tensor(es[:, :], self.col("sinks", 0, NQ), m[:, :], ALU.subtract))
                made = p.dve(nc.vector.tensor_tensor(sn, sn, m[:, :].unsqueeze(2).to_broadcast([P, NQ, nk]), ALU.subtract))
                p.wait("act", made)
                p.act(nc.scalar.activation(es[:, :], es[:, :], ACT.Exp))
                made = p.act(nc.scalar.activation(sn, sn, ACT.Exp))
                p.wait("dve", made)
                made = p.dve(nc.vector.tensor_reduce(rs[:, :], sn, AX.X, ALU.add))
                p.wait("dve", made)
                made = p.dve(nc.vector.tensor_tensor(rs[:, :], rs[:, :], es[:, :], ALU.add))
                p.wait("dve", made)
                made = p.dve(nc.vector.reciprocal(rs[:, :], rs[:, :]))
                p.wait("dve", made)
                probs = p.dve(nc.vector.tensor_tensor(sn, sn, rs[:, :].unsqueeze(2).to_broadcast([P, NQ, nk]), ALU.mult))
                nkb = nk // P
                p.wait("pe", probs)
                for i in range(NQ):
                    for j in range(nkb):
                        u = i * nkb + j
                        last = nc.tensor.matmul(self.ps[:, 4 + u // 4, (u % 4) * P:(u % 4 + 1) * P], sn[:, i, j * P:(j + 1) * P],
                                                self.ident[:, :], is_transpose=True, start=True, stop=True)
                turned = p.pe(last)
                nu = NQ * nkb
                p.wait("act", turned)
                moved = p.act(nc.scalar.activation(pt[:, 0:nu, :],
                              self.ps[:, 4:4 + nu // 4, :].rearrange("p b (i t) -> p (b i) t", t=P), ACT.Copy))
                p.wait("pe", moved)
                for i, h in enumerate(order):
                    rows = slice((h % 2) * 64, (h % 2) * 64 + 64)
                    for j in range(nkb):
                        last = nc.tensor.matmul(self.ps[rows, 4, (h // 2) * P:(h // 2 + 1) * P],
                                                v[:, k0 // P + j, (h // 4) * 64:(h // 4) * 64 + 64], pt[:, i * nkb + j, :],
                                                start=j == 0, stop=j == nkb - 1)
                mixed = p.pe(last)
                p.wait("act", mixed)
                free = p.act(nc.scalar.activation(o[:, :, n * P:(n + 1) * P],
                                                  self.ps[:, 4, :].rearrange("p (i t) -> p i t", t=P), ACT.Copy))
            for f in range(QT):
                self.h_done = self.split(4 + f, CTX, LAT, o[:, f, :], free)
            self.att_free = [self.h_done, self.h_done]

    def pool_mixer(self, layer):
        p, nc, ins = self.p, self.nc, self.ins
        with ExitStack() as ctx:
            sb = lambda name, shape, dt=F32: ctx.enter_context(nc.sbuf_tensor(name, shape, dt))
            h, recip = sb("pool_h", [P, KD, LAT]), sb("pool_recip", [P, 4, LAT])
            gate, wins = sb("pool_gate", [P, KD]), [sb(f"pool_win{i}", [P, LAT]) for i in range(4)]
            loaded = self.load(recip[:, :, :], ins["recip"], self.x_done)
            self.modulate1(layer, 0, plain=h)
            p.wait("dve", self.mods_made)
            gated = p.dve(nc.vector.tensor_tensor(gate[:, :], self.mods1[:, layer, 2 * KD:3 * KD], self.col("pool_scale", 0, KD), ALU.mult))
            p.wait("dve", self.h_done, loaded)
            self.h_done = None
            for f in range(KD):
                src = h[:, f, :]
                made = None
                for d in range(f // 2 + 1):
                    w = 1 << d
                    dst = wins[d % 2 + 2 * (f % 2)][:, :]
                    p.wait("dve", made, self.tmp_free[f % 2])
                    p.dve(nc.vector.tensor_tensor(dst[:, w:], src[:, w:], src[:, 0:LAT - w], ALU.add))
                    made = p.dve(nc.vector.tensor_copy(dst[:, 0:w], src[:, 0:w]))
                    src = dst
                p.wait("dve", made)
                made = p.dve(nc.vector.tensor_tensor(src, src, recip[:, f // 2, :], ALU.mult))
                p.wait("dve", made)
                made = p.dve(nc.vector.tensor_tensor(src, src, h[:, f, :], ALU.subtract))
                self.h_done = self.tmp_free[f % 2] = self.split(f, CTX, LAT, src, made)
            for g in range(4):
                at = slice(2 * g, 2 * g + 2)
                self.straight("pool", 2 * g, 2, 2, self.h_hi[:, at, :], self.h_lo[:, at, :], LAT,
                              self.shifted(self.residual(0, layer, 2, LAT, gate=lambda n: gate[:, n:n + 1]), 2 * g))

    def shifted(self, consume, by):
        return lambda n, s, ps, product: consume(n + by, s, ps, product)

    def even_mixer2(self):
        p, nc, ins = self.p, self.nc, self.ins
        T = TALL
        with ExitStack() as ctx:
            sb = lambda name, shape, dt=F32: ctx.enter_context(nc.sbuf_tensor(name, shape, dt))
            v = sb("v2", [P, T // P, 4 * P])
            z = sb("z2", [P, 9, T])
            with ExitStack() as inner:
                more = inner.enter_context(nc.sbuf_tensor("z2more", [P, 8, T], F32))
                self.z_free = self.h_done
                self.straight("in2", 0, 9, KD, self.h_hi, self.h_lo, T, self.keep(z, T), act=4)
                self.straight("in2", 9, 8, KD, self.h_hi, self.h_lo, T, self.keep(more, T), act=4)
                z_done = self.z_done
                for f in range(4):
                    units = [(slice(0, P), slice(t * P, (t + 1) * P)) for t in range(T // P)]
                    self.transposes(v[:, :, f * P:(f + 1) * P], more[:, f, :], units, z_done)
                self.z_free = self.evicted
                self.fourier(inner, more, z_done)
            self.gla(z, v)
            self.straight("out2", 0, KD, KD, self.h_hi, self.h_lo, T, self.residual(1, 0, 2, T), dve=4)

    def fourier(self, ctx, more, z_done):
        p, nc, ins = self.p, self.nc, self.ins
        sb = lambda name, shape, dt=F32: ctx.enter_context(nc.sbuf_tensor(name, shape, dt))
        feat = sb("dft_f", [P, 2 * P])
        lat, con = sb("dft_lat", [P, 2, LAT // P, LAT]), sb("dft_ctx", [P, 2, CTX // P, CTX])
        a = more[:, 0:2, :].rearrange("p k t -> p (k t)").rearrange("p (t c) -> p t c", c=2 * P)
        f, u = more[:, 2, :], more[:, 4:8, :]
        self.load(feat[:, :], ins["dft_f"], self.z_free)
        self.load(lat[:, :, :, :], ins["dft_lat"])
        loaded = self.load(con[:, :, :, :], ins["dft_ctx"])
        done = None
        for g in range(4):
            p.wait("pe", loaded, z_done, done, self.att_free[0], self.att_free[1])
            for t in range(TALL // P):
                last = nc.tensor.matmul(self.ps[:, 4 + t // 2, (t % 2) * 256:(t % 2) * 256 + 256],
                                        u[:, g, t * P:(t + 1) * P], feat[:, :], start=True, stop=True)
            got = p.pe(last)
            p.wait("act", got, done)
            rows = p.act(nc.scalar.activation(a, self.ps[:, 4:7, :].rearrange("p b (i c) -> p (b i) c", c=2 * P), ACT.Copy))
            p.wait("pe", rows)
            for t0, tn, bank in segments(TALL):
                basis = con if bank == 0 else lat
                nt = tn // P
                for part in range(2):
                    for t in range(nt):
                        last = nc.tensor.matmul(self.ps[:, 4 + bank, 0:tn], a[:, t0 // P + t, part * P:(part + 1) * P],
                                                basis[:, part, t, :], start=part == 0 and t == 0,
                                                stop=part == 1 and t == nt - 1)
            got = p.pe(last)
            p.wait("act", got, done)
            p.act(nc.scalar.activation(f[:, 0:CTX], self.ps[:, 4, 0:CTX], ACT.Copy))
            made = p.act(nc.scalar.activation(f[:, CTX:TALL], self.ps[:, 5, 0:LAT], ACT.Copy))
            done = self.split(g, 0, TALL, f, made)
        self.h_done = done
        self.att_free = [done, done]

    def gla(self, z, v):
        p, nc, ins = self.p, self.nc, self.ins
        T, H, NC = TALL, 4, TALL // CHUNK
        W = 2 * T
        with ExitStack() as ctx:
            sb = lambda name, shape, dt=F32: ctx.enter_context(nc.sbuf_tensor(name, shape, dt))
            flat = lambda i, n: z[:, i:i + n, :].rearrange("p h t -> p (h t)")
            q, k = flat(0, 2), flat(2, 2)
            b = [sb(f"gb{d}", [P, W]) for d in range(2)]
            comb = sb("gcomb", [P, W])
            att = sb("gatt", [P, H * NC, P])
            kd_t = [sb(f"gkdt{d}", [P, 2 * NC, P]) for d in range(2)]
            masks = sb("gmasks", [P, 2 * LEVELS + 1, P], U8)
            reset = sb("greset", [P, T])
            wg = self.tmp[0][0:16, :].rearrange("p (f c) -> p f c", c=P)
            ends = sb("gends", [P, 2, 2 * NC])
            loga = comb
            start = self.h_done
            self.load(wg, ins["w_gate"], start)
            self.load(reset[:, :], ins["reset2"])
            loaded, zeroed = self.load_masks(masks, "masks2", att, start)
            p.wait("dve", start)
            made = p.dve(nc.vector.tensor_scalar(q, q, 0.125, None, ALU.mult))
            free = made
            sums = []
            for d in range(2):
                p.wait("pe", loaded, free, self.h_done)
                for f in range(2):
                    for t0, tn, bank in segments(T):
                        last = nc.tensor.matmul(self.ps[:, 4 + 2 * f + bank, 0:tn], wg[:, 2 * d + f, :],
                                                z[0:16, 8, t0:t0 + tn], start=True, stop=True)
                got = p.pe(last)
                p.wait("act", got, free)
                for f in range(2):
                    for t0, tn, bank in segments(T):
                        x = p.act(nc.scalar.activation(loga[:, f * T + t0:f * T + t0 + tn], self.ps[:, 4 + 2 * f + bank, 0:tn],
                                                       ACT.Identity, bias=self.col("bgate", 2 * d + f)))
                e = b[d][:, :]
                p.wait("dve", x)
                made = p.dve(nc.vector.scalar_tensor_tensor(e, loga[:, :], -1.0, loga[:, :], ALU.mult, ALU.min))
                p.wait("act", made)
                made = p.act(nc.scalar.activation(e, e, ACT.Exp))
                p.wait("act", made)
                made2 = p.act(nc.scalar.activation(e, e, ACT.Ln, bias=1.0))
                p.wait("dve", made2)
                made = p.dve(nc.vector.tensor_scalar(loga[:, :], loga[:, :], 0.0, None, ALU.min))
                p.wait("dve", made)
                made = p.dve(nc.vector.tensor_tensor(loga[:, :], loga[:, :], e, ALU.subtract))
                p.wait("dve", made)
                made = p.dve(nc.vector.tensor_scalar(loga[:, :], loga[:, :], 1.0 / 16.0, None, ALU.mult))
                p.wait("dve", made, loaded)
                for f in range(2):
                    at = slice(f * T, (f + 1) * T)
                    free = p.dve(nc.vector.tensor_tensor_scan(e[:, at], reset[:, :], loga[:, at], 0.0, ALU.mult, ALU.add))
                if d == 1:
                    p.wait("dve", free)
                    n3 = lambda a: a.rearrange("p (n c) -> p n c", c=CHUNK)
                    free = p.dve(nc.vector.tensor_tensor(e, e, loga[:, :], ALU.subtract))
                    total = ends[:, 1, :].unsqueeze(2)
                    p.wait("dve", free)
                    free = p.dve(nc.vector.tensor_tensor(total, n3(e)[:, :, CHUNK - 1:CHUNK], n3(loga[:, :])[:, :, CHUNK - 1:CHUNK], ALU.add))
                sums.append(free)
            units = [(slice((h % 2) * 64, (h % 2) * 64 + 64), slice((h // 2) * T + c * CHUNK, (h // 2) * T + (c + 1) * CHUNK))
                     for h in (0, 2, 1, 3) for c in range(NC)]
            p.wait("dve", sums[1])
            made = p.dve(nc.vector.tensor_scalar(comb[:, :], k, 2.0, None, ALU.mult))
            p.wait("dve", zeroed)
            read = self.products_to(att, [(comb, q)], units, made, masks[:, 2 * LEVELS, :])
            for d in range(2):
                read = self.decayed_products(LEVELS, att, masks, q, k, b[d][:, :], comb[:, :], W, units, read, d == 1, d * LEVELS)
            v3 = lambda a: a.rearrange("p (n c) -> p n c", c=CHUNK)
            full = [(slice(0, P), slice(f * T + c * CHUNK, f * T + (c + 1) * CHUNK)) for f in range(2) for c in range(NC)]
            e0, e1 = b[0][:, :], b[1][:, :]
            p.wait("dve", read, self.att_done)
            kept = p.dve(nc.vector.tensor_copy(ends[:, 0, :].unsqueeze(2), v3(e0)[:, :, CHUNK - 1:CHUNK]))
            p.wait("dve", kept)
            made = p.dve(nc.vector.tensor_tensor(v3(comb[:, :]), ends[:, 0, :].unsqueeze(2).to_broadcast([P, 2 * NC, CHUNK]), v3(e0), ALU.subtract))
            p.wait("act", made)
            made = p.act(nc.scalar.activation(comb[:, :], comb[:, :], ACT.Exp))
            p.wait("dve", made)
            made = p.dve(nc.vector.tensor_tensor(comb[:, :], comb[:, :], k, ALU.mult))
            read = self.transposes(kd_t[0], comb, full, made)
            p.wait("act", read)
            made = p.act(nc.scalar.activation(comb[:, :], e1, ACT.Exp))
            p.wait("dve", made)
            made = p.dve(nc.vector.tensor_tensor(comb[:, :], comb[:, :], k, ALU.mult))
            read = self.transposes(kd_t[1], comb, full, made)
            p.wait("act", kept)
            f_done = p.act(nc.scalar.activation(e0, e0, ACT.Exp))
            p.wait("dve", made, f_done)
            p.dve(nc.vector.tensor_tensor(e0, e0, q, ALU.mult))
            made = p.dve(nc.vector.tensor_tensor(v3(e1), ends[:, 1, :].unsqueeze(2).to_broadcast([P, 2 * NC, CHUNK]), v3(e1), ALU.subtract))
            p.wait("act", made)
            made = p.act(nc.scalar.activation(e1, e1, ACT.Exp))
            ends_e = p.act(nc.scalar.activation(ends[:, :, :], ends[:, :, :], ACT.Exp))
            p.wait("dve", made)
            q_done = p.dve(nc.vector.tensor_tensor(e1, e1, q, ALU.mult))
            state = flat(0, 4).rearrange("p (d n v) -> p d n v", d=2, v=P)
            lat0 = CTX // CHUNK
            orders = [list(range(NC)), list(range(lat0 - 1, -1, -1)) + list(range(NC - 1, lat0 - 1, -1))]
            p.wait("pool", q_done)
            for d in range(2):
                for f in range(2):
                    init = p.pool(nc.gpsimd.memset(state[:, d, f * NC + orders[d][0], :], 0.0))
            p.wait("dve", ends_e, init)
            stepped = [self.evicted, self.evicted]
            for n in range(NC - 1):
                for d in range(2):
                    c, nxt = orders[d][n], orders[d][n + 1]
                    bank = 4 + 2 * d + n % 2
                    p.wait("pe", *stepped, self.att_free[0], self.att_free[1])
                    for h in range(H):
                        rows = slice((h % 2) * 64, (h % 2) * 64 + 64)
                        last = nc.tensor.matmul(self.ps[rows, bank, (h // 2) * P:(h // 2 + 1) * P],
                                                kd_t[d][:, (h // 2) * NC + c, rows], v[:, c, h * P:(h + 1) * P], start=True, stop=True)
                    got = p.pe(last)
                    p.wait("dve", got, stepped[d])
                    for f in range(2):
                        stepped[d] = p.dve(nc.vector.scalar_tensor_tensor(
                            state[:, d, f * NC + nxt, :], state[:, d, f * NC + c, :], ends[:, d, f * NC + c:f * NC + c + 1],
                            self.ps[:, bank, f * P:(f + 1) * P], ALU.mult, ALU.add))
            p.wait("pe", self.att_done, q_done, *stepped)
            free_o = [None, None]
            o = comb
            for h in range(H):
                rows = slice((h % 2) * 64, (h % 2) * 64 + 64)
                b0 = 4 + 2 * (h % 2)
                p.wait("pe", free_o[h % 2])
                for t0, tn, bank in segments(T):
                    for c in range(t0 // P, (t0 + tn) // P):
                        out = self.ps[:, b0 + bank, c * P - t0:(c + 1) * P - t0]
                        nc.tensor.matmul(out, v[:, c, h * P:(h + 1) * P], att[:, ((h % 2) * 2 + h // 2) * NC + c, :], start=True, stop=False)
                        cols = slice((h // 2) * T + c * CHUNK, (h // 2) * T + (c + 1) * CHUNK)
                        nc.tensor.matmul(out, state[rows, 0, (h // 2) * NC + c, :], e0[rows, cols], start=False, stop=False)
                        last = nc.tensor.matmul(out, state[rows, 1, (h // 2) * NC + c, :], e1[rows, cols], start=False, stop=True)
                got = p.pe(last)
                for t0, tn, bank in segments(T):
                    at = o[:, (h % 2) * T + t0:(h % 2) * T + t0 + tn]
                    p.wait("act", got, read, self.h_done)
                    copied = p.act(nc.scalar.activation(at, self.ps[:, b0 + bank, 0:tn], ACT.Copy))
                    rstd = self.head_norm(at, h, b0 + bank, P, EPS, copied, tn)
                    p.wait("dve", rstd)
                    made = p.dve(nc.vector.scalar_tensor_tensor(at, at, self.col("ggla", h), self.rstd[:, 0:tn], ALU.mult, ALU.mult))
                    self.rstd_free = made
                    gate = z[:, 4 + h, t0:t0 + tn]
                    p.wait("act", made)
                    silu = p.act(nc.scalar.activation(gate, gate, ACT.Silu))
                    p.wait("dve", silu)
                    made = p.dve(nc.vector.tensor_tensor(at, at, gate, ALU.mult))
                    self.h_done = self.split(4 + h, t0, tn, at, made)
                free_o[h % 2] = self.h_done
            self.att_free = [self.h_done, self.h_done]

    def attention(self):
        p, nc, ins = self.p, self.nc, self.ins
        T, NH, NKV, NT = TALL, 8, 2, LAT // P
        NS = T // P
        with ExitStack() as ctx:
            sb = lambda name, shape, dt=F32: ctx.enter_context(nc.sbuf_tensor(name, shape, dt))
            q, k = sb("aq", [P, NH, LAT]), sb("ak", [P, NKV, T])
            v = sb("av", [P, NS, NKV * P])
            cos, sin, rot = sb("acos", [P, LAT]), sb("asin", [P, LAT]), sb("arot", [P, P])
            s, pt = sb("ascores", [P, 2, NT, T]), sb("aprobs", [P, NS, LAT])
            nm, rs = sb("anm", [P, 2 * NT]), sb("ars", [P, 2 * NT])
            turned = sb("aturn", [P, LAT])
            o = sb("ao", [P, 2, LAT])
            self.z_free = self.h_done
            self.load(cos[:, :], ins["cos2"], self.h_done)
            self.load(sin[:, :], ins["sin2"])
            loaded = self.load(rot[:, :], ins["rot2"])
            self.straight("qkv", 0, 8, KD, self.h_hi, self.h_lo, LAT, self.keep(q, LAT), act=2)
            self.straight("qkv", 8, 2, KD, self.h_hi, self.h_lo, T, self.keep(k, T), act=4)
            vf = s[:, 0, 0:2, :]
            self.straight("qkv", 10, 2, KD, self.h_hi, self.h_lo, T, self.keep(vf, T))
            z_done = self.z_done
            for f in range(2):
                units = [(slice(0, P), slice(t * P, (t + 1) * P)) for t in range(NS)]
                self.transposes(v[:, :, f * P:(f + 1) * P], vf[:, f, :], units, z_done)
            z_done = self.evicted
            h_read = self.free_hl[1 - self.slot]
            roped = None
            for j in range(NKV + NH):
                x, gain = (k[:, j, :], self.col("gk")) if j < NKV else (q[:, j - NKV, :], self.col("gq"))
                parts = [(t0, tn) for t0, tn, _ in segments(T)] if j < NKV else [(0, LAT)]
                for t0, tn in parts:
                    xs = x[:, t0:t0 + tn]
                    rstd = self.head_norm(xs, j, 4 + j % 2, P, EPS, z_done, tn)
                    p.wait("dve", rstd)
                    normed = p.dve(nc.vector.scalar_tensor_tensor(xs, xs, gain, self.rstd[:, 0:tn], ALU.mult, ALU.mult))
                    self.rstd_free = normed
                    ready = normed
                    if tn == LAT:
                        p.wait("pe", normed, loaded, rs_free if j else None)
                        got = p.pe(nc.tensor.matmul(self.ps[:, 6, :], rot[:, :], xs, start=True, stop=True))
                        p.wait("dve", got, loaded, roped)
                        made = rs_free = p.dve(nc.vector.tensor_tensor(turned[:, :], self.ps[:, 6, :], sin[:, :], ALU.mult))
                        made2 = p.dve(nc.vector.tensor_tensor(xs, xs, cos[:, :], ALU.mult))
                        p.wait("dve", made, made2)
                        ready = roped = p.dve(nc.vector.tensor_tensor(xs, xs, turned[:, :], ALU.add))
            free_s, free_pt = [None, None], None
            free_bank = [ready, ready]
            free_t = [ready, ready]
            for h in range(NH):
                sl = h % 2
                for t in range(NT):
                    bank = 2 * (t % 2)
                    p.wait("pe", ready, free_bank[t % 2], *self.free_ps[t % 2])
                    for i in range(2):
                        last = nc.tensor.matmul(self.ps[:, bank + i, 0:T // 2], q[:, h, t * P:(t + 1) * P],
                                                k[:, h // 4, i * (T // 2):(i + 1) * (T // 2)], start=True, stop=True)
                    scored = p.pe(last)
                    got = self.ps[:, bank:bank + 2, 0:T // 2]
                    sc = s[:, sl, t, :]
                    at = slice(sl * NT + t, sl * NT + t + 1)
                    p.wait("dve", scored, free_s[sl])
                    made = p.dve(nc.vector.tensor_reduce(nm[:, at], got, AX.XY, ALU.max))
                    p.wait("dve", made)
                    made = p.dve(nc.vector.tensor_scalar(nm[:, at], nm[:, at], -(P ** -0.5), None, ALU.mult))
                    p.wait("act", made)
                    made = free_bank[t % 2] = p.act(nc.scalar.activation(sc.rearrange("p (i k) -> p i k", i=2), got, ACT.Exp,
                                                    scale=P ** -0.5, bias=nm[:, at], accum_out=rs[:, at]))
                    p.wait("dve", made)
                    made = p.dve(nc.vector.reciprocal(rs[:, at], rs[:, at]))
                    p.wait("dve", made)
                    probs = p.dve(nc.vector.tensor_scalar(sc, sc, rs[:, at], None, ALU.mult))
                for j in range(NS):
                    p.wait("pe", probs, free_t[j % 2])
                    for t in range(NT):
                        last = nc.tensor.matmul(self.ps[:, 4 + j % 2, t * P:(t + 1) * P], s[:, sl, t, j * P:(j + 1) * P],
                                                self.ident[:, :], is_transpose=True, start=True, stop=True)
                    got = p.pe(last)
                    if j % 2:
                        p.wait("dve", got, free_pt)
                        free_t[1] = p.dve(nc.vector.tensor_copy(pt[:, j, :], self.ps[:, 5, :]))
                    else:
                        p.wait("act", got, free_pt)
                        free_t[0] = p.act(nc.scalar.activation(pt[:, j, :], self.ps[:, 4, :], ACT.Copy))
                free_s[sl] = got
                p.wait("pe", free_t[0], free_t[1], free_o[sl] if h > 1 else None)
                for j in range(NS):
                    last = nc.tensor.matmul(self.ps[:, 6 + sl, :], v[:, j, (h // 4) * P:(h // 4 + 1) * P], pt[:, j, :],
                                            start=j == 0, stop=j == NS - 1)
                mixed = free_pt = p.pe(last)
                p.wait("act", mixed, free_o[sl] if h > 1 else None, h_read)
                if h == 0:
                    free_o = [None, None]
                copied = p.act(nc.scalar.activation(o[:, sl, :], self.ps[:, 6 + sl, :], ACT.Copy))
                free_o[sl] = self.h_done = self.split(h, CTX, LAT, o[:, sl, :], copied)
            self.att_free = [self.h_done, self.h_done]
            self.free_ps = [[self.h_done], [self.h_done]]
            self.straight("attout", 0, KD, KD, self.h_hi, self.h_lo, LAT, self.residual(1, 1, 2, LAT), dve=2)

    def final_norm(self):
        p, nc = self.p, self.nc
        summed = self.column_sum(self.x, CTX, LAT, 6, True)
        rstd = self.reciprocal_root(CTX, LAT, 6, summed, D, EPS)
        p.wait("dve", rstd)
        for f in range(KD):
            x = self.x[:, f, LATS]
            made = p.dve(nc.vector.scalar_tensor_tensor(x, x, self.col("gfin", f), self.rstd[:, LATS], ALU.mult, ALU.mult))
            p.wait("sp", made)
            stored = p.done("store", nc.sync.dma_start(self.out[:, f, :], x), 16)
        p.wait("sp", stored)


def build(nc, ins, out):
    with ExitStack() as ctx:
        k = Stages(nc, ctx, ins, out)
        k.att_free, k.rstd_free, k.z_free = [None, None], None, None
        k.constants()
        k.condition_start()
        k.x_tile = [k.consts] * KD
        k.x_done = k.consts
        k.modulate1(0, 0)
        k.even_mixer1()
        k.layer_norm(0)
        k.modulate1(0, 3)
        half = JOBS // 2
        k.ffn(0, 0, LAT, [
            lambda space: Modulations(space, 0, 1, 0, half + 1, [0]),
            lambda space: Modulations(space, 1, 0, 0, KD, [1, 2]),
            lambda space: Modulations(space, 0, 1, half - 1, half + 1, [0]),
            lambda space: Modulations(space, 1, 0, KD, KD, [1, 2]),
            lambda: k.columns_of(0, 1, [0], 0, NMOD)])
        k.layer_norm(1)
        k.pool_mixer(1)
        k.layer_norm(2)
        k.modulate1(1, 3)
        k.ffn(0, 1, LAT, [
            lambda space: Modulations(space, 1, 1, 0, half + 1, [1, 2]),
            lambda space: Modulations(space, 1, 0, 2 * KD, KD, [1, 2]),
            lambda space: Modulations(space, 1, 1, half - 1, half + 1, [1, 2]),
            lambda space: Modulations(space, 1, 0, 3 * KD, KD, [1, 2]),
            lambda: (k.columns_of(1, 0, [1, 2], 0, NMOD), k.columns_of(1, 1, [1, 2], 0, NMOD))])
        k.layer_norm(3)
        k.rms_modulate(0, 0, "gmix", TALL)
        k.even_mixer2()
        k.rms_modulate(0, 3, "gffn", TALL)
        k.ffn(1, 0, TALL)
        k.rms_modulate(1, 0, "gmix", TALL)
        k.attention()
        k.rms_modulate(1, 3, "gffn", LAT)
        k.ffn(1, 1, LAT)
        k.final_norm()


def shape_constants():
    c = {"ident": np.eye(P, dtype=np.float32)}
    s, t = np.meshgrid(np.arange(P), np.arange(P), indexing="ij")

    def level_masks(first, second):
        return [((s >> (l + 1)) == (t >> (l + 1))) & (((s >> l) & 1) == first) & (((t >> l) & 1) == second)
                for l in range(LEVELS)]

    fwd, bwd = level_masks(0, 1), level_masks(1, 0)
    pack = lambda ms: np.ascontiguousarray(np.stack(ms, 1).astype(np.int32))
    c["masks1"], c["masks2"] = pack(fwd + [s == t]), pack(fwd + bwd + [s == t])
    for name, n in (("reset1", LAT), ("reset2", TALL)):
        c[name] = np.ascontiguousarray(np.broadcast_to((np.arange(n) % CHUNK != 0).astype(np.float32), (P, n)))
    rel = np.arange(P)[:, None] + P - np.arange(2 * P)[None, :]
    c["wmask"] = np.where((rel >= 0) & (rel < P), 0.0, NEG).astype(np.float32)
    rot1 = np.zeros((P, 3, P), np.float32)
    for head in (0, 64):
        for i in range(8):
            rot1[head + 8 + i, 0, head + i] = -1.0
            rot1[head + i, 0, head + 8 + i] = 1.0
    for g in range(2):
        for i in range(64):
            rot1[g * 64 + i, 1 + g, i] = rot1[g * 64 + i, 1 + g, 64 + i] = 1.0
    c["rot1"] = rot1
    rot2 = np.zeros((P, P), np.float32)
    for i in range(64):
        rot2[64 + i, i], rot2[i, 64 + i] = -1.0, 1.0
    c["rot2"] = rot2
    recip = np.stack([1.0 / np.minimum(np.arange(LAT) + 1, w) for w in (2, 4, 8, 16)])
    c["recip"] = np.ascontiguousarray(np.broadcast_to(recip.astype(np.float32), (P, 4, LAT)))
    def dft(n):
        a = 2.0 * np.pi * (np.outer(np.arange(n), np.arange(n)) % n) / n
        return np.cos(a), np.sin(a)
    c["dft_f"] = np.concatenate(dft(P), 1).astype(np.float32)
    for name, n in (("dft_lat", LAT), ("dft_ctx", CTX)):
        cn, sn = dft(n)
        m = np.stack([cn, -sn]) / np.sqrt(n * P)
        c[name] = np.ascontiguousarray(m.reshape(2, n // P, P, n).transpose(2, 0, 1, 3).astype(np.float32))
    inv = (10000.0 ** (-np.arange(0, 64, 2, dtype=np.float32) / 64)).astype(np.float32)
    r, col = np.meshgrid(np.arange(LAT // 64), np.arange(64), indexing="ij")
    ang = np.concatenate([r.reshape(-1, 1).astype(np.float32) * inv, col.reshape(-1, 1).astype(np.float32) * inv], -1)
    for name, fn in (("cos2", np.cos), ("sin2", np.sin)):
        c[name] = np.ascontiguousarray(np.concatenate([fn(ang), fn(ang)], 1).T.astype(np.float32))
    inv1 = (500000.0 ** (-np.arange(0, 16, 2, dtype=np.float32) / 16)).astype(np.float32)
    per = np.zeros(64, np.float32)
    per[0:8] = per[8:16] = inv1
    c["inv_freq"] = np.concatenate([per, per]).reshape(P, 1)
    return c


def tiles(w, pad=None):
    rows, cols = w.shape
    return w.reshape(rows // P, P, cols // P, P).transpose(2, 1, 0, 3).reshape(cols // P, P, (rows // P) * P)


def columns(a):
    return np.moveaxis(a.reshape(*a.shape[:-1], a.shape[-1] // P, P), -1, 0).reshape(P, -1)


def layout(inputs):
    g = {n: np.asarray(a) for n, a in inputs.items()}
    c = shape_constants()
    a = {n: v for n, v in c.items() if n != "inv_freq"}
    a["x"] = g["x"][0].T.reshape(KD, P, LAT).transpose(1, 0, 2)
    a["ctx"] = g["ctx_2"][0].T.reshape(KD, P, CTX).transpose(1, 0, 2)
    a["positions"] = g["positions"].reshape(1, LAT)
    parts = {
        "c1": columns(g["c"][0]), "c2": columns(g["c_2"][0]), "cc2": columns(g["c_ctx_2"]),
        "ada_b": columns(g["ada_b"]), "mod_b": columns(g["b_mod_2"]), "ln_g": columns(g["ln_g"]), "ln_b": columns(g["ln_b"]),
        "lb_raw": columns(g["hgrn_lb_raw"]), "norm_g": columns(g["hgrn_norm_g"]), "pool_scale": columns(g["pool_scale"]),
        "fcw": columns(g["ffn_conv_w"]), "fcb": columns(g["ffn_conv_b"]), "gmix": columns(g["g_norm_mix_2"]),
        "gffn": columns(g["g_norm_ffn_2"]), "gfin": columns(g["g_norm_final_2"]), "bgate": columns(g["b_gla_gate_2"]),
        "ggla": columns(g["g_gla_out_2"]), "gq": columns(g["g_q_2"]), "gk": columns(g["g_k_2"]),
        "cw2": columns(g["w_ffn_conv_2"].reshape(2, 3, 2, F_FF).transpose(0, 2, 1, 3)),
        "cb2": columns(g["b_ffn_conv_2"]), "inv_freq": c["inv_freq"],
        "sinks": np.broadcast_to(g["attn_sinks"][:, HEAD_ORDER], (P, 8)),
    }
    a["small"] = np.concatenate([parts[n] for n in SMALL], 1)
    for name, w in (("ada_w", g["ada_w"]), ("w_mod", g["w_mod_2"])):
        t = w.reshape(2, KD, P, JOBS, JW).transpose(0, 3, 2, 1, 4).reshape(2 * JOBS, P, KD * JW)
        a[name] = np.concatenate([t, np.zeros((2, P, KD * JW), np.float32)])
    w = g["ab_w_in"][0]
    a["in1"] = tiles(np.concatenate([w[:, 0:1024], w[:, 1536:2048], w[:, 2048:2816], w[:, 1024:1536]], 1))
    a["out1"] = tiles(g["ab_w_out"][0])
    a["pool"] = np.concatenate([tiles(g["pool_w"][0, i]) for i in range(4)])
    for name, up, down in (("0", g["ffn_w_up"], g["ffn_w_down"]), ("1", g["w_ffn_up_2"], g["w_ffn_down_2"])):
        for layer in range(2):
            t = tiles(up[layer])
            a[f"up{name}{layer}"] = t.reshape(2, FT, P, D).transpose(1, 0, 2, 3).reshape(2 * FT, P, D)
            a[f"down{name}{layer}"] = np.concatenate([tiles(down[layer][h * FG * P:(h + 1) * FG * P]) for h in range(2)])
    w = g["w_even_in_2"][0]
    low = np.concatenate([w[:, 2048:2064], np.zeros((D, P - 16), np.float32)], 1)
    a["in2"] = tiles(np.concatenate([w[:, 512:1024], w[:, 1536:2048], low, w[:, 1024:1536], w[:, 0:512]], 1))
    a["out2"] = tiles(g["w_even_out_2"][0])
    a["w_gate"] = g["w_gla_gate_2"][0].transpose(1, 0, 2).reshape(16, 4, P)
    a["qkv"] = tiles(g["w_qkv_2"][0])
    a["attout"] = tiles(g["w_att_out_2"][0])
    return {n: np.ascontiguousarray(v) for n, v in a.items()}


def kernel(**inputs):
    import concourse.bacc as bacc
    from concourse.bass_utils import run_bass_kernel_spmd

    nc = bacc.Bacc("TRN2", target_bir_lowering=False, num_devices=1)
    arrays = layout(inputs)
    ins = {n: nc.dram_tensor(f"in_{n}", v.shape, mybir.dt.from_np(v.dtype), kind="ExternalInput").ap()
           for n, v in arrays.items()}
    out = nc.dram_tensor("out_y", (P, KD, LAT), F32, kind="ExternalOutput").ap()
    build(nc, ins, out)
    r = run_bass_kernel_spmd(nc, [{f"in_{n}": v for n, v in arrays.items()}], core_ids=[0])
    return np.ascontiguousarray(r.results[0]["out_y"].transpose(2, 1, 0).reshape(1, LAT, D))
```

```python
from contextlib import ExitStack, contextmanager

import numpy as np

import concourse.bass as bass
from concourse import mybir

F32 = mybir.dt.float32
F32R = mybir.dt.float32r
I32 = mybir.dt.int32
U8 = mybir.dt.uint8
ALU = mybir.AluOpType
ACT = mybir.ActivationFunctionType
AX = mybir.AxisListType

P = 128
D = 1024
KD = D // P
CTX, LAT = 256, 512
TALL = CTX + LAT
CHUNK = 128
LEVELS = 7
F_FF = 2816
FT = F_FF // P
FG = FT // 2
NMOD = 6 * KD
JW = 192
JOBS = 6 * D // JW
ROW_OF = {0: 0, 1: 0, 2: 1}
SEG_OF = {1: 0, 2: 1}
BANK = 512
ALPHA = 4.0 ** 0.25
LN_EPS, RMS_EPS, EPS = 1e-5, 1e-6, 1e-6
EPS_COL = {1e-5: "eps5", 1e-6: "eps6"}
NEG = -1.0e30
TWO_PI = 2.0 * np.pi
LATS = slice(CTX, TALL)
HEAD_ORDER = [0, 2, 4, 6, 1, 3, 5, 7]


class Ticket:

    def __init__(self, counter, value, loop):
        self.counter, self.value, self.loop = counter, value, loop


class Counter:
    def __init__(self, name, sem):
        self.name, self.sem, self.value = name, sem, 0


class Loop:
    def __init__(self, index, count, strides):
        self.index, self.count, self.strides, self.closed = index, count, strides, False


class Program:

    def __init__(self, nc, ctx):
        self.nc, self.loop, self.waited = nc, None, {}
        self.engines = {"pe": nc.tensor, "act": nc.scalar, "dve": nc.vector, "pool": nc.gpsimd, "sp": nc.sync}
        self.counters = {}
        for name in ("pe", "act", "dve", "pool", "w0", "w1", "m0", "m1", "load", "store", "r0", "r1", "turn"):
            self.counters[name] = Counter(name, ctx.enter_context(nc.semaphore(f"done_{name}")))

    def wait(self, engine, *tickets):
        due = []
        for t in tickets:
            if t is None:
                continue
            value = t.value
            if t.loop is not None and t.loop.closed:
                value += (t.loop.count - 1) * t.loop.strides.get(t.counter.name, 0)
            inside = t.loop is not None and not t.loop.closed
            key = (engine, t.counter.name, inside)
            if self.waited.get(key, -1) >= value:
                continue
            self.waited[key] = value
            if inside:
                value = self.engines[engine].snap(value + t.loop.index * t.loop.strides.get(t.counter.name, 0))
            due.append((t.counter.sem, value))
        for sem, value in due:
            self.engines[engine].wait_ge(sem, value)

    def previous(self, t):
        return Ticket(t.counter, t.value - t.loop.strides[t.counter.name], t.loop)

    def done(self, name, instruction, step=1):
        c = self.counters[name]
        instruction.then_inc(c.sem, step)
        c.value += step
        return Ticket(c, c.value, self.loop)

    def at(self, name):
        return Ticket(self.counters[name], self.counters[name].value, self.loop)

    def pe(self, instruction):
        return self.done("pe", instruction)

    def act(self, instruction):
        return self.done("act", instruction)

    def dve(self, instruction):
        return self.done("dve", instruction)

    def pool(self, instruction):
        return self.done("pool", instruction)

    @contextmanager
    def repeat(self, count, **strides):
        start = {k: c.value for k, c in self.counters.items()}
        self.waited = {}
        with self.nc.Fori(0, count) as i:
            loop = self.loop = Loop(i, count, strides)
            yield i
        made = {k: c.value - start[k] for k, c in self.counters.items() if c.value != start[k]}
        assert made == strides, f"a pass of this loop adds {made}"
        loop.closed, self.loop, self.waited = True, None, {}
        for k, n in strides.items():
            self.counters[k].value += (count - 1) * n


class Kernel:
    def __init__(self, nc, ctx, ins, out):
        self.nc, self.ins, self.out = nc, ins, out
        self.p = Program(nc, ctx)
        self.tile = 0
        self.loaded, self.low = [None, None], [None, None]
        self.h_ready = [None] * KD
        self.sums, self.due = None, []
        self.tmp_turn = 0
        self.free_w = [None, None]
        self.free_hl = [None, None]
        self.free_ps = [[], []]
        sb = lambda name, shape, dt=F32: ctx.enter_context(nc.sbuf_tensor(name, shape, dt))
        self.x = sb("x", [P, KD, TALL])
        self.h_hi = sb("h_hi", [P, KD, TALL], F32R)
        self.h_lo = sb("h_lo", [P, KD, TALL], F32R)
        self.w_raw = [sb(f"w_raw{i}", [P, FG * P]) for i in range(2)]
        self.w_hi = [sb(f"w_hi{i}", [P, FG * P], F32R) for i in range(2)]
        self.w_lo = [sb(f"w_lo{i}", [P, FG * P], F32R) for i in range(2)]
        self.ones = sb("ones", [P, P])
        self.ident = sb("ident", [P, P])
        self.mods1 = sb("mods1", [P, 2, NMOD])
        self.mods2 = sb("mods2", [P, 2, NMOD, 2])
        self.small = sb("small", [P, SMALL_COLS])
        self.mean = sb("mean", [P, LAT])
        self.rstd = sb("rstd", [P, TALL])
        self.coef = sb("coef", [P, 4, 2, KD])
        self.c_act = sb("c_act", [P, 3 * KD])
        self.rows = nc.dram_tensor("mod_rows", (4, 2, 6 * D), F32, kind="Internal").ap()
        self.modulations_done = []
        self.columns_read = None
        self.tmp = [sb(f"tmp{i}", [P, LAT]) for i in range(2)]
        self.ps = ctx.enter_context(nc.psum_tensor("ps", [P, 8, BANK], F32))
        self.x_done = self.h_done = self.coef_read = self.bank_free = self.mods_made = self.rstd_free = None
        self.h_plain = [None] * KD
        self.x_tile, self.tmp_free = [None] * KD, [[], []]

    def col(self, name, i=0, n=1):
        at = SMALL[name][0] + i
        return self.small[:, at:at + n]

    def fetch_tile(self, s, name, n, kt):
        p, nc = self.p, self.nc
        if isinstance(n, int):
            at = self.ins[name][n, :, :]
        else:
            at = self.ins[name][bass.ds(nc.sync.snap(n), 1), :, :].rearrange("o p c -> (o p) c")
        p.wait("sp", self.free_w[s])
        self.loaded[s] = p.done(f"w{s}", nc.sync.dma_start(self.w_raw[s][:, 0:kt * P], at), 16)

    def split_tile(self, s, kt):
        p, nc = self.p, self.nc
        raw, hi, lo = (t[s][:, 0:kt * P] for t in (self.w_raw, self.w_hi, self.w_lo))
        p.wait("act", self.loaded[s], self.free_hl[s])
        high = p.act(nc.scalar.activation(hi, raw, ACT.Copy))
        p.wait("dve", high)
        self.low[s] = self.free_w[s] = p.dve(nc.vector.tensor_tensor(lo, raw, hi.bitcast(F32), ALU.subtract))

    def first_tiles(self):
        for g in range(3):
            self.fetch_tile(g % 2, *ORDER[g])
            if g == 0:
                self.split_tile(0, ORDER[0][2])

    def next_tmp(self):
        self.tmp_turn ^= 1
        return self.tmp_turn

    def add_sums(self):
        while self.due:
            self.sums.add(*self.due.pop(0))

    def load(self, dst, src, *after):
        p = self.p
        p.wait("sp", *after)
        return p.done("load", self.nc.sync.dma_start(dst, src), 16)


def _small_table():
    sizes = [("c1", 8), ("cc2", 8), ("c2", 8), ("ada_b", 96), ("mod_b", 96), ("ln_g", 32), ("ln_b", 32),
             ("lb_raw", 4), ("norm_g", 1), ("pool_scale", 8), ("fcw", 2 * 3 * FT), ("fcb", 2 * FT),
             ("gmix", 16), ("gffn", 16), ("gfin", 8), ("bgate", 4), ("ggla", 4), ("gq", 1), ("gk", 1),
             ("cw2", 2 * 3 * 2 * FT), ("cb2", 2 * 2 * FT), ("inv_freq", 1), ("sinks", 8), ("eps5", 1), ("eps6", 1)]
    table, at = {}, 0
    for name, n in sizes:
        table[name] = (at, n)
        at += n
    return table, at


SMALL, SMALL_COLS = _small_table()


def _order():
    def ffn(block, layer):
        return [(f"{kind}{block}{layer}", half * n + i, kt) for half in range(2)
                for kind, n, kt in (("up", 2 * FG, KD), ("down", KD, FG)) for i in range(n)]

    def run(name, n, kt=KD):
        return [(name, i, kt) for i in range(n)]

    return (run("in1", 22) + run("out1", KD) + ffn(0, 0) + run("pool", KD, 2) + ffn(0, 1) + run("in2", 17)
            + run("out2", KD) + ffn(1, 0) + run("qkv", 12) + run("attout", KD) + ffn(1, 1))


ORDER = _order()


def segments(tokens):
    both = [(0, CTX, 0), (CTX, LAT, 1)]
    return both if tokens == TALL else both[1:]


class Stream:

    def __init__(self, k, name, first, count, hi, lo, tokens, ready=None):
        self.k, self.name, self.first, self.count, self.kt = k, name, first, count, ORDER[k.tile][2]
        self.hi, self.lo, self.tokens = hi, lo, tokens
        self.ready = list(k.h_ready[:self.kt]) if ready is None else ready
        self.kept = {}
        self.jobs = None
        assert ORDER[k.tile][:2] == (name, first) and ORDER[k.tile + count - 1][:2] == (name, first + count - 1)

    def host(self, jobs):
        self.jobs, self.job0, self.pending = jobs, 1 if self.count > KD else 0, False
        jobs.start((self.k.tile + self.job0) % 2)
        return self

    def hosted(self, n):
        return not isinstance(n, int) or self.job0 <= n < self.job0 + self.jobs.count

    def product(self, s, low, ps):
        k, p, nc = self.k, self.k.p, self.k.nc
        p.wait("pe", low, *k.free_ps[s])
        wh = k.w_hi[s][:, 0:self.kt * P].rearrange("p (k n) -> p k n", n=P)
        wl = k.w_lo[s][:, 0:self.kt * P].rearrange("p (k n) -> p k n", n=P)
        for c in range(self.kt):
            if self.ready:
                p.wait("pe", self.ready[c])
            for n, (a, b) in enumerate(((wh, self.hi), (wh, self.lo), (wl, self.hi))):
                for t0, tn, bank in segments(self.tokens):
                    t0 -= TALL - b.shape[2]
                    last = nc.tensor.matmul(ps[:, bank, 0:tn], a[:, c, :], b[:, c, t0:t0 + tn],
                                            start=c == 0 and n == 0, stop=c == self.kt - 1 and n == 2)
        self.ready = ()
        product = p.pe(last)
        k.free_hl[s] = product
        return product

    def step(self, n, s, consume):
        k = self.k
        ps = k.ps[:, 2 * s:2 * s + 2, :]
        product = self.product(s, k.low[s], ps)
        if isinstance(n, int):
            if k.tile + 1 < len(ORDER):
                k.split_tile(1 - s, ORDER[k.tile + 1][2])
            if k.tile + 3 < len(ORDER):
                k.fetch_tile(1 - s, *ORDER[k.tile + 3])
            k.tile += 1
        else:
            k.split_tile(1 - s, self.kt)
            k.fetch_tile(1 - s, self.name, n + (3 + self.first), self.kt)
        if self.jobs is not None:
            j = n - self.job0
            if self.pending:
                self.jobs.reduce(j - 1, 1 - s)
            self.pending = self.hosted(n)
            if self.pending:
                self.jobs.compute(j, s)
        k.add_sums()
        k.free_ps[s] = list(consume(n, s, ps, product))

    def run(self, consume, **strides):
        k, p = self.k, self.k.p
        s0, count = k.tile % 2, self.count
        total = {"pe": 2, "act": 2, "dve": 2, "w0": 16, "w1": 16}
        if self.jobs is not None:
            nv = len(self.jobs.vectors)
            for name, n in (("pe", 2), ("act", 2), ("dve", 2 * nv * KD), ("m0", 16), ("m1", 16), ("r0", 16), ("r1", 16)):
                total[name] = total.get(name, 0) + n
        for name, n in strides.items():
            total[name] = total.get(name, 0) + n

        def tiles(ns):
            for n in ns:
                self.step(n, s0 if n % 2 == 0 else 1 - s0, consume)

        passes = (count - 2 - 3) // 2
        if passes < 2:
            tiles(range(count))
        else:
            tiles(range(2))
            with p.repeat(passes, **total) as i:
                carry = lambda t: t and Ticket(t.counter, t.value, p.loop)
                k.free_hl = [carry(t) for t in k.free_hl]
                k.free_w = [carry(t) for t in k.free_w]
                k.free_ps = [[carry(t) for t in ts] for ts in k.free_ps]
                k.low = [carry(t) for t in k.low]
                k.loaded = [carry(t) for t in k.loaded]
                self.kept = {name: carry(t) for name, t in self.kept.items()}
                if self.jobs is not None:
                    self.jobs.kept = {name: carry(t) for name, t in self.jobs.kept.items()}
                    self.jobs.made = carry(self.jobs.made)
                for u in range(2):
                    self.step(i * 2 + (2 + u), s0 if u == 0 else 1 - s0, consume)
            k.tile += 2 * passes
            tiles(range(2 + 2 * passes, count))
        if self.jobs is not None:
            if self.pending:
                self.jobs.reduce(count - 1 - self.job0, (s0 + count - 1) % 2)
            k.modulations_done = self.jobs.read_all()


class Sums:

    def __init__(self, k, tokens, square):
        self.k, self.tokens, self.square, self.count = k, tokens, square, 0

    def add(self, f, written):
        k, p, nc = self.k, self.k.p, self.k.nc
        first, stop = self.count == 0, self.count == KD - 1
        if first:
            p.wait("pe", k.ones_set, k.bank_free, k.columns_read)
        self.count += 1
        for t0, tn, bank in segments(self.tokens):
            value = k.x[:, f, t0:t0 + tn]
            i = k.next_tmp()
            if self.square:
                p.wait("act", written, *k.tmp_free[i])
                squared = p.act(nc.scalar.activation(k.tmp[i][:, 0:tn], value, ACT.Square))
                p.wait("pe", squared)
                value = k.tmp[i][:, 0:tn]
            else:
                p.wait("pe", written)
            self.done = p.pe(nc.tensor.matmul(k.ps[:, 6 + (bank if self.tokens == TALL else 0), 0:tn], k.ones[:, :],
                                              value, start=first, stop=stop))
            if self.square:
                k.tmp_free[i] = [self.done]


class Space:

    def __init__(self, k, ctx, name):
        sb = lambda n, shape: ctx.enter_context(k.nc.sbuf_tensor(f"{n}_{name}", shape, F32))
        self.k = k
        self.raw = [sb(f"m_raw{s}", [P, KD, JW]) for s in range(2)]
        self.acc = [sb(f"m_acc{s}", [P, 2, JW]) for s in range(2)]
        self.row = [sb(f"m_row{s}", [1, 2, JW]) for s in range(2)]


class Modulations:

    def __init__(self, space, block, layer, first, count, vectors):
        k = space.k
        self.k, self.block, self.layer, self.first, self.count, self.vectors = k, block, layer, first, count, vectors
        nv = len(vectors)
        self.raw = space.raw
        self.acc, self.row = ([t[:, 0:nv, :] for t in ts] for ts in (space.acc, space.row))
        self.kept = {"stored0": k.p.at("r0"), "stored1": k.p.at("r1")}
        self.after = list(k.modulations_done)

    def fetch(self, j, s, *after):
        k, p = self.k, self.k.p
        first = (self.layer * JOBS) + self.first
        src = k.ins["ada_w" if self.block == 0 else "w_mod"]
        if isinstance(j, int):
            at = src[first + j, :, :]
        else:
            at = src[bass.ds(k.nc.sync.snap(j + first), 1), :, :].rearrange("o p c -> (o p) c")
        p.wait("sp", *after)
        self.kept[f"loaded{s}"] = p.done(f"m{s}", k.nc.sync.dma_start(
            self.raw[s][:, :, :].rearrange("p k n -> p (k n)"), at), 16)

    def start(self, s0, *after):
        self.fetch(0, s0, *self.after, *after)
        self.fetch(1, 1 - s0)

    def compute(self, j, s):
        k, p, nc = self.k, self.k.p, self.k.nc
        static = isinstance(j, int)
        p.wait("dve", self.kept[f"loaded{s}"], self.kept[f"stored{s}"], k.c_done if static else None)
        made = [None] * len(self.vectors)
        for kk in range(KD):
            for i, v in enumerate(self.vectors):
                c = k.c_act[:, v * KD + kk:v * KD + kk + 1]
                w, acc = self.raw[s][:, kk, :], self.acc[s][:, i, :]
                if kk == 0:
                    made[i] = p.dve(nc.vector.tensor_scalar(acc, w, c, None, ALU.mult))
                else:
                    p.wait("dve", made[i])
                    made[i] = p.dve(nc.vector.scalar_tensor_tensor(acc, w, c, acc, ALU.mult, ALU.add))
        self.made = made[-1]
        if not static or j + 2 < self.count:
            self.fetch(j + 2, s, self.made)

    def reduce(self, j, s):
        k, p, nc = self.k, self.k.p, self.k.nc
        p.wait("pe", self.made, self.kept[f"stored{s}"], k.ones_set if isinstance(j, int) else None)
        for i in range(len(self.vectors)):
            last = nc.tensor.matmul(k.ps[0:1, 4 + s, i * JW:(i + 1) * JW], k.ones[:, 0:1], self.acc[s][:, i, :],
                                    start=True, stop=True)
        summed = p.pe(last)
        p.wait("act", summed, self.kept[f"stored{s}"])
        n = len(self.vectors) * JW
        row = self.row[s][:, :, :].rearrange("p v n -> p (v n)")
        read = p.act(nc.scalar.activation(row, k.ps[0:1, 4 + s, 0:n], ACT.Copy))
        v0 = ROW_OF[self.vectors[0]]
        rows = k.rows[self.block * 2 + self.layer, :, :].rearrange("v (j n) -> v j n", n=JW)[v0:v0 + len(self.vectors)]
        if isinstance(j, int):
            out = rows[:, self.first + j, :]
        else:
            out = rows[:, bass.ds(nc.gpsimd.snap(j + self.first), 1), :].rearrange("v o n -> v (o n)")
        p.wait("pool", read)
        self.kept[f"stored{s}"] = p.done(
            f"r{s}", nc.gpsimd.dma_start(out.unsqueeze(0), self.row[s][:, :, :]), 16)
        self.stores = [self.kept["stored0"], self.kept["stored1"]]

    def read_all(self):
        return [self.made, *self.stores]


class Stages(Kernel):
    def constants(self):
        p, nc, ins = self.p, self.nc, self.ins
        self.load(self.small[:, :], ins["small"])
        self.load(self.ident[:, :], ins["ident"])
        self.load(self.x[:, :, LATS], ins["x"])
        self.consts = self.load(self.x[:, :, 0:CTX], ins["ctx"])
        self.ones_set = p.pool(nc.gpsimd.memset(self.ones[:, :], 1.0))

    def condition_start(self):
        p, nc = self.p, self.nc
        p.wait("act", self.consts)
        self.c_done = p.act(nc.scalar.activation(self.c_act[:, :], self.col("c1", 0, 3 * KD), ACT.Silu))
        with ExitStack() as ctx:
            jobs = Modulations(Space(self, ctx, "start"), 0, 0, 0, JOBS // 2 - 1, [0])
            jobs.start(0)
            for n in range(jobs.count):
                jobs.compute(n, n % 2)
                jobs.reduce(n, n % 2)
            self.modulations_done = jobs.read_all()
        self.columns_of(0, 0, [0], 0, 2 * KD)

    def columns_of(self, block, layer, vectors, f0, f1):
        p, nc = self.p, self.nc
        n, nv = f1 - f0, len(vectors)
        mods = self.mods1 if block == 0 else self.mods2
        turn = self.rstd[0:NMOD, 0:2 * P].rearrange("f (v c) -> f v c", v=2)
        rows = self.rows[block * 2 + layer, :, :].rearrange("v (f c) -> v f c", c=P)
        for v in range(nv):
            p.wait("sp", *self.modulations_done, self.rstd_free)
            loaded = p.done("turn", nc.sync.dma_start(turn[0:n, v, :], rows[ROW_OF[vectors[v]], f0:f1, :]), 16)
        p.wait("pe", loaded, self.columns_read)
        for v in range(nv):
            last = nc.tensor.matmul(self.ps[:, 7, v * n:(v + 1) * n], turn[0:n, v, :], self.ident[0:n, 0:n],
                                    is_transpose=True, start=True, stop=True)
        self.rstd_free = turned = p.pe(last)
        p.wait("dve", turned, self.consts)
        bias = self.col("ada_b" if block == 0 else "mod_b", layer * NMOD + f0, n)
        for v in range(nv):
            out = mods[:, layer, f0:f1] if block == 0 else mods[:, layer, f0:f1, SEG_OF[vectors[v]]]
            made = p.dve(nc.vector.tensor_tensor(out, self.ps[:, 7, v * n:(v + 1) * n], bias, ALU.add))
        self.columns_read = self.mods_made = made
        p.wait("dve", made)
        for m in (KD, 4 * KD):
            if f0 <= m < f1:
                for v in range(nv):
                    out = mods[:, layer, m:m + KD] if block == 0 else mods[:, layer, m:m + KD, SEG_OF[vectors[v]]]
                    self.mods_made = p.dve(nc.vector.tensor_scalar(out, out, 1.0, None, ALU.add))

    def mod(self, block, layer, m, f, seg=1):
        at = m * KD + f if isinstance(f, int) else f + m * KD
        at = slice(at, at + 1) if isinstance(at, int) else bass.ds(at, 1)
        if block == 0:
            return self.mods1[:, layer, at]
        return self.mods2[:, layer, at, seg]

    def split(self, f, t0, tn, value, made):
        p, nc = self.p, self.nc
        hi, lo = self.h_hi[:, f, t0:t0 + tn], self.h_lo[:, f, t0:t0 + tn]
        p.wait("act", made)
        high = p.act(nc.scalar.activation(hi, value, ACT.Copy))
        p.wait("dve", high)
        self.h_ready[f] = p.dve(nc.vector.tensor_tensor(lo, value, hi.bitcast(F32), ALU.subtract))
        return self.h_ready[f]

    def residual(self, block, layer, m, tokens, gate=None):
        x_ready = self.x_done

        def consume(n, s, ps, product):
            p, nc = self.p, self.nc
            p.wait("dve", product, x_ready if isinstance(n, int) else None)
            for t0, tn, bank in segments(tokens):
                g = self.mod(block, layer, m, n, seg=bank) if gate is None else gate(n)
                x = self.x[:, n if isinstance(n, int) else bass.ds(n, 1), t0:t0 + tn]
                if not isinstance(n, int):
                    x = x.rearrange("p o t -> p (o t)")
                done = p.dve(nc.vector.scalar_tensor_tensor(x, ps[:, bank, 0:tn], g, x, ALU.mult, ALU.add))
            self.x_done = done
            if self.sums is not None:
                self.due.append((n, done))
            return (done,)
        return consume

    def reciprocal_root(self, r, total, width, eps, made):
        p, nc = self.p, self.nc
        p.wait("act", made, self.rstd_free)
        log = self.bank_free = p.act(nc.scalar.activation(r, total, ACT.Ln, scale=1.0 / width, bias=self.col(EPS_COL[eps])))
        p.wait("act", log)
        return p.act(nc.scalar.activation(r, r, ACT.Exp, scale=-0.5))

    def coefficients(self, block, layer, m, which, seg):
        p, nc = self.p, self.nc
        scale, shift = (self.mods1[:, layer, i * KD:(i + 1) * KD] if block == 0 else
                        self.mods2[:, layer, i * KD:(i + 1) * KD, seg] for i in (m + 1, m))
        g, b, ga, ba = (self.coef[:, i, seg, :] for i in range(4))
        p.wait("dve", self.mods_made, self.consts, self.coef_read)
        if block == 1:
            made = p.dve(nc.vector.tensor_tensor(g, scale, self.col(which, layer * KD, KD), ALU.mult))
            p.dve(nc.vector.tensor_copy(b, shift))
            return p.at("dve")
        made = p.dve(nc.vector.tensor_tensor(b, scale, self.col("ln_b", which * KD, KD), ALU.mult))
        p.dve(nc.vector.tensor_tensor(g, scale, self.col("ln_g", which * KD, KD), ALU.mult))
        p.dve(nc.vector.tensor_scalar(ga, self.col("ln_g", which * KD, KD), ALPHA, None, ALU.mult))
        p.dve(nc.vector.tensor_scalar(ba, self.col("ln_b", which * KD, KD), ALPHA, None, ALU.mult))
        p.wait("dve", made)
        return p.dve(nc.vector.tensor_tensor(b, b, shift, ALU.add))

    def modulated(self, f, t0, tn, xr, seg, made, plain=None):
        p, nc = self.p, self.nc
        g, b = self.coef[:, 0, seg, f:f + 1], self.coef[:, 1, seg, f:f + 1]
        i = self.next_tmp()
        h = self.tmp[i][:, 0:tn] if plain is None else plain[:, f, :]
        p.wait("dve", made, *(self.tmp_free[i] if plain is None else ()))
        value = p.dve(nc.vector.tensor_scalar(h, xr, g, b, ALU.mult, ALU.add))
        if plain is None:
            self.h_done = self.split(f, t0, tn, h, value)
            self.tmp_free[i] = [self.h_done]
        else:
            self.h_done = self.h_plain[f] = value
        return value

    def layer_norm(self, which, layer=None, m=None, plain=None):
        p, nc = self.p, self.nc
        t0, tn = CTX, LAT
        mean, r = self.mean[:, :], self.rstd[:, t0:t0 + tn]
        ready = self.coefficients(0, layer, m, which, 1) if m is not None else None
        self.add_sums()
        p.wait("act", self.sums.done)
        made = self.bank_free = p.act(nc.scalar.activation(mean, self.ps[:, 6, 0:tn], ACT.Copy, scale=1.0 / D))
        self.sums = Sums(self, LAT, True)
        for f in range(KD):
            x = self.x[:, f, t0:t0 + tn]
            p.wait("dve", made)
            self.x_tile[f] = p.dve(nc.vector.tensor_tensor(x, x, mean, ALU.subtract))
            self.sums.add(f, self.x_tile[f])
        rstd = self.reciprocal_root(r, self.ps[:, 6, 0:tn], D, LN_EPS, self.sums.done)
        self.sums = None
        p.wait("dve", rstd, ready)
        if m is not None:
            p.wait("pool", ready)
        for f in range(KD):
            x = self.x[:, f, t0:t0 + tn]
            xr = p.dve(nc.vector.tensor_tensor(x, x, r, ALU.mult))
            if m is None:
                p.wait("dve", xr)
                self.x_tile[f] = p.dve(nc.vector.tensor_scalar(x, x, self.col("ln_g", which * KD + f),
                                                               self.col("ln_b", which * KD + f), ALU.mult, ALU.add))
            else:
                value = self.modulated(f, t0, tn, x, 1, xr, plain)
                p.wait("pool", value)
                self.x_tile[f] = p.pool(nc.gpsimd.tensor_scalar(x, x, self.coef[:, 2, 1, f:f + 1], self.coef[:, 3, 1, f:f + 1],
                                                                ALU.mult, ALU.add))
        self.rstd_free = xr
        self.x_done = self.coef_read = self.x_tile[KD - 1]

    def modulate_first(self):
        p, nc = self.p, self.nc
        g, b = self.coef[:, 0, 1, :], self.coef[:, 1, 1, :]
        p.wait("dve", self.mods_made)
        p.dve(nc.vector.tensor_copy(g, self.mods1[:, 0, KD:2 * KD]))
        ready = p.dve(nc.vector.tensor_copy(b, self.mods1[:, 0, 0:KD]))
        for f in range(KD):
            x = self.x[:, f, LATS]
            value = self.modulated(f, CTX, LAT, x, 1, ready)
            p.wait("pool", value)
            self.x_tile[f] = p.pool(nc.gpsimd.tensor_scalar(x, x, ALPHA, None, ALU.mult))
        self.x_done = self.coef_read = self.x_tile[KD - 1]

    def rms_modulate(self, layer, m, gain, tokens):
        p, nc = self.p, self.nc
        for _, _, bank in segments(tokens):
            ready = self.coefficients(1, layer, m, gain, bank)
        self.add_sums()
        roots = {}
        for t0, tn, bank in segments(tokens):
            roots[bank] = self.reciprocal_root(self.rstd[:, t0:t0 + tn], self.ps[:, 6 + (bank if tokens == TALL else 0), 0:tn],
                                               D, EPS, self.sums.done)
        self.sums = None
        for f in range(KD):
            for t0, tn, bank in segments(tokens):
                x = self.x[:, f, t0:t0 + tn]
                i = self.next_tmp()
                xr = self.tmp[i][:, 0:tn]
                p.wait("dve", roots[bank], ready, *self.tmp_free[i])
                scaled = p.dve(nc.vector.tensor_tensor(xr, x, self.rstd[:, t0:t0 + tn], ALU.mult))
                p.wait("dve", scaled)
                value = p.dve(nc.vector.tensor_scalar(xr, xr, self.coef[:, 0, bank, f:f + 1], self.coef[:, 1, bank, f:f + 1],
                                                      ALU.mult, ALU.add))
                self.h_done = self.split(f, t0, tn, xr, value)
                self.tmp_free[i] = [self.h_done]
        self.rstd_free = self.coef_read = self.h_done

    def ffn(self, block, layer, tokens, sums, hosting=None):
        p, nc = self.p, self.nc
        with ExitStack() as ctx:
            sb = lambda name, shape, dt=F32: ctx.enter_context(nc.sbuf_tensor(f"{name}_{block}{layer}", shape, dt))
            t_first = TALL - tokens
            g_hi, g_lo = sb("g_hi", [P, FG, tokens], F32R), sb("g_lo", [P, FG, tokens], F32R)
            conv = [sb("conv_u", [P, TALL]), sb("conv_v", [P, TALL])]
            act = sb("silu_u", [P, TALL])
            g = sb("gated", [P, TALL])
            self.job_space = Space(self, ctx, f"{block}{layer}") if hosting else None
            cw, cb, parts = ("fcw", "fcb", 1) if block == 0 else ("cw2", "cb2", 2)
            base_w, base_b = SMALL[cw][0], SMALL[cb][0]
            down_done = self.h_done
            for half in range(2):
                up = Stream(self, f"up{block}{layer}", half * 2 * FG, 2 * FG, self.h_hi, self.h_lo, tokens)
                if hosting:
                    up.host(hosting.pop(0)(self.job_space))

                def taps(j, part, tap):
                    width = parts * 3 * FT
                    at = base_w + layer * width + (part * 3 + tap) * FT + half * FG
                    return self.small[:, at + j:at + j + 1] if isinstance(j, int) else self.small[:, bass.ds(j + at, 1)]

                def bias(j, part):
                    at = base_b + layer * parts * FT + part * FT + half * FG
                    return self.small[:, at + j:at + j + 1] if isinstance(j, int) else self.small[:, bass.ds(j + at, 1)]

                def convolve(j, part, ps, product, kept):
                    out = conv[part]
                    shifts = ((2, 0), (1, 1), (0, 2)) if block == 0 else ((1, 0), (0, 1), (-1, 2))
                    p.wait("act", product, kept)
                    for t0, tn, bank in segments(tokens):
                        centre = next(tap for d, tap in shifts if d == 0)
                        first = p.act(nc.scalar.activation(out[:, t0:t0 + tn], ps[:, bank, 0:tn], ACT.Identity,
                                                           scale=taps(j, part, centre), bias=bias(j, part)))
                    last = first
                    for d, tap in shifts:
                        if d == 0:
                            continue
                        p.wait("dve", last)
                        for t0, tn, bank in segments(tokens):
                            lo, hi = max(d, 0), tn + min(d, 0)
                            o = out[:, t0 + lo:t0 + hi]
                            last = p.dve(nc.vector.scalar_tensor_tensor(o, ps[:, bank, lo - d:hi - d], taps(j, part, tap),
                                                                        o, ALU.mult, ALU.add))
                    return last

                tall = slice(t_first, TALL)

                def consume(n, s, ps, product):
                    if isinstance(n, int):
                        is_u, j = n % 2 == 0, n // 2
                    else:
                        is_u, j = s == consume.s0, consume.pair
                    if is_u:
                        made = convolve(j, 0, ps, product, up.kept.get("silu"))
                        p.wait("act", made, up.kept.get("gated"))
                        up.kept["silu"] = p.act(nc.scalar.activation(act[:, tall], conv[0][:, tall], ACT.Silu))
                        return (made,)
                    where = j if isinstance(j, int) else bass.ds(j, 1)
                    hi, lo = g_hi[:, where, :], g_lo[:, where, :]
                    if not isinstance(j, int):
                        hi, lo = hi.rearrange("p o t -> p (o t)"), lo.rearrange("p o t -> p (o t)")
                    if block == 1:
                        made = convolve(j, 1, ps, product, up.kept.get("gated"))
                        p.wait("dve", made, up.kept["silu"], up.kept.get("low"))
                        gated = p.dve(nc.vector.tensor_tensor(g[:, tall], act[:, tall], conv[1][:, tall], ALU.mult))
                        read = made
                    else:
                        p.wait("dve", product, up.kept["silu"], up.kept.get("low"))
                        read = gated = p.dve(nc.vector.tensor_tensor(g[:, tall], act[:, tall], ps[:, 1, 0:LAT], ALU.mult))
                    up.kept["gated"] = gated
                    p.wait("act", gated, down_done)
                    high = p.act(nc.scalar.activation(hi, g[:, tall], ACT.Copy))
                    p.wait("dve", high)
                    low = up.kept["low"] = p.dve(nc.vector.tensor_tensor(lo, g[:, tall], hi.bitcast(F32), ALU.subtract))
                    self.g_ready = [*self.g_ready[1:], low]
                    return (read,)

                consume.s0 = self.tile % 2
                self.g_ready = [None, None]
                self.run_pairs(up, consume, block, tokens)
                if half == 1:
                    self.sums = sums
                ready = [self.g_ready[0]] * (FG - 1) + [self.g_ready[1]]
                down = Stream(self, f"down{block}{layer}", half * KD, KD, g_hi, g_lo, tokens, ready)
                if hosting:
                    down.host(hosting.pop(0)(self.job_space))
                down.run(self.residual(block, layer, 5, tokens))
                down_done = self.free_hl[1 - self.tile % 2]
                if half == 1 and hosting:
                    hosting.pop(0)()

    def run_pairs(self, up, consume, block, tokens):
        n_seg = len(segments(tokens))
        conv = n_seg * (1 if block == 0 else 2)
        orig = up.step

        def step(n, s, c):
            if not isinstance(n, int):
                consume.pair = self.p.loop.index + 1
            orig(n, s, c)

        up.step = step
        up.run(consume, act=conv + 2, dve=2 * conv + 2)

    def keep(self, dst, tokens, scale=1.0, func=ACT.Copy):
        t_first = TALL - tokens

        def consume(n, s, ps, product):
            p, nc = self.p, self.nc
            p.wait("act", product, self.z_free if isinstance(n, int) else None)
            for t0, tn, bank in segments(tokens):
                at = dst[:, n if isinstance(n, int) else bass.ds(n, 1), t0 - t_first:t0 - t_first + tn]
                if not isinstance(n, int):
                    at = at.rearrange("p o t -> p (o t)")
                self.z_done = p.act(nc.scalar.activation(at, ps[:, bank, 0:tn], func, scale=scale))
            return (self.z_done,)
        return consume

    def straight(self, name, first, count, tokens, consume, **strides):
        Stream(self, name, first, count, self.h_hi, self.h_lo, tokens).run(consume, **strides)

    def decayed_products(self, levels, att, masks, q, k, b, comb, width, heads_of, ready, backward, first_mask):
        p, nc = self.p, self.nc
        n_tok = width
        read = ready
        for level in range(levels):
            half = 1 << level
            v = lambda a: a.rearrange("p (n c) -> p n c", c=2 * half)
            bb, cc, qq, kk = v(b), v(comb), v(q), v(k)
            left, right = slice(0, half), slice(half, 2 * half)
            shape = [P, n_tok // (2 * half), half]
            p.wait("dve", read)
            if not backward:
                mid = bb[:, :, half - 1:half].to_broadcast(shape)
                p.dve(nc.vector.tensor_tensor(cc[:, :, left], mid, bb[:, :, left], ALU.subtract))
                made = p.dve(nc.vector.tensor_tensor(cc[:, :, right], bb[:, :, right], mid, ALU.subtract))
                sides = ((left, kk), (right, qq))
            else:
                mid = bb[:, :, half:half + 1].to_broadcast(shape)
                p.dve(nc.vector.tensor_tensor(cc[:, :, left], mid, bb[:, :, left], ALU.subtract))
                made = p.dve(nc.vector.tensor_tensor(cc[:, :, right], bb[:, :, right], mid, ALU.subtract))
                sides = ((left, qq), (right, kk))
            p.wait("act", made)
            decays = p.act(nc.scalar.activation(comb, comb, ACT.Exp))
            p.wait("dve", decays)
            for side, factor in sides:
                made = p.dve(nc.vector.tensor_tensor(cc[:, :, side], cc[:, :, side], factor[:, :, side], ALU.mult))
            read = self.products_to(att, [(comb, comb)], heads_of, made, masks[:, first_mask + level, :])
        return read

    def load_masks(self, masks, name, att, after):
        p, nc = self.p, self.nc
        n = masks.shape[1]
        wide = att[:, 0:n, :].bitcast(I32)
        loaded = self.load(wide, self.ins[name], after)
        p.wait("pool", loaded)
        packed = p.pool(nc.gpsimd.tensor_copy(masks[:, :, :], wide))
        p.wait("pool", packed)
        return packed, p.pool(nc.gpsimd.memset(att[:, :, :], 0.0))

    def products_to(self, att, pairs, units, made, mask):
        p, nc = self.p, self.nc
        lhs, rhs = pairs[0]
        last = None
        for b0 in range(0, len(units), 8):
            pair = (b0 // 8) % 2
            group = units[b0:b0 + 8]
            p.wait("pe", made, self.att_free[pair])
            for i, (rows, cols) in enumerate(group):
                out = self.ps[:, 4 + 2 * pair + i // 4, (i % 4) * P:(i % 4 + 1) * P]
                last = nc.tensor.matmul(out, lhs[rows, cols], rhs[rows, cols], start=True, stop=True)
            last = p.pe(last)
            p.wait("dve", last)
            n = len(group)
            got = self.ps[:, 4 + 2 * pair:6 + 2 * pair, :].rearrange("p b (i t) -> p (b i) t", t=P)[:, 0:n, :]
            self.att_free[pair] = self.att_done = p.dve(nc.vector.copy_predicated(
                att[:, b0:b0 + n, :], mask.unsqueeze(1).to_broadcast([P, n, P]), got))
        return last

    def even_mixer1(self):
        p, nc, ins = self.p, self.nc, self.ins
        self.z_free = None
        NC = LAT // CHUNK
        with ExitStack() as ctx:
            sb = lambda name, shape, dt=F32: ctx.enter_context(nc.sbuf_tensor(name, shape, dt))
            z = sb("z1", [P, 22, LAT])
            v = sb("v1", [P, NC, 5 * P])
            with ExitStack() as inner:
                st = Stream(self, "in1", 0, 22, self.h_hi, self.h_lo, LAT)
                st.host(Modulations(Space(self, inner, "in1"), 0, 0, JOBS // 2 - 1, JOBS // 2 + 1, [0]))
                st.run(self.keep(z, LAT), act=2)
                self.columns_of(0, 0, [0], 2 * KD, NMOD)
            for f in range(5):
                units = [(slice(0, P), slice(t * P, (t + 1) * P)) for t in range(NC)]
                self.transposes(v[:, :, f * P:(f + 1) * P], z[:, 17 + f, :], units, self.z_done)
            self.z_done = self.evicted
            zk = z[:, 16:17, :]
            z_done = self.z_done
            self.hgrn(ins, z, v, z_done)
            self.window_attention(ins, z, zk, v, z_done)
            self.sums = Sums(self, LAT, False)
            self.straight("out1", 0, KD, LAT, self.residual(0, 0, 2, LAT), dve=2)

    def hgrn(self, ins, z, v, z_done):
        p, nc = self.p, self.nc
        H, NC = 4, LAT // CHUNK
        W = H * LAT
        with ExitStack() as ctx:
            sb = lambda name, shape, dt=F32: ctx.enter_context(nc.sbuf_tensor(name, shape, dt))
            flat = lambda a, i: a[:, i:i + H, :].rearrange("p h t -> p (h t)")
            q, f, gate = flat(z, 0), flat(z, 4), flat(z, 8)
            k = sb("hk", [P, W])
            b = sb("hb", [P, W])
            comb = sb("hcomb", [P, W])
            att = sb("hatt", [P, H * NC, P])
            kd_t = flat(z, 18).rearrange("p (n c) -> p n c", c=P)
            state = f.rearrange("p (h c v) -> p h c v", h=H, c=NC)
            reset = self.mean
            masks = sb("hmasks", [P, LEVELS + 1, P], U8)
            lb = sb("hlb", [P, 4 * H])
            loaded = self.load(reset[:, :], ins["reset1"])
            loaded, zeroed = self.load_masks(masks, "masks1", att, None)
            raw, e, prob, one_less = (lb[:, i * H:(i + 1) * H] for i in range(4))
            p.wait("dve", self.consts)
            made = p.dve(nc.vector.tensor_tensor(e, self.col("lb_raw", 0, H), self.col("lb_raw", 0, H), ALU.subtract))
            p.wait("act", made, z_done)
            made = p.act(nc.scalar.activation(e, e, ACT.Exp))
            p.wait("dve", made)
            made = p.dve(nc.vector.reciprocal(raw, e))
            p.wait("dve", made)
            made = p.dve(nc.vector.tensor_tensor(prob, e, raw, ALU.mult))
            p.wait("dve", made)
            made = p.dve(nc.vector.tensor_tensor(raw, prob, prob, ALU.subtract))
            p.wait("dve", made)
            lower = p.dve(nc.vector.tensor_scalar(one_less, raw, -1.0, 1.0, ALU.mult, ALU.add))
            p.wait("dve", z_done)
            made = p.dve(nc.vector.tensor_scalar(f, f, -1.0, 80.0, ALU.mult, ALU.min))
            p.wait("act", made)
            made = p.act(nc.scalar.activation(k[:, :], f, ACT.Exp))
            p.wait("dve", made)
            made = p.dve(nc.vector.tensor_scalar(f, k[:, :], 1.0, None, ALU.add))
            p.wait("dve", made)
            made = p.dve(nc.vector.reciprocal(f, f))
            p.wait("dve", made, lower)
            made = p.dve(nc.vector.tensor_tensor(k[:, :], k[:, :], f, ALU.mult))
            p.wait("dve", made)
            for h in range(H):
                at = slice(h * LAT, (h + 1) * LAT)
                p.dve(nc.vector.tensor_scalar(k[:, at], k[:, at], one_less[:, h:h + 1], None, ALU.mult))
                gates = p.dve(nc.vector.tensor_scalar(f[:, at], f[:, at], one_less[:, h:h + 1], raw[:, h:h + 1],
                                                      ALU.mult, ALU.add))
            p.wait("act", gates)
            logs = p.act(nc.scalar.activation(f, f, ACT.Ln))
            p.wait("dve", logs, loaded)
            for h in range(H):
                at = slice(h * LAT, (h + 1) * LAT)
                summed = p.dve(nc.vector.tensor_tensor_scan(b[:, at], reset[:, :], f[:, at], 0.0, ALU.mult, ALU.add))
            units = [(slice(0, P), slice(h * LAT + c * CHUNK, h * LAT + (c + 1) * CHUNK))
                     for h in range(H) for c in range(NC)]
            p.wait("dve", zeroed)
            self.products_to(att, [(k, q)], units, summed, masks[:, LEVELS, :])
            read = self.decayed_products(LEVELS, att, masks, q, k[:, :], b[:, :], comb[:, :], W, units, summed, False, 0)
            v3 = lambda a: a.rearrange("p (n c) -> p n c", c=CHUNK)
            ends = v3(b[:, :])[:, :, CHUNK - 1:CHUNK]
            p.wait("dve", read, summed)
            made = p.dve(nc.vector.tensor_tensor(v3(comb[:, :]), ends.to_broadcast([P, H * NC, CHUNK]), v3(b[:, :]), ALU.subtract))
            p.wait("act", made)
            made = p.act(nc.scalar.activation(comb[:, :], comb[:, :], ACT.Exp))
            p.wait("dve", made)
            made = p.dve(nc.vector.tensor_tensor(comb[:, :], comb[:, :], k[:, :], ALU.mult))
            kd_read = self.transposes(kd_t, comb, units, made)
            p.wait("act", self.att_done, read)
            qd = k
            p.wait("act", made)
            e2 = p.act(nc.scalar.activation(qd[:, :], b[:, :], ACT.Exp))
            ends_e = reset
            made_e = p.act(nc.scalar.activation(ends_e[:, 0:H * NC].unsqueeze(2), ends, ACT.Exp))
            p.wait("dve", e2)
            q_done = p.dve(nc.vector.tensor_tensor(qd[:, :], qd[:, :], q, ALU.mult))
            p.wait("pe", self.evicted, self.att_free[0], self.att_free[1])
            p.wait("dve", made_e)
            zero = p.dve(nc.vector.memset(state[:, :, 0, :], 0.0))
            for c in range(NC - 1):
                for h in range(H):
                    last = nc.tensor.matmul(self.ps[:, 4 + c, h * P:(h + 1) * P], kd_t[:, h * NC + c, :],
                                            v[:, c, (1 + h) * P:(2 + h) * P], start=True, stop=True)
                got = p.pe(last)
                p.wait("dve", got, zero)
                for h in range(H):
                    zero_next = p.dve(nc.vector.scalar_tensor_tensor(
                        state[:, h, c + 1, :], state[:, h, c, :], ends_e[:, h * NC + c:h * NC + c + 1],
                        self.ps[:, 4 + c, h * P:(h + 1) * P], ALU.mult, ALU.add))
                zero = zero_next
            p.wait("pe", self.att_done, q_done, zero)
            outs = []
            for h in range(H):
                for c in range(NC):
                    out = self.ps[:, 4 + h, c * P:(c + 1) * P]
                    nc.tensor.matmul(out, v[:, c, (1 + h) * P:(2 + h) * P], att[:, h * NC + c, :], start=True, stop=False)
                    last = nc.tensor.matmul(out, state[:, h, c, :], qd[:, h * LAT + c * CHUNK:h * LAT + (c + 1) * CHUNK],
                                            start=False, stop=True)
                outs.append(p.pe(last))
            for h in range(H):
                at = slice(h * LAT, (h + 1) * LAT)
                o = comb[:, at]
                p.wait("act", outs[h], kd_read)
                copied = p.act(nc.scalar.activation(o, self.ps[:, 4 + h, :], ACT.Copy))
                squared = self.head_norm(o, 4 + h, P, RMS_EPS, copied, LAT)
                p.wait("dve", squared, copied)
                made = p.dve(nc.vector.scalar_tensor_tensor(o, o, self.col("norm_g"), self.rstd[:, 0:LAT], ALU.mult, ALU.mult))
                p.wait("act", made)
                silu = p.act(nc.scalar.activation(gate[:, at], gate[:, at], ACT.Silu))
                p.wait("dve", silu)
                made = p.dve(nc.vector.tensor_tensor(o, o, gate[:, at], ALU.mult))
                self.rstd_free = made
                self.h_done = self.split(h, CTX, LAT, o, made)
            self.att_free = [self.h_done, self.h_done]

    def head_norm(self, value, bank, width, eps, made, tn):
        p, nc = self.p, self.nc
        i = self.next_tmp()
        t = self.tmp[i][:, 0:tn]
        p.wait("act", made, *self.tmp_free[i])
        squared = p.act(nc.scalar.activation(t, value, ACT.Square))
        p.wait("pe", squared, made)
        summed = p.pe(nc.tensor.matmul(self.ps[:, bank, 0:tn], self.ones[:, :], t, start=True, stop=True))
        self.tmp_free[i] = [summed]
        keep = self.bank_free
        rstd = self.reciprocal_root(self.rstd[:, 0:tn], self.ps[:, bank, 0:tn], width, eps, summed)
        self.bank_free = keep
        return rstd

    def transposes(self, dst, src, units, made):
        p, nc = self.p, self.nc
        for b0 in range(0, len(units), 8):
            pair = (b0 // 8) % 2
            group = units[b0:b0 + 8]
            p.wait("pe", made, self.att_free[pair])
            rows_n = group[0][0].stop - group[0][0].start
            for i, (rows, cols) in enumerate(group):
                last = nc.tensor.matmul(self.ps[:, 4 + 2 * pair + i // 4, (i % 4) * P:(i % 4) * P + rows_n], src[rows, cols],
                                        self.ident[rows, rows], is_transpose=True, start=True, stop=True)
            last = p.pe(last)
            p.wait("act", last)
            n = len(group)
            got = self.ps[:, 4 + 2 * pair:6 + 2 * pair, :].rearrange("p b (i t) -> p (b i) t", t=P)[:, 0:n, 0:rows_n]
            self.att_free[pair] = self.evicted = p.act(nc.scalar.activation(dst[:, b0:b0 + n, 0:rows_n], got, ACT.Copy))
        return last

    def window_attention(self, ins, z, zk, v, z_done):
        p, nc = self.p, self.nc
        NB, QT, NQ = LAT // P, 4, 8
        with ExitStack() as ctx:
            sb = lambda name, shape, dt=F32: ctx.enter_context(nc.sbuf_tensor(name, shape, dt))
            pos_i = sb("pos_i", [P, LAT], I32)
            ang, turns = sb("ang", [P, LAT]), sb("turns", [P, LAT])
            sin, cos = sb("sin1", [P, LAT]), sb("cos1", [P, LAT])
            rot = sb("rot1", [P, 3, P])
            kk = sb("kk1", [P, 2, LAT])
            mask = sb("wmask", [P, 2 * P])
            s = sb("scores1", [P, NQ, 2 * P])
            pt = sb("probs1t", [P, 2 * NQ, P])
            m, rs, es = sb("wm", [P, NQ]), sb("wrs", [P, NQ]), sb("wes", [P, NQ])
            o = z[:, 8:12, :]
            self.load(rot[:, :, :], ins["rot1"], self.h_done)
            self.load(mask[:, :], ins["wmask"])
            loaded = self.load(pos_i[:, :], ins["positions"].to_broadcast([P, LAT]))
            p.wait("dve", loaded, self.h_done)
            made = p.dve(nc.vector.tensor_copy(ang[:, :], pos_i[:, :]))
            p.wait("dve", made)
            angles = p.dve(nc.vector.tensor_scalar(ang[:, :], ang[:, :], self.col("inv_freq"), None, ALU.mult))
            parts = [6.28125, 0.0019350051879882812, 3.0199159819e-07]
            for dst, quarter in ((sin, 0.0), (cos, 0.25)):
                p.wait("dve", angles)
                made = p.dve(nc.vector.tensor_scalar(turns[:, :], ang[:, :], float(1.0 / TWO_PI), quarter, ALU.mult, ALU.add))
                p.wait("dve", made)
                made = p.dve(nc.vector.tensor_scalar(turns[:, :], turns[:, :], 12582912.0, -12582912.0, ALU.add, ALU.add))
                src = ang
                for part in parts:
                    p.wait("dve", made)
                    made = p.dve(nc.vector.scalar_tensor_tensor(dst[:, :], turns[:, :], -part, src[:, :], ALU.mult, ALU.add))
                    src = dst
                p.wait("dve", made)
                made = p.dve(nc.vector.tensor_scalar(dst[:, :], dst[:, :], quarter * TWO_PI, 3.1415925, ALU.add, ALU.min))
                p.wait("dve", made)
                angles = made = p.dve(nc.vector.tensor_scalar(dst[:, :], dst[:, :], -3.1415925, None, ALU.max))
                p.wait("act", made)
                tables = p.act(nc.scalar.activation(dst[:, :], dst[:, :], ACT.Sin))
            rotated, roped = [], None
            for j in range(QT + 1):
                x = z[:, 12 + j, :] if j < QT else zk[:, 0, :]
                bank = 4 + j % 2
                p.wait("pe", loaded, z_done, rotated[j - 2] if j > 1 else self.h_done)
                got = p.pe(nc.tensor.matmul(self.ps[:, bank, :], rot[:, 0, :], x, start=True, stop=True))
                p.wait("dve", got, tables, roped)
                made = p.dve(nc.vector.tensor_tensor(turns[:, :], self.ps[:, bank, :], sin[:, :], ALU.mult))
                rotated.append(made)
                made2 = p.dve(nc.vector.tensor_tensor(x, x, cos[:, :], ALU.mult))
                p.wait("dve", made2, made)
                roped = p.dve(nc.vector.tensor_tensor(x, x, turns[:, :], ALU.add))
            for g in range(2):
                p.wait("pe", roped, *rotated)
                got = p.pe(nc.tensor.matmul(self.ps[:, 4 + g, :], rot[:, 1 + g, :], zk[:, 0, :], start=True, stop=True))
                p.wait("act", got)
                keys = p.act(nc.scalar.activation(kk[:, g, :], self.ps[:, 4 + g, :], ACT.Copy))
            free = keys
            order = HEAD_ORDER
            for n in range(NB):
                k0 = max(n - 1, 0) * P
                nk = (n + 1) * P - k0
                m0 = 2 * P - nk
                p.wait("pe", roped, free)
                for i, h in enumerate(order):
                    rows = slice((h % 2) * 64, (h % 2) * 64 + 64)
                    last = nc.tensor.matmul(self.ps[:, 4 + i // 2, (i % 2) * 256:(i % 2) * 256 + nk],
                                            z[rows, 12 + h // 2, n * P:(n + 1) * P], kk[rows, h // 4, k0:k0 + nk],
                                            start=True, stop=True)
                scored = p.pe(last)
                got = self.ps[:, 4:8, :].rearrange("p b (i k) -> p (b i) k", k=256)[:, :, 0:nk]
                sn = s[:, :, 0:nk]
                p.wait("dve", scored, free)
                made = p.dve(nc.vector.scalar_tensor_tensor(sn, got, 64 ** -0.5,
                             mask[:, m0:2 * P].unsqueeze(1).to_broadcast([P, NQ, nk]), ALU.mult, ALU.add))
                p.wait("dve", made)
                made = p.dve(nc.vector.tensor_reduce(m[:, :], sn, AX.X, ALU.max))
                p.wait("dve", made)
                made = p.dve(nc.vector.tensor_tensor(m[:, :], m[:, :], self.col("sinks", 0, NQ), ALU.max))
                p.wait("dve", made)
                p.dve(nc.vector.tensor_tensor(es[:, :], self.col("sinks", 0, NQ), m[:, :], ALU.subtract))
                made = p.dve(nc.vector.tensor_tensor(sn, sn, m[:, :].unsqueeze(2).to_broadcast([P, NQ, nk]), ALU.subtract))
                p.wait("act", made)
                p.act(nc.scalar.activation(es[:, :], es[:, :], ACT.Exp))
                made = p.act(nc.scalar.activation(sn, sn, ACT.Exp))
                p.wait("dve", made)
                made = p.dve(nc.vector.tensor_reduce(rs[:, :], sn, AX.X, ALU.add))
                p.wait("dve", made)
                made = p.dve(nc.vector.tensor_tensor(rs[:, :], rs[:, :], es[:, :], ALU.add))
                p.wait("dve", made)
                made = p.dve(nc.vector.reciprocal(rs[:, :], rs[:, :]))
                p.wait("dve", made)
                probs = p.dve(nc.vector.tensor_tensor(sn, sn, rs[:, :].unsqueeze(2).to_broadcast([P, NQ, nk]), ALU.mult))
                nkb = nk // P
                p.wait("pe", probs)
                for i in range(NQ):
                    for j in range(nkb):
                        u = i * nkb + j
                        last = nc.tensor.matmul(self.ps[:, 4 + u // 4, (u % 4) * P:(u % 4 + 1) * P], sn[:, i, j * P:(j + 1) * P],
                                                self.ident[:, :], is_transpose=True, start=True, stop=True)
                turned = p.pe(last)
                nu = NQ * nkb
                p.wait("act", turned)
                moved = p.act(nc.scalar.activation(pt[:, 0:nu, :],
                              self.ps[:, 4:4 + nu // 4, :].rearrange("p b (i t) -> p (b i) t", t=P), ACT.Copy))
                p.wait("pe", moved)
                for i, h in enumerate(order):
                    rows = slice((h % 2) * 64, (h % 2) * 64 + 64)
                    for j in range(nkb):
                        last = nc.tensor.matmul(self.ps[rows, 4, (h // 2) * P:(h // 2 + 1) * P],
                                                v[:, k0 // P + j, (h // 4) * 64:(h // 4) * 64 + 64], pt[:, i * nkb + j, :],
                                                start=j == 0, stop=j == nkb - 1)
                mixed = p.pe(last)
                p.wait("act", mixed)
                free = p.act(nc.scalar.activation(o[:, :, n * P:(n + 1) * P],
                                                  self.ps[:, 4, :].rearrange("p (i t) -> p i t", t=P), ACT.Copy))
            for f in range(QT):
                self.h_done = self.split(4 + f, CTX, LAT, o[:, f, :], free)
            self.att_free = [self.h_done, self.h_done]

    def pool_mixer(self, layer, which):
        p, nc, ins = self.p, self.nc, self.ins
        with ExitStack() as ctx:
            sb = lambda name, shape, dt=F32: ctx.enter_context(nc.sbuf_tensor(name, shape, dt))
            h, recip = sb("pool_h", [P, KD, LAT]), sb("pool_recip", [P, 4, LAT])
            gate, wins = sb("pool_gate", [P, KD]), [sb(f"pool_win{i}", [P, LAT]) for i in range(4)]
            loaded = self.load(recip[:, :, :], ins["recip"], self.x_done)
            wins_free = [None, None]
            self.layer_norm(which, layer, 0, plain=h)
            p.wait("dve", self.mods_made)
            gated = p.dve(nc.vector.tensor_tensor(gate[:, :], self.mods1[:, layer, 2 * KD:3 * KD], self.col("pool_scale", 0, KD), ALU.mult))
            p.wait("dve", loaded, gated)
            self.sums = Sums(self, LAT, False)
            for f in range(KD):
                p.wait("dve", self.h_plain[f])
                src = h[:, f, :]
                made = wins_free[f % 2]
                for d in range(f // 2 + 1):
                    w = 1 << d
                    dst = wins[d % 2 + 2 * (f % 2)][:, :]
                    p.wait("dve", made)
                    p.dve(nc.vector.tensor_tensor(dst[:, w:], src[:, w:], src[:, 0:LAT - w], ALU.add))
                    made = p.dve(nc.vector.tensor_copy(dst[:, 0:w], src[:, 0:w]))
                    src = dst
                p.wait("dve", made)
                made = p.dve(nc.vector.tensor_tensor(src, src, recip[:, f // 2, :], ALU.mult))
                p.wait("dve", made)
                made = p.dve(nc.vector.tensor_tensor(src, src, h[:, f, :], ALU.subtract))
                self.h_done = wins_free[f % 2] = self.split(f, CTX, LAT, src, made)
            for g in range(4):
                at = slice(2 * g, 2 * g + 2)
                Stream(self, "pool", 2 * g, 2, self.h_hi[:, at, :], self.h_lo[:, at, :], LAT, self.h_ready[at]).run(
                              self.shifted(self.residual(0, layer, 2, LAT, gate=lambda n: gate[:, n:n + 1]), 2 * g))

    def shifted(self, consume, by):
        return lambda n, s, ps, product: consume(n + by, s, ps, product)

    def even_mixer2(self):
        p, nc, ins = self.p, self.nc, self.ins
        T = TALL
        with ExitStack() as ctx:
            sb = lambda name, shape, dt=F32: ctx.enter_context(nc.sbuf_tensor(name, shape, dt))
            v = sb("v2", [P, T // P, 4 * P])
            z = sb("z2", [P, 9, T])
            with ExitStack() as inner:
                more = inner.enter_context(nc.sbuf_tensor("z2more", [P, 8, T], F32))
                self.z_free = self.h_done
                self.straight("in2", 0, 9, T, self.keep(z, T), act=4)
                self.straight("in2", 9, 8, T, self.keep(more, T), act=4)
                z_done = self.z_done
                for f in range(4):
                    units = [(slice(0, P), slice(t * P, (t + 1) * P)) for t in range(T // P)]
                    self.transposes(v[:, :, f * P:(f + 1) * P], more[:, f, :], units, z_done)
                self.z_free = self.evicted
                self.fourier(inner, more, z_done)
            self.gla(z, v)
            self.sums = Sums(self, T, True)
            self.straight("out2", 0, KD, T, self.residual(1, 0, 2, T), dve=4)

    def fourier(self, ctx, more, z_done):
        p, nc, ins = self.p, self.nc, self.ins
        sb = lambda name, shape, dt=F32: ctx.enter_context(nc.sbuf_tensor(name, shape, dt))
        feat = sb("dft_f", [P, 2 * P])
        lat, con = sb("dft_lat", [P, 2, LAT // P, LAT]), sb("dft_ctx", [P, 2, CTX // P, CTX])
        a = more[:, 0:2, :].rearrange("p k t -> p (k t)").rearrange("p (t c) -> p t c", c=2 * P)
        f, u = more[:, 2, :], more[:, 4:8, :]
        self.load(feat[:, :], ins["dft_f"], self.z_free)
        self.load(lat[:, :, :, :], ins["dft_lat"])
        loaded = self.load(con[:, :, :, :], ins["dft_ctx"])
        done = None
        for g in range(4):
            p.wait("pe", loaded, z_done, done, self.att_free[0], self.att_free[1])
            for t in range(TALL // P):
                last = nc.tensor.matmul(self.ps[:, 4 + t // 2, (t % 2) * 256:(t % 2) * 256 + 256],
                                        u[:, g, t * P:(t + 1) * P], feat[:, :], start=True, stop=True)
            got = p.pe(last)
            p.wait("act", got, done)
            rows = p.act(nc.scalar.activation(a, self.ps[:, 4:7, :].rearrange("p b (i c) -> p (b i) c", c=2 * P), ACT.Copy))
            p.wait("pe", rows)
            for t0, tn, bank in segments(TALL):
                basis = con if bank == 0 else lat
                nt = tn // P
                for part in range(2):
                    for t in range(nt):
                        last = nc.tensor.matmul(self.ps[:, 4 + bank, 0:tn], a[:, t0 // P + t, part * P:(part + 1) * P],
                                                basis[:, part, t, :], start=part == 0 and t == 0,
                                                stop=part == 1 and t == nt - 1)
            got = p.pe(last)
            p.wait("act", got, done)
            p.act(nc.scalar.activation(f[:, 0:CTX], self.ps[:, 4, 0:CTX], ACT.Copy))
            made = p.act(nc.scalar.activation(f[:, CTX:TALL], self.ps[:, 5, 0:LAT], ACT.Copy))
            done = self.split(g, 0, TALL, f, made)
        self.h_done = done
        self.att_free = [done, done]

    def gla(self, z, v):
        p, nc, ins = self.p, self.nc, self.ins
        T, H, NC = TALL, 4, TALL // CHUNK
        W = 2 * T
        with ExitStack() as ctx:
            sb = lambda name, shape, dt=F32: ctx.enter_context(nc.sbuf_tensor(name, shape, dt))
            flat = lambda i, n: z[:, i:i + n, :].rearrange("p h t -> p (h t)")
            q, k = flat(0, 2), flat(2, 2)
            b = [sb(f"gb{d}", [P, W]) for d in range(2)]
            comb = sb("gcomb", [P, W])
            att = sb("gatt", [P, H * NC, P])
            kd_t = [sb(f"gkdt{d}", [P, 2 * NC, P]) for d in range(2)]
            masks = sb("gmasks", [P, 2 * LEVELS + 1, P], U8)
            reset = sb("greset", [P, T])
            wg = self.tmp[0][0:16, :].rearrange("p (f c) -> p f c", c=P)
            ends = sb("gends", [P, 2, 2 * NC])
            loga = comb
            start = self.h_done
            self.load(wg, ins["w_gate"], start)
            self.load(reset[:, :], ins["reset2"])
            loaded, zeroed = self.load_masks(masks, "masks2", att, start)
            p.wait("dve", start)
            made = p.dve(nc.vector.tensor_scalar(q, q, 0.125, None, ALU.mult))
            free = made
            sums = []
            for d in range(2):
                p.wait("pe", loaded, free, self.h_done)
                for f in range(2):
                    for t0, tn, bank in segments(T):
                        last = nc.tensor.matmul(self.ps[:, 4 + 2 * f + bank, 0:tn], wg[:, 2 * d + f, :],
                                                z[0:16, 8, t0:t0 + tn], start=True, stop=True)
                got = p.pe(last)
                p.wait("act", got, free)
                for f in range(2):
                    for t0, tn, bank in segments(T):
                        x = p.act(nc.scalar.activation(loga[:, f * T + t0:f * T + t0 + tn], self.ps[:, 4 + 2 * f + bank, 0:tn],
                                                       ACT.Identity, bias=self.col("bgate", 2 * d + f)))
                e = b[d][:, :]
                p.wait("dve", x)
                made = p.dve(nc.vector.scalar_tensor_tensor(e, loga[:, :], -1.0, loga[:, :], ALU.mult, ALU.min))
                p.wait("act", made)
                made = p.act(nc.scalar.activation(e, e, ACT.Exp))
                p.wait("act", made)
                made2 = p.act(nc.scalar.activation(e, e, ACT.Ln, bias=1.0))
                p.wait("dve", made2)
                made = p.dve(nc.vector.tensor_scalar(loga[:, :], loga[:, :], 0.0, None, ALU.min))
                p.wait("dve", made)
                made = p.dve(nc.vector.tensor_tensor(loga[:, :], loga[:, :], e, ALU.subtract))
                p.wait("dve", made)
                made = p.dve(nc.vector.tensor_scalar(loga[:, :], loga[:, :], 1.0 / 16.0, None, ALU.mult))
                p.wait("dve", made, loaded)
                for f in range(2):
                    at = slice(f * T, (f + 1) * T)
                    free = p.dve(nc.vector.tensor_tensor_scan(e[:, at], reset[:, :], loga[:, at], 0.0, ALU.mult, ALU.add))
                if d == 1:
                    p.wait("dve", free)
                    n3 = lambda a: a.rearrange("p (n c) -> p n c", c=CHUNK)
                    free = p.dve(nc.vector.tensor_tensor(e, e, loga[:, :], ALU.subtract))
                    total = ends[:, 1, :].unsqueeze(2)
                    p.wait("dve", free)
                    free = p.dve(nc.vector.tensor_tensor(total, n3(e)[:, :, CHUNK - 1:CHUNK], n3(loga[:, :])[:, :, CHUNK - 1:CHUNK], ALU.add))
                sums.append(free)
            units = [(slice((h % 2) * 64, (h % 2) * 64 + 64), slice((h // 2) * T + c * CHUNK, (h // 2) * T + (c + 1) * CHUNK))
                     for h in (0, 2, 1, 3) for c in range(NC)]
            p.wait("dve", sums[1])
            made = p.dve(nc.vector.tensor_scalar(comb[:, :], k, 2.0, None, ALU.mult))
            p.wait("dve", zeroed)
            read = self.products_to(att, [(comb, q)], units, made, masks[:, 2 * LEVELS, :])
            for d in range(2):
                read = self.decayed_products(LEVELS, att, masks, q, k, b[d][:, :], comb[:, :], W, units, read, d == 1, d * LEVELS)
            v3 = lambda a: a.rearrange("p (n c) -> p n c", c=CHUNK)
            full = [(slice(0, P), slice(f * T + c * CHUNK, f * T + (c + 1) * CHUNK)) for f in range(2) for c in range(NC)]
            e0, e1 = b[0][:, :], b[1][:, :]
            p.wait("dve", read, self.att_done)
            kept = p.dve(nc.vector.tensor_copy(ends[:, 0, :].unsqueeze(2), v3(e0)[:, :, CHUNK - 1:CHUNK]))
            p.wait("dve", kept)
            made = p.dve(nc.vector.tensor_tensor(v3(comb[:, :]), ends[:, 0, :].unsqueeze(2).to_broadcast([P, 2 * NC, CHUNK]), v3(e0), ALU.subtract))
            p.wait("act", made)
            made = p.act(nc.scalar.activation(comb[:, :], comb[:, :], ACT.Exp))
            p.wait("dve", made)
            made = p.dve(nc.vector.tensor_tensor(comb[:, :], comb[:, :], k, ALU.mult))
            read = self.transposes(kd_t[0], comb, full, made)
            p.wait("act", read)
            made = p.act(nc.scalar.activation(comb[:, :], e1, ACT.Exp))
            p.wait("dve", made)
            made = p.dve(nc.vector.tensor_tensor(comb[:, :], comb[:, :], k, ALU.mult))
            read = self.transposes(kd_t[1], comb, full, made)
            p.wait("act", kept)
            f_done = p.act(nc.scalar.activation(e0, e0, ACT.Exp))
            p.wait("dve", made, f_done)
            p.dve(nc.vector.tensor_tensor(e0, e0, q, ALU.mult))
            made = p.dve(nc.vector.tensor_tensor(v3(e1), ends[:, 1, :].unsqueeze(2).to_broadcast([P, 2 * NC, CHUNK]), v3(e1), ALU.subtract))
            p.wait("act", made)
            made = p.act(nc.scalar.activation(e1, e1, ACT.Exp))
            ends_e = p.act(nc.scalar.activation(ends[:, :, :], ends[:, :, :], ACT.Exp))
            p.wait("dve", made)
            q_done = p.dve(nc.vector.tensor_tensor(e1, e1, q, ALU.mult))
            state = flat(0, 4).rearrange("p (d n v) -> p d n v", d=2, v=P)
            lat0 = CTX // CHUNK
            orders = [list(range(NC)), list(range(lat0 - 1, -1, -1)) + list(range(NC - 1, lat0 - 1, -1))]
            p.wait("pool", q_done)
            for d in range(2):
                for f in range(2):
                    init = p.pool(nc.gpsimd.memset(state[:, d, f * NC + orders[d][0], :], 0.0))
            p.wait("dve", ends_e, init)
            stepped = [self.evicted, self.evicted]
            for n in range(NC - 1):
                for d in range(2):
                    c, nxt = orders[d][n], orders[d][n + 1]
                    bank = 4 + 2 * d + n % 2
                    p.wait("pe", *stepped, self.att_free[0], self.att_free[1])
                    for h in range(H):
                        rows = slice((h % 2) * 64, (h % 2) * 64 + 64)
                        last = nc.tensor.matmul(self.ps[rows, bank, (h // 2) * P:(h // 2 + 1) * P],
                                                kd_t[d][:, (h // 2) * NC + c, rows], v[:, c, h * P:(h + 1) * P], start=True, stop=True)
                    got = p.pe(last)
                    p.wait("dve", got, stepped[d])
                    for f in range(2):
                        stepped[d] = p.dve(nc.vector.scalar_tensor_tensor(
                            state[:, d, f * NC + nxt, :], state[:, d, f * NC + c, :], ends[:, d, f * NC + c:f * NC + c + 1],
                            self.ps[:, bank, f * P:(f + 1) * P], ALU.mult, ALU.add))
            p.wait("pe", self.att_done, q_done, *stepped)
            free_o = [None, None]
            o = comb
            for h in range(H):
                rows = slice((h % 2) * 64, (h % 2) * 64 + 64)
                b0 = 4 + 2 * (h % 2)
                p.wait("pe", free_o[h % 2])
                for t0, tn, bank in segments(T):
                    for c in range(t0 // P, (t0 + tn) // P):
                        out = self.ps[:, b0 + bank, c * P - t0:(c + 1) * P - t0]
                        nc.tensor.matmul(out, v[:, c, h * P:(h + 1) * P], att[:, ((h % 2) * 2 + h // 2) * NC + c, :], start=True, stop=False)
                        cols = slice((h // 2) * T + c * CHUNK, (h // 2) * T + (c + 1) * CHUNK)
                        nc.tensor.matmul(out, state[rows, 0, (h // 2) * NC + c, :], e0[rows, cols], start=False, stop=False)
                        last = nc.tensor.matmul(out, state[rows, 1, (h // 2) * NC + c, :], e1[rows, cols], start=False, stop=True)
                got = p.pe(last)
                for t0, tn, bank in segments(T):
                    at = o[:, (h % 2) * T + t0:(h % 2) * T + t0 + tn]
                    p.wait("act", got, read, self.h_done)
                    copied = p.act(nc.scalar.activation(at, self.ps[:, b0 + bank, 0:tn], ACT.Copy))
                    rstd = self.head_norm(at, b0 + bank, P, EPS, copied, tn)
                    p.wait("dve", rstd)
                    made = p.dve(nc.vector.scalar_tensor_tensor(at, at, self.col("ggla", h), self.rstd[:, 0:tn], ALU.mult, ALU.mult))
                    self.rstd_free = made
                    gate = z[:, 4 + h, t0:t0 + tn]
                    p.wait("act", made)
                    silu = p.act(nc.scalar.activation(gate, gate, ACT.Silu))
                    p.wait("dve", silu)
                    made = p.dve(nc.vector.tensor_tensor(at, at, gate, ALU.mult))
                    self.h_done = self.split(4 + h, t0, tn, at, made)
                free_o[h % 2] = self.h_done
            self.att_free = [self.h_done, self.h_done]

    def attention(self):
        p, nc, ins = self.p, self.nc, self.ins
        T, NH, NKV, NT = TALL, 8, 2, LAT // P
        NS = T // P
        with ExitStack() as ctx:
            sb = lambda name, shape, dt=F32: ctx.enter_context(nc.sbuf_tensor(name, shape, dt))
            q, k = sb("aq", [P, NH, LAT]), sb("ak", [P, NKV, T])
            v = sb("av", [P, NS, NKV * P])
            cos, sin, rot = sb("acos", [P, LAT]), sb("asin", [P, LAT]), sb("arot", [P, P])
            s, pt = sb("ascores", [P, 2, NT, T]), sb("aprobs", [P, NS, LAT])
            nm, rs = sb("anm", [P, 2 * NT]), sb("ars", [P, 2 * NT])
            turned = sb("aturn", [P, LAT])
            o = sb("ao", [P, 2, LAT])
            self.z_free = self.h_done
            self.load(cos[:, :], ins["cos2"], self.h_done)
            self.load(sin[:, :], ins["sin2"])
            loaded = self.load(rot[:, :], ins["rot2"])
            self.straight("qkv", 0, 8, LAT, self.keep(q, LAT), act=2)
            self.straight("qkv", 8, 2, T, self.keep(k, T), act=4)
            vf = s[:, 0, 0:2, :]
            self.straight("qkv", 10, 2, T, self.keep(vf, T))
            z_done = self.z_done
            for f in range(2):
                units = [(slice(0, P), slice(t * P, (t + 1) * P)) for t in range(NS)]
                self.transposes(v[:, :, f * P:(f + 1) * P], vf[:, f, :], units, z_done)
            z_done = self.evicted
            h_read = self.free_hl[1 - self.tile % 2]
            roped = None
            for j in range(NKV + NH):
                x, gain = (k[:, j, :], self.col("gk")) if j < NKV else (q[:, j - NKV, :], self.col("gq"))
                parts = [(t0, tn) for t0, tn, _ in segments(T)] if j < NKV else [(0, LAT)]
                for t0, tn in parts:
                    xs = x[:, t0:t0 + tn]
                    rstd = self.head_norm(xs, 4 + j % 2, P, EPS, z_done, tn)
                    p.wait("dve", rstd)
                    normed = p.dve(nc.vector.scalar_tensor_tensor(xs, xs, gain, self.rstd[:, 0:tn], ALU.mult, ALU.mult))
                    self.rstd_free = normed
                    ready = normed
                    if tn == LAT:
                        p.wait("pe", normed, loaded, rs_free if j else None)
                        got = p.pe(nc.tensor.matmul(self.ps[:, 6, :], rot[:, :], xs, start=True, stop=True))
                        p.wait("dve", got, loaded, roped)
                        made = rs_free = p.dve(nc.vector.tensor_tensor(turned[:, :], self.ps[:, 6, :], sin[:, :], ALU.mult))
                        made2 = p.dve(nc.vector.tensor_tensor(xs, xs, cos[:, :], ALU.mult))
                        p.wait("dve", made, made2)
                        ready = roped = p.dve(nc.vector.tensor_tensor(xs, xs, turned[:, :], ALU.add))
            free_s, free_pt = [None, None], None
            free_bank = [ready, ready]
            free_t = [ready, ready]
            for h in range(NH):
                sl = h % 2
                for t in range(NT):
                    bank = 2 * (t % 2)
                    p.wait("pe", ready, free_bank[t % 2], *self.free_ps[t % 2])
                    for i in range(2):
                        last = nc.tensor.matmul(self.ps[:, bank + i, 0:T // 2], q[:, h, t * P:(t + 1) * P],
                                                k[:, h // 4, i * (T // 2):(i + 1) * (T // 2)], start=True, stop=True)
                    scored = p.pe(last)
                    got = self.ps[:, bank:bank + 2, 0:T // 2]
                    sc = s[:, sl, t, :]
                    at = slice(sl * NT + t, sl * NT + t + 1)
                    p.wait("dve", scored, free_s[sl])
                    made = p.dve(nc.vector.tensor_reduce(nm[:, at], got, AX.XY, ALU.max))
                    p.wait("dve", made)
                    made = p.dve(nc.vector.tensor_scalar(nm[:, at], nm[:, at], -(P ** -0.5), None, ALU.mult))
                    p.wait("act", made)
                    made = free_bank[t % 2] = p.act(nc.scalar.activation(sc.rearrange("p (i k) -> p i k", i=2), got, ACT.Exp,
                                                    scale=P ** -0.5, bias=nm[:, at], accum_out=rs[:, at]))
                    p.wait("dve", made)
                    made = p.dve(nc.vector.reciprocal(rs[:, at], rs[:, at]))
                    p.wait("dve", made)
                    probs = p.dve(nc.vector.tensor_scalar(sc, sc, rs[:, at], None, ALU.mult))
                for j in range(NS):
                    p.wait("pe", probs, free_t[j % 2])
                    for t in range(NT):
                        last = nc.tensor.matmul(self.ps[:, 4 + j % 2, t * P:(t + 1) * P], s[:, sl, t, j * P:(j + 1) * P],
                                                self.ident[:, :], is_transpose=True, start=True, stop=True)
                    got = p.pe(last)
                    if j % 2:
                        p.wait("dve", got, free_pt)
                        free_t[1] = p.dve(nc.vector.tensor_copy(pt[:, j, :], self.ps[:, 5, :]))
                    else:
                        p.wait("act", got, free_pt)
                        free_t[0] = p.act(nc.scalar.activation(pt[:, j, :], self.ps[:, 4, :], ACT.Copy))
                free_s[sl] = got
                p.wait("pe", free_t[0], free_t[1], free_o[sl] if h > 1 else None)
                for j in range(NS):
                    last = nc.tensor.matmul(self.ps[:, 6 + sl, :], v[:, j, (h // 4) * P:(h // 4 + 1) * P], pt[:, j, :],
                                            start=j == 0, stop=j == NS - 1)
                mixed = free_pt = p.pe(last)
                p.wait("act", mixed, free_o[sl] if h > 1 else None, h_read)
                if h == 0:
                    free_o = [None, None]
                copied = p.act(nc.scalar.activation(o[:, sl, :], self.ps[:, 6 + sl, :], ACT.Copy))
                free_o[sl] = self.h_done = self.split(h, CTX, LAT, o[:, sl, :], copied)
            self.att_free = [self.h_done, self.h_done]
            self.free_ps = [[self.h_done], [self.h_done]]
            self.sums = Sums(self, LAT, True)
            self.straight("attout", 0, KD, LAT, self.residual(1, 1, 2, LAT), dve=2)

    def final_norm(self):
        p, nc = self.p, self.nc
        self.add_sums()
        rstd = self.reciprocal_root(self.rstd[:, LATS], self.ps[:, 6, 0:LAT], D, EPS, self.sums.done)
        p.wait("dve", rstd)
        for f in range(KD):
            x = self.x[:, f, LATS]
            made = p.dve(nc.vector.scalar_tensor_tensor(x, x, self.col("gfin", f), self.rstd[:, LATS], ALU.mult, ALU.mult))
            p.wait("sp", made)
            stored = p.done("store", nc.sync.dma_start(self.out[:, f, :], x), 16)
        p.wait("sp", stored)


def build(nc, ins, out):
    with ExitStack() as ctx:
        k = Stages(nc, ctx, ins, out)
        k.att_free, k.z_free = [None, None], None
        k.constants()
        k.condition_start()
        k.first_tiles()
        k.x_tile = [k.consts] * KD
        k.x_done = k.consts
        k.modulate_first()
        k.even_mixer1()
        k.layer_norm(0, 0, 3)
        half = JOBS // 2
        k.ffn(0, 0, LAT, Sums(k, LAT, False), [
            lambda space: Modulations(space, 0, 1, 0, half + 1, [0]),
            lambda space: Modulations(space, 1, 0, 0, KD, [1, 2]),
            lambda space: Modulations(space, 0, 1, half - 1, half + 1, [0]),
            lambda space: Modulations(space, 1, 0, KD, KD, [1, 2]),
            lambda: k.columns_of(0, 1, [0], 0, NMOD)])
        k.pool_mixer(1, 1)
        k.layer_norm(2, 1, 3)
        k.ffn(0, 1, LAT, Sums(k, LAT, False), [
            lambda space: Modulations(space, 1, 1, 0, half + 1, [1, 2]),
            lambda space: Modulations(space, 1, 0, 2 * KD, KD, [1, 2]),
            lambda space: Modulations(space, 1, 1, half - 1, half + 1, [2]),
            lambda space: Modulations(space, 1, 0, 3 * KD, KD, [1, 2]),
            lambda: (k.columns_of(1, 0, [1, 2], 0, NMOD), k.columns_of(1, 1, [1, 2], 0, 2 * KD),
                     k.columns_of(1, 1, [2], 2 * KD, NMOD))])
        k.layer_norm(3)
        k.sums = Sums(k, TALL, True)
        for f in range(KD):
            k.sums.add(f, k.x_tile[f])
        k.rms_modulate(0, 0, "gmix", TALL)
        k.even_mixer2()
        k.rms_modulate(0, 3, "gffn", TALL)
        k.ffn(1, 0, TALL, Sums(k, TALL, True))
        k.rms_modulate(1, 0, "gmix", TALL)
        k.attention()
        k.rms_modulate(1, 3, "gffn", LAT)
        k.ffn(1, 1, LAT, Sums(k, LAT, True))
        k.final_norm()


def shape_constants():
    c = {"ident": np.eye(P, dtype=np.float32)}
    s, t = np.meshgrid(np.arange(P), np.arange(P), indexing="ij")

    def level_masks(first, second):
        return [((s >> (l + 1)) == (t >> (l + 1))) & (((s >> l) & 1) == first) & (((t >> l) & 1) == second)
                for l in range(LEVELS)]

    fwd, bwd = level_masks(0, 1), level_masks(1, 0)
    pack = lambda ms: np.ascontiguousarray(np.stack(ms, 1).astype(np.int32))
    c["masks1"], c["masks2"] = pack(fwd + [s == t]), pack(fwd + bwd + [s == t])
    for name, n in (("reset1", LAT), ("reset2", TALL)):
        c[name] = np.ascontiguousarray(np.broadcast_to((np.arange(n) % CHUNK != 0).astype(np.float32), (P, n)))
    rel = np.arange(P)[:, None] + P - np.arange(2 * P)[None, :]
    c["wmask"] = np.where((rel >= 0) & (rel < P), 0.0, NEG).astype(np.float32)
    rot1 = np.zeros((P, 3, P), np.float32)
    for head in (0, 64):
        for i in range(8):
            rot1[head + 8 + i, 0, head + i] = -1.0
            rot1[head + i, 0, head + 8 + i] = 1.0
    for g in range(2):
        for i in range(64):
            rot1[g * 64 + i, 1 + g, i] = rot1[g * 64 + i, 1 + g, 64 + i] = 1.0
    c["rot1"] = rot1
    rot2 = np.zeros((P, P), np.float32)
    for i in range(64):
        rot2[64 + i, i], rot2[i, 64 + i] = -1.0, 1.0
    c["rot2"] = rot2
    recip = np.stack([1.0 / np.minimum(np.arange(LAT) + 1, w) for w in (2, 4, 8, 16)])
    c["recip"] = np.ascontiguousarray(np.broadcast_to(recip.astype(np.float32), (P, 4, LAT)))
    def dft(n):
        a = 2.0 * np.pi * (np.outer(np.arange(n), np.arange(n)) % n) / n
        return np.cos(a), np.sin(a)
    c["dft_f"] = np.concatenate(dft(P), 1).astype(np.float32)
    for name, n in (("dft_lat", LAT), ("dft_ctx", CTX)):
        cn, sn = dft(n)
        m = np.stack([cn, -sn]) / np.sqrt(n * P)
        c[name] = np.ascontiguousarray(m.reshape(2, n // P, P, n).transpose(2, 0, 1, 3).astype(np.float32))
    inv = (10000.0 ** (-np.arange(0, 64, 2, dtype=np.float32) / 64)).astype(np.float32)
    r, col = np.meshgrid(np.arange(LAT // 64), np.arange(64), indexing="ij")
    ang = np.concatenate([r.reshape(-1, 1).astype(np.float32) * inv, col.reshape(-1, 1).astype(np.float32) * inv], -1)
    for name, fn in (("cos2", np.cos), ("sin2", np.sin)):
        c[name] = np.ascontiguousarray(np.concatenate([fn(ang), fn(ang)], 1).T.astype(np.float32))
    inv1 = (500000.0 ** (-np.arange(0, 16, 2, dtype=np.float32) / 16)).astype(np.float32)
    per = np.zeros(64, np.float32)
    per[0:8] = per[8:16] = inv1
    c["inv_freq"] = np.concatenate([per, per]).reshape(P, 1)
    return c


def tiles(w, pad=None):
    rows, cols = w.shape
    return w.reshape(rows // P, P, cols // P, P).transpose(2, 1, 0, 3).reshape(cols // P, P, (rows // P) * P)


def columns(a):
    return np.moveaxis(a.reshape(*a.shape[:-1], a.shape[-1] // P, P), -1, 0).reshape(P, -1)


def layout(inputs):
    g = {n: np.asarray(a) for n, a in inputs.items()}
    c = shape_constants()
    a = {n: v for n, v in c.items() if n != "inv_freq"}
    a["x"] = g["x"][0].T.reshape(KD, P, LAT).transpose(1, 0, 2)
    a["ctx"] = g["ctx_2"][0].T.reshape(KD, P, CTX).transpose(1, 0, 2)
    a["positions"] = g["positions"].reshape(1, LAT)
    parts = {
        "c1": columns(g["c"][0]), "c2": columns(g["c_2"][0]), "cc2": columns(g["c_ctx_2"]),
        "ada_b": columns(g["ada_b"]), "mod_b": columns(g["b_mod_2"]), "ln_g": columns(g["ln_g"]), "ln_b": columns(g["ln_b"]),
        "lb_raw": columns(g["hgrn_lb_raw"]), "norm_g": columns(g["hgrn_norm_g"]), "pool_scale": columns(g["pool_scale"]),
        "fcw": columns(g["ffn_conv_w"]), "fcb": columns(g["ffn_conv_b"]), "gmix": columns(g["g_norm_mix_2"]),
        "gffn": columns(g["g_norm_ffn_2"]), "gfin": columns(g["g_norm_final_2"]), "bgate": columns(g["b_gla_gate_2"]),
        "ggla": columns(g["g_gla_out_2"]), "gq": columns(g["g_q_2"]), "gk": columns(g["g_k_2"]),
        "cw2": columns(g["w_ffn_conv_2"].reshape(2, 3, 2, F_FF).transpose(0, 2, 1, 3)),
        "cb2": columns(g["b_ffn_conv_2"]), "inv_freq": c["inv_freq"],
        "eps5": np.full((P, 1), LN_EPS, np.float32), "eps6": np.full((P, 1), EPS, np.float32),
        "sinks": np.broadcast_to(g["attn_sinks"][:, HEAD_ORDER], (P, 8)),
    }
    a["small"] = np.concatenate([parts[n] for n in SMALL], 1)
    for name, w in (("ada_w", g["ada_w"]), ("w_mod", g["w_mod_2"])):
        t = w.reshape(2, KD, P, JOBS, JW).transpose(0, 3, 2, 1, 4).reshape(2 * JOBS, P, KD * JW)
        a[name] = np.concatenate([t, np.zeros((2, P, KD * JW), np.float32)])
    w = g["ab_w_in"][0]
    a["in1"] = tiles(np.concatenate([w[:, 0:1024], w[:, 1536:2048], w[:, 2048:2816], w[:, 1024:1536]], 1))
    a["out1"] = tiles(g["ab_w_out"][0])
    a["pool"] = np.concatenate([tiles(g["pool_w"][0, i]) for i in range(4)])
    for name, up, down in (("0", g["ffn_w_up"], g["ffn_w_down"]), ("1", g["w_ffn_up_2"], g["w_ffn_down_2"])):
        for layer in range(2):
            t = tiles(up[layer])
            a[f"up{name}{layer}"] = t.reshape(2, FT, P, D).transpose(1, 0, 2, 3).reshape(2 * FT, P, D)
            a[f"down{name}{layer}"] = np.concatenate([tiles(down[layer][h * FG * P:(h + 1) * FG * P]) for h in range(2)])
    w = g["w_even_in_2"][0]
    low = np.concatenate([w[:, 2048:2064], np.zeros((D, P - 16), np.float32)], 1)
    a["in2"] = tiles(np.concatenate([w[:, 512:1024], w[:, 1536:2048], low, w[:, 1024:1536], w[:, 0:512]], 1))
    a["out2"] = tiles(g["w_even_out_2"][0])
    a["w_gate"] = g["w_gla_gate_2"][0].transpose(1, 0, 2).reshape(16, 4, P)
    a["qkv"] = tiles(g["w_qkv_2"][0])
    a["attout"] = tiles(g["w_att_out_2"][0])
    return {n: np.ascontiguousarray(v) for n, v in a.items()}


def kernel(**inputs):
    import concourse.bacc as bacc
    from concourse.bass_utils import run_bass_kernel_spmd

    nc = bacc.Bacc("TRN2", target_bir_lowering=False, num_devices=1)
    arrays = layout(inputs)
    ins = {n: nc.dram_tensor(f"in_{n}", v.shape, mybir.dt.from_np(v.dtype), kind="ExternalInput").ap()
           for n, v in arrays.items()}
    out = nc.dram_tensor("out_y", (P, KD, LAT), F32, kind="ExternalOutput").ap()
    build(nc, ins, out)
    r = run_bass_kernel_spmd(nc, [{f"in_{n}": v for n, v in arrays.items()}], core_ids=[0])
    return np.ascontiguousarray(r.results[0]["out_y"].transpose(2, 1, 0).reshape(1, LAT, D))
```

```python
from contextlib import ExitStack, contextmanager

import numpy as np

import concourse.bass as bass
from concourse import mybir

F32 = mybir.dt.float32
F32R = mybir.dt.float32r
I32 = mybir.dt.int32
U8 = mybir.dt.uint8
ALU = mybir.AluOpType
ACT = mybir.ActivationFunctionType
AX = mybir.AxisListType

P = 128
D = 1024
KD = D // P
CTX, LAT = 256, 512
TALL = CTX + LAT
CHUNK = 128
LEVELS = 7
F_FF = 2816
FT = F_FF // P
FG = FT // 2
NMOD = 6 * KD
JW = 192
JOBS = 6 * D // JW
START_JOBS = -(-2 * D // JW)
POOL_TILES = {1: 3, 2: 3}
ROW_OF = {0: 0, 1: 0, 2: 1}
SEG_OF = {1: 0, 2: 1}
BANK = 512
ALPHA = 4.0 ** 0.25
LN_EPS, RMS_EPS, EPS = 1e-5, 1e-6, 1e-6
EPS_COL = {1e-5: "eps5", 1e-6: "eps6"}
NEG = -1.0e30
TWO_PI = 2.0 * np.pi
LATS = slice(CTX, TALL)
WINDOW = 16
HEAD_ORDER = [0, 2, 4, 6, 1, 3, 5, 7]


class Ticket:

    def __init__(self, counter, value, loop):
        self.counter, self.value, self.loop = counter, value, loop


class Counter:
    def __init__(self, name, sem):
        self.name, self.sem, self.value = name, sem, 0


class Loop:
    def __init__(self, index, count, strides):
        self.index, self.count, self.strides, self.closed = index, count, strides, False


class Program:

    def __init__(self, nc, ctx):
        self.nc, self.loop, self.waited = nc, None, {}
        self.engines = {"pe": nc.tensor, "act": nc.scalar, "dve": nc.vector, "pool": nc.gpsimd, "sp": nc.sync}
        self.counters = {}
        for name in ("pe", "act", "dve", "pool", "w0", "w1", "m0", "m1", "load", "store", "r0", "r1", "turn"):
            self.counters[name] = Counter(name, ctx.enter_context(nc.semaphore(f"done_{name}")))

    def wait(self, engine, *tickets):
        due = []
        for t in tickets:
            if t is None:
                continue
            value = t.value
            if t.loop is not None and t.loop.closed:
                value += (t.loop.count - 1) * t.loop.strides.get(t.counter.name, 0)
            inside = t.loop is not None and not t.loop.closed
            key = (engine, t.counter.name, inside)
            if self.waited.get(key, -1) >= value:
                continue
            self.waited[key] = value
            if inside:
                value = self.engines[engine].snap(value + t.loop.index * t.loop.strides.get(t.counter.name, 0))
            due.append((t.counter.sem, value))
        for sem, value in due:
            self.engines[engine].wait_ge(sem, value)

    def previous(self, t):
        return Ticket(t.counter, t.value - t.loop.strides[t.counter.name], t.loop)

    def done(self, name, instruction, step=1):
        c = self.counters[name]
        instruction.then_inc(c.sem, step)
        c.value += step
        return Ticket(c, c.value, self.loop)

    def at(self, name):
        return Ticket(self.counters[name], self.counters[name].value, self.loop)

    def pe(self, instruction):
        return self.done("pe", instruction)

    def act(self, instruction):
        return self.done("act", instruction)

    def dve(self, instruction):
        return self.done("dve", instruction)

    def pool(self, instruction):
        return self.done("pool", instruction)

    @contextmanager
    def repeat(self, count, **strides):
        start = {k: c.value for k, c in self.counters.items()}
        self.waited = {}
        with self.nc.Fori(0, count) as i:
            loop = self.loop = Loop(i, count, strides)
            yield i
        made = {k: c.value - start[k] for k, c in self.counters.items() if c.value != start[k]}
        assert made == strides, f"a pass of this loop adds {made}"
        loop.closed, self.loop, self.waited = True, None, {}
        for k, n in strides.items():
            self.counters[k].value += (count - 1) * n


class Kernel:
    def __init__(self, nc, ctx, ins, out):
        self.nc, self.ins, self.out = nc, ins, out
        self.p = Program(nc, ctx)
        self.tile = 0
        self.loaded, self.low = [None, None], [None, None]
        self.h_ready = [None] * KD
        self.rest = None
        self.sums, self.due = None, []
        self.tmp_turn = 0
        self.free_w = [None, None]
        self.free_hl = [None, None]
        self.free_ps = [[], []]
        sb = lambda name, shape, dt=F32: ctx.enter_context(nc.sbuf_tensor(name, shape, dt))
        self.x = sb("x", [P, KD, TALL])
        self.h_hi = sb("h_hi", [P, KD, TALL], F32R)
        self.h_lo = sb("h_lo", [P, KD, TALL], F32R)
        self.w_raw = [sb(f"w_raw{i}", [P, FG * P]) for i in range(2)]
        self.w_hi = [sb(f"w_hi{i}", [P, FG * P], F32R) for i in range(2)]
        self.w_lo = [sb(f"w_lo{i}", [P, FG * P], F32R) for i in range(2)]
        self.ones = sb("ones", [P, P])
        self.ident = sb("ident", [P, P])
        self.mods1 = sb("mods1", [P, 2, NMOD])
        self.mods2 = sb("mods2", [P, 2, NMOD, 2])
        self.small = sb("small", [P, SMALL_COLS])
        self.mean = sb("mean", [P, LAT])
        self.rstd = sb("rstd", [P, TALL])
        self.coef = sb("coef", [P, 4, 2, KD])
        self.c_act = sb("c_act", [P, 3 * KD])
        self.rows = nc.dram_tensor("mod_rows", (4, 2, 6 * D), F32, kind="Internal").ap()
        self.modulations_done = []
        self.columns_read = None
        self.tmp = [sb(f"tmp{i}", [P, LAT]) for i in range(2)]
        self.ps = ctx.enter_context(nc.psum_tensor("ps", [P, 8, BANK], F32))
        self.x_done = self.h_done = self.coef_read = self.bank_free = self.mods_made = self.rstd_free = None
        self.h_plain = [None] * KD
        self.x_tile, self.tmp_free = [None] * KD, [[], []]

    def col(self, name, i=0, n=1):
        at = SMALL[name][0] + i
        return self.small[:, at:at + n]

    def fetch_tile(self, s, name, n, kt):
        p, nc = self.p, self.nc
        if isinstance(n, int):
            at = self.ins[name][n, :, :]
        else:
            at = self.ins[name][bass.ds(nc.sync.snap(n), 1), :, :].rearrange("o p c -> (o p) c")
        p.wait("sp", self.free_w[s])
        self.loaded[s] = p.done(f"w{s}", nc.sync.dma_start(self.w_raw[s][:, 0:kt * P], at), 16)

    def split_tile(self, s, kt):
        p, nc = self.p, self.nc
        raw, hi, lo = (t[s][:, 0:kt * P] for t in (self.w_raw, self.w_hi, self.w_lo))
        p.wait("act", self.loaded[s], self.free_hl[s])
        high = p.act(nc.scalar.activation(hi, raw, ACT.Copy))
        p.wait("dve", high)
        self.low[s] = self.free_w[s] = p.dve(nc.vector.tensor_tensor(lo, raw, hi.bitcast(F32), ALU.subtract))

    def first_tiles(self):
        for g in range(3):
            self.fetch_tile(g % 2, *ORDER[g])
            if g == 0:
                self.split_tile(0, ORDER[0][2])

    def next_tmp(self):
        self.tmp_turn ^= 1
        return self.tmp_turn

    def add_sums(self):
        while self.due:
            self.sums.add(*self.due.pop(0))

    def load(self, dst, src, *after):
        p = self.p
        p.wait("sp", *after)
        return p.done("load", self.nc.sync.dma_start(dst, src), 16)


def _small_table():
    sizes = [("c1", 8), ("cc2", 8), ("c2", 8), ("ada_b", 96), ("mod_b", 96), ("ln_g", 32), ("ln_b", 32),
             ("lb_raw", 4), ("norm_g", 1), ("pool_scale", 8), ("fcw", 2 * 3 * FT), ("fcb", 2 * FT),
             ("gmix", 16), ("gffn", 16), ("gfin", 8), ("bgate", 4), ("ggla", 4), ("gq", 1), ("gk", 1),
             ("cw2", 2 * 3 * 2 * FT), ("cb2", 2 * 2 * FT), ("inv_freq", 1), ("sinks", 8), ("eps5", 1), ("eps6", 1)]
    table, at = {}, 0
    for name, n in sizes:
        table[name] = (at, n)
        at += n
    return table, at


SMALL, SMALL_COLS = _small_table()


def _order():
    def ffn(block, layer):
        return [(f"{kind}{block}{layer}", half * n + i, kt) for half in range(2)
                for kind, n, kt in (("up", 2 * FG, KD), ("down", KD, FG)) for i in range(n)]

    def run(name, n, kt=KD):
        return [(name, i, kt) for i in range(n)]

    return (run("in1", 22) + run("out1", KD) + ffn(0, 0) + run("pool", KD, 2) + ffn(0, 1) + run("in2", 17)
            + run("out2", KD) + ffn(1, 0) + run("qkv", 12) + run("attout", KD) + ffn(1, 1))


ORDER = _order()


def segments(tokens):
    both = [(0, CTX, 0), (CTX, LAT, 1)]
    return both if tokens == TALL else both[1:]


class Stream:

    def __init__(self, k, name, first, count, hi, lo, tokens, ready=None):
        self.k, self.name, self.first, self.count, self.kt = k, name, first, count, ORDER[k.tile][2]
        self.hi, self.lo, self.tokens = hi, lo, tokens
        self.ready = list(k.h_ready[:self.kt]) if ready is None else ready
        self.kept = {}
        self.jobs = self.made = None
        assert ORDER[k.tile][:2] == (name, first) and ORDER[k.tile + count - 1][:2] == (name, first + count - 1)

    def host(self, jobs):
        self.jobs = jobs
        jobs.start(self.k.tile % 2)
        return self

    def hosted(self, n, back):
        return not isinstance(n, int) or 0 <= n - back < self.jobs.count

    def product(self, s, low, ps):
        k, p, nc = self.k, self.k.p, self.k.nc
        p.wait("pe", low, *k.free_ps[s])
        wh = k.w_hi[s][:, 0:self.kt * P].rearrange("p (k n) -> p k n", n=P)
        wl = k.w_lo[s][:, 0:self.kt * P].rearrange("p (k n) -> p k n", n=P)
        for c in range(self.kt):
            if self.ready:
                p.wait("pe", self.ready[c])
            for n, (a, b) in enumerate(((wh, self.hi), (wh, self.lo), (wl, self.hi))):
                for t0, tn, bank in segments(self.tokens):
                    t0 -= TALL - b.shape[2]
                    last = nc.tensor.matmul(ps[:, bank, 0:tn], a[:, c, :], b[:, c, t0:t0 + tn],
                                            start=c == 0 and n == 0, stop=c == self.kt - 1 and n == 2)
        self.ready = ()
        product = p.pe(last)
        k.free_hl[s] = product
        return product

    def step(self, n, s, consume):
        k = self.k
        ps = k.ps[:, 2 * s:2 * s + 2, :]
        product = self.product(s, k.low[s], ps)
        if isinstance(n, int):
            if k.tile + 1 < len(ORDER):
                k.split_tile(1 - s, ORDER[k.tile + 1][2])
            if k.tile + 3 < len(ORDER):
                k.fetch_tile(1 - s, *ORDER[k.tile + 3])
            k.tile += 1
        else:
            k.split_tile(1 - s, self.kt)
            k.fetch_tile(1 - s, self.name, n + (3 + self.first), self.kt)
        if self.jobs is not None:
            if self.hosted(n, 2):
                self.jobs.store(n - 2, s)
            if self.hosted(n, 1):
                self.jobs.reduce(1 - s)
        k.add_sums()
        if self.made is not None:
            self.take(n - 1, 1 - s, consume)
        if self.jobs is not None and self.hosted(n, 0):
            self.jobs.compute(n, s)
        self.made = product

    def take(self, n, s, consume):
        self.k.free_ps[s] = list(consume(n, s, self.k.ps[:, 2 * s:2 * s + 2, :], self.made))

    def run(self, consume, **strides):
        k, p = self.k, self.k.p
        s0, count = k.tile % 2, self.count
        total = {"pe": 2, "act": 2, "dve": 2, "w0": 16, "w1": 16}
        if self.jobs is not None:
            nv = len(self.jobs.vectors)
            for name, n in (("pe", 2), ("act", 2), ("dve", 2 * nv * (KD - POOL_TILES[nv] + 1)), ("m0", 16), ("m1", 16), ("r0", 16), ("r1", 16)):
                total[name] = total.get(name, 0) + n
            total["pool"] = 2 * nv * (2 * POOL_TILES[nv] - 1)
        for name, n in strides.items():
            total[name] = total.get(name, 0) + n

        def tiles(ns):
            for n in ns:
                self.step(n, s0 if n % 2 == 0 else 1 - s0, consume)

        peeled = 3
        passes = (count - 2 * peeled) // 2
        if self.jobs is not None:
            passes = min(passes, (self.jobs.count - peeled) // 2)
        if passes < 2:
            tiles(range(count))
        else:
            tiles(range(peeled))
            with p.repeat(passes, **total) as i:
                carry = lambda t: t and Ticket(t.counter, t.value, p.loop)
                k.free_hl = [carry(t) for t in k.free_hl]
                k.free_w = [carry(t) for t in k.free_w]
                k.free_ps = [[carry(t) for t in ts] for ts in k.free_ps]
                k.low = [carry(t) for t in k.low]
                k.loaded = [carry(t) for t in k.loaded]
                self.kept = {name: carry(t) for name, t in self.kept.items()}
                self.made = carry(self.made)
                if self.jobs is not None:
                    self.jobs.kept = {name: carry(t) for name, t in self.jobs.kept.items()}
                    self.jobs.made = carry(self.jobs.made)
                for u in range(2):
                    self.step(i * 2 + (peeled + u), 1 - s0 if u == 0 else s0, consume)
            k.tile += 2 * passes
            tiles(range(peeled + 2 * passes, count))
        self.take(count - 1, (s0 + count - 1) % 2, consume)
        if self.jobs is not None:
            for n in range(count, self.jobs.count + 2):
                slot = (s0 + n) % 2
                self.jobs.store(n - 2, slot)
                if self.hosted(n, 1):
                    self.jobs.reduce(1 - slot)
            k.modulations_done = self.jobs.read_all()


class Sums:

    def __init__(self, k, tokens, square):
        self.k, self.tokens, self.square, self.count = k, tokens, square, 0

    def add(self, f, written):
        k, p, nc = self.k, self.k.p, self.k.nc
        first, stop = self.count == 0, self.count == KD - 1
        if first:
            p.wait("pe", k.ones_set, k.bank_free, k.columns_read)
        self.count += 1
        for t0, tn, bank in segments(self.tokens):
            value = k.x[:, f, t0:t0 + tn]
            i = k.next_tmp()
            if self.square:
                p.wait("act", written, *k.tmp_free[i])
                squared = p.act(nc.scalar.activation(k.tmp[i][:, 0:tn], value, ACT.Square))
                p.wait("pe", squared)
                value = k.tmp[i][:, 0:tn]
            else:
                p.wait("pe", written)
            self.done = p.pe(nc.tensor.matmul(k.ps[:, 6 + (bank if self.tokens == TALL else 0), 0:tn], k.ones[:, :],
                                              value, start=first, stop=stop))
            if self.square:
                k.tmp_free[i] = [self.done]


class Space:

    def __init__(self, k, ctx, name):
        sb = lambda n, shape: ctx.enter_context(k.nc.sbuf_tensor(f"{n}_{name}", shape, F32))
        self.k = k
        self.raw = [sb(f"m_raw{s}", [P, KD, JW]) for s in range(2)]
        self.acc = [sb(f"m_acc{s}", [P, 2, JW]) for s in range(2)]
        self.part, self.term = sb("m_part", [P, 2, JW]), sb("m_term", [P, 2, JW])
        self.row = [sb(f"m_row{s}", [1, 2, JW]) for s in range(2)]


class Modulations:

    def __init__(self, space, block, layer, first, count, vectors):
        k = space.k
        self.k, self.block, self.layer, self.first, self.count, self.vectors = k, block, layer, first, count, vectors
        nv = len(vectors)
        self.raw, self.part, self.term, self.made = space.raw, space.part, space.term, None
        self.acc, self.row = ([t[:, 0:nv, :] for t in ts] for ts in (space.acc, space.row))
        self.kept = {"stored0": k.p.at("r0"), "stored1": k.p.at("r1")}
        self.after = list(k.modulations_done)

    def fetch(self, j, s, *after):
        k, p = self.k, self.k.p
        first = (self.layer * JOBS) + self.first
        src = k.ins["ada_w" if self.block == 0 else "w_mod"]
        if isinstance(j, int):
            at = src[first + j, :, :]
        else:
            at = src[bass.ds(k.nc.sync.snap(j + first), 1), :, :].rearrange("o p c -> (o p) c")
        p.wait("sp", *after)
        self.kept[f"loaded{s}"] = p.done(f"m{s}", k.nc.sync.dma_start(
            self.raw[s][:, :, :].rearrange("p k n -> p (k n)"), at), 16)

    def start(self, s0, *after):
        self.fetch(0, s0, *self.after, *after)
        self.fetch(1, 1 - s0)

    def compute(self, j, s):
        k, p, nc = self.k, self.k.p, self.k.nc
        static = isinstance(j, int)
        ready = [self.kept[f"loaded{s}"], self.kept.get(f"reduced{s}"), k.c_done if static else None]
        c = lambda v, kk: k.c_act[:, v * KD + kk:v * KD + kk + 1]
        made = [None] * len(self.vectors)
        p.wait("pool", *ready, self.made)
        n_pool = POOL_TILES[len(self.vectors)]
        for kk in range(KD - n_pool, KD):
            for i, v in enumerate(self.vectors):
                w, part, term = self.raw[s][:, kk, :], self.part[:, i, :], self.term[:, i, :]
                if kk == KD - n_pool:
                    made[i] = p.pool(nc.gpsimd.tensor_tensor(part, w, c(v, kk).to_broadcast([P, JW]), ALU.mult))
                else:
                    p.wait("pool", made[i])
                    made[i] = p.pool(nc.gpsimd.tensor_tensor(term, w, c(v, kk).to_broadcast([P, JW]), ALU.mult))
            if kk > KD - n_pool:
                for i in range(len(self.vectors)):
                    part, term = self.part[:, i, :], self.term[:, i, :]
                    p.wait("pool", made[i])
                    made[i] = p.pool(nc.gpsimd.tensor_tensor(part, part, term, ALU.add))
        parts, made = made[-1], [None] * len(self.vectors)
        p.wait("dve", *ready)
        for kk in range(KD - n_pool):
            for i, v in enumerate(self.vectors):
                w, acc = self.raw[s][:, kk, :], self.acc[s][:, i, :]
                if kk == 0:
                    made[i] = p.dve(nc.vector.tensor_scalar(acc, w, c(v, kk), None, ALU.mult))
                else:
                    p.wait("dve", made[i])
                    made[i] = p.dve(nc.vector.scalar_tensor_tensor(acc, w, c(v, kk), acc, ALU.mult, ALU.add))
        p.wait("dve", parts, *made)
        for i in range(len(self.vectors)):
            acc = self.acc[s][:, i, :]
            made[i] = p.dve(nc.vector.tensor_tensor(acc, acc, self.part[:, i, :], ALU.add))
        self.made = made[-1]
        if not static or j + 2 < self.count:
            self.fetch(j + 2, s, self.made)

    def reduce(self, s):
        k, p, nc = self.k, self.k.p, self.k.nc
        p.wait("pe", self.made, self.kept.get(f"taken{s}"), k.ones_set)
        for i in range(len(self.vectors)):
            last = nc.tensor.matmul(k.ps[0:1, 4 + s, i * JW:(i + 1) * JW], k.ones[:, 0:1], self.acc[s][:, i, :],
                                    start=True, stop=True)
        self.kept[f"reduced{s}"] = p.pe(last)

    def store(self, j, s):
        k, p, nc = self.k, self.k.p, self.k.nc
        p.wait("act", self.kept[f"reduced{s}"], self.kept[f"stored{s}"])
        n = len(self.vectors) * JW
        row = self.row[s][:, :, :].rearrange("p v n -> p (v n)")
        read = self.kept[f"taken{s}"] = p.act(nc.scalar.activation(row, k.ps[0:1, 4 + s, 0:n], ACT.Copy))
        v0 = ROW_OF[self.vectors[0]]
        rows = k.rows[self.block * 2 + self.layer, :, :].rearrange("v (j n) -> v j n", n=JW)[v0:v0 + len(self.vectors)]
        if isinstance(j, int):
            out = rows[:, self.first + j, :]
        else:
            out = rows[:, bass.ds(nc.sync.snap(j + self.first), 1), :].rearrange("v o n -> v (o n)")
        p.wait("sp", read)
        self.kept[f"stored{s}"] = p.done(
            f"r{s}", nc.sync.dma_start(out.unsqueeze(0), self.row[s][:, :, :]), 16)
        self.stores = [self.kept["stored0"], self.kept["stored1"]]

    def read_all(self):
        return [self.made, *self.stores]


class Stages(Kernel):
    def constants(self):
        p, nc, ins = self.p, self.nc, self.ins
        self.load(self.small[:, :], ins["small"])
        self.load(self.ident[:, :], ins["ident"])
        self.load(self.x[:, :, LATS], ins["x"])
        self.load(self.mean[:, :].bitcast(I32), ins["positions"].to_broadcast([P, LAT]))
        self.consts = self.load(self.x[:, :, 0:CTX], ins["ctx"])
        self.ones_set = p.pool(nc.gpsimd.memset(self.ones[:, :], 1.0))

    def condition_start(self):
        p, nc = self.p, self.nc
        p.wait("act", self.consts)
        self.c_done = p.act(nc.scalar.activation(self.c_act[:, :], self.col("c1", 0, 3 * KD), ACT.Silu))
        with ExitStack() as ctx:
            jobs = Modulations(Space(self, ctx, "start"), 0, 0, 0, START_JOBS, [0])
            jobs.start(0)
            for n in range(jobs.count):
                jobs.compute(n, n % 2)
                jobs.reduce(n % 2)
                jobs.store(n, n % 2)
            self.modulations_done = jobs.read_all()
        self.columns_of(0, 0, [0], 0, 2 * KD)

    def rotary_table(self, i):
        p, nc = self.p, self.nc
        ang, turns, dst, quarter = self.mean[:, :], self.rstd[:, 0:LAT], self.tmp[i][:, :], (0.0, 0.25)[i]
        if i == 0:
            p.wait("dve", self.consts)
            made = p.dve(nc.vector.tensor_copy(ang, ang.bitcast(I32)))
            p.wait("dve", made)
            self.angles = p.dve(nc.vector.tensor_scalar(ang, ang, self.col("inv_freq"), None, ALU.mult))
        p.wait("dve", self.angles, self.rstd_free, *self.tmp_free[i])
        made = p.dve(nc.vector.tensor_scalar(turns, ang, float(1.0 / TWO_PI), quarter, ALU.mult, ALU.add))
        p.wait("dve", made)
        made = p.dve(nc.vector.tensor_scalar(turns, turns, 12582912.0, -12582912.0, ALU.add, ALU.add))
        src = ang
        for part in (6.28125, 0.0019350051879882812, 3.0199159819e-07):
            p.wait("dve", made)
            made = self.rstd_free = p.dve(nc.vector.scalar_tensor_tensor(dst, turns, -part, src, ALU.mult, ALU.add))
            src = dst
        p.wait("dve", made)
        made = p.dve(nc.vector.tensor_scalar(dst, dst, quarter * TWO_PI, 3.1415925, ALU.add, ALU.min))
        p.wait("dve", made)
        self.angles_read = p.dve(nc.vector.tensor_scalar(dst, dst, -3.1415925, None, ALU.max))
        p.wait("act", self.angles_read)
        self.tables = p.act(nc.scalar.activation(dst, dst, ACT.Sin))

    def columns_of(self, block, layer, vectors, f0, f1):
        p, nc = self.p, self.nc
        n, nv = f1 - f0, len(vectors)
        mods = self.mods1 if block == 0 else self.mods2
        turn = self.rstd[0:NMOD, 0:2 * P].rearrange("f (v c) -> f v c", v=2)
        rows = self.rows[block * 2 + layer, :, :].rearrange("v (f c) -> v f c", c=P)
        for v in range(nv):
            p.wait("sp", *self.modulations_done, self.rstd_free)
            loaded = p.done("turn", nc.sync.dma_start(turn[0:n, v, :], rows[ROW_OF[vectors[v]], f0:f1, :]), 16)
        p.wait("pe", loaded, self.columns_read)
        for v in range(nv):
            last = nc.tensor.matmul(self.ps[:, 7, v * n:(v + 1) * n], turn[0:n, v, :], self.ident[0:n, 0:n],
                                    is_transpose=True, start=True, stop=True)
        self.rstd_free = turned = p.pe(last)
        p.wait("dve", turned, self.consts)
        bias = self.col("ada_b" if block == 0 else "mod_b", layer * NMOD + f0, n)
        for v in range(nv):
            out = mods[:, layer, f0:f1] if block == 0 else mods[:, layer, f0:f1, SEG_OF[vectors[v]]]
            made = p.dve(nc.vector.tensor_tensor(out, self.ps[:, 7, v * n:(v + 1) * n], bias, ALU.add))
        self.columns_read = self.mods_made = made
        p.wait("dve", made)
        for m in (KD, 4 * KD):
            if f0 <= m < f1:
                for v in range(nv):
                    out = mods[:, layer, m:m + KD] if block == 0 else mods[:, layer, m:m + KD, SEG_OF[vectors[v]]]
                    self.mods_made = p.dve(nc.vector.tensor_scalar(out, out, 1.0, None, ALU.add))

    def mod(self, block, layer, m, f, seg=1):
        at = m * KD + f if isinstance(f, int) else f + m * KD
        at = slice(at, at + 1) if isinstance(at, int) else bass.ds(at, 1)
        if block == 0:
            return self.mods1[:, layer, at]
        return self.mods2[:, layer, at, seg]

    def split(self, f, t0, tn, value, made):
        p, nc = self.p, self.nc
        hi, lo = self.h_hi[:, f, t0:t0 + tn], self.h_lo[:, f, t0:t0 + tn]
        p.wait("act", made)
        high = p.act(nc.scalar.activation(hi, value, ACT.Copy))
        p.wait("dve", high)
        self.h_ready[f] = p.dve(nc.vector.tensor_tensor(lo, value, hi.bitcast(F32), ALU.subtract))
        return self.h_ready[f]

    def split_later(self, f, t0, tn, value, made, i):
        p, nc = self.p, self.nc
        hi, lo = self.h_hi[:, f, t0:t0 + tn], self.h_lo[:, f, t0:t0 + tn]
        p.wait("act", made)
        high = p.act(nc.scalar.activation(hi, value, ACT.Copy))
        self.split_rest()
        self.rest = (f, i, lo, value, hi, high)

    def split_rest(self):
        if self.rest is None:
            return
        p, nc = self.p, self.nc
        f, i, lo, value, hi, high = self.rest
        p.wait("dve", high)
        low = p.dve(nc.vector.tensor_tensor(lo, value, hi.bitcast(F32), ALU.subtract))
        self.h_ready[f] = self.h_done = low
        self.tmp_free[i], self.rest = [low], None

    def residual(self, block, layer, m, tokens, gate=None):
        x_ready = self.x_done

        def consume(n, s, ps, product):
            p, nc = self.p, self.nc
            p.wait("dve", product, x_ready if isinstance(n, int) else None)
            for t0, tn, bank in segments(tokens):
                g = self.mod(block, layer, m, n, seg=bank) if gate is None else gate(n)
                x = self.x[:, n if isinstance(n, int) else bass.ds(n, 1), t0:t0 + tn]
                if not isinstance(n, int):
                    x = x.rearrange("p o t -> p (o t)")
                done = p.dve(nc.vector.scalar_tensor_tensor(x, ps[:, bank, 0:tn], g, x, ALU.mult, ALU.add))
            self.x_done = done
            if self.sums is not None:
                self.due.append((n, done))
            return (done,)
        return consume

    def reciprocal_root(self, r, total, width, eps, made):
        p, nc = self.p, self.nc
        p.wait("act", made, self.rstd_free)
        log = self.bank_free = p.act(nc.scalar.activation(r, total, ACT.Ln, scale=1.0 / width, bias=self.col(EPS_COL[eps])))
        p.wait("act", log)
        return p.act(nc.scalar.activation(r, r, ACT.Exp, scale=-0.5))

    def coefficients(self, block, layer, m, which, seg):
        p, nc = self.p, self.nc
        scale, shift = (self.mods1[:, layer, i * KD:(i + 1) * KD] if block == 0 else
                        self.mods2[:, layer, i * KD:(i + 1) * KD, seg] for i in (m + 1, m))
        g, b, ga, ba = (self.coef[:, i, seg, :] for i in range(4))
        p.wait("dve", self.mods_made, self.consts, self.coef_read)
        if block == 1:
            made = p.dve(nc.vector.tensor_tensor(g, scale, self.col(which, layer * KD, KD), ALU.mult))
            p.dve(nc.vector.tensor_copy(b, shift))
            return p.at("dve")
        made = p.dve(nc.vector.tensor_tensor(b, scale, self.col("ln_b", which * KD, KD), ALU.mult))
        p.dve(nc.vector.tensor_tensor(g, scale, self.col("ln_g", which * KD, KD), ALU.mult))
        p.dve(nc.vector.tensor_scalar(ga, self.col("ln_g", which * KD, KD), ALPHA, None, ALU.mult))
        p.dve(nc.vector.tensor_scalar(ba, self.col("ln_b", which * KD, KD), ALPHA, None, ALU.mult))
        p.wait("dve", made)
        return p.dve(nc.vector.tensor_tensor(b, b, shift, ALU.add))

    def modulated(self, f, t0, tn, xr, seg, made, plain=None):
        p, nc = self.p, self.nc
        g, b = self.coef[:, 0, seg, f:f + 1], self.coef[:, 1, seg, f:f + 1]
        i = self.next_tmp()
        h = self.tmp[i][:, 0:tn] if plain is None else plain[:, f, :]
        p.wait("dve", made, *(self.tmp_free[i] if plain is None else ()))
        value = p.dve(nc.vector.tensor_scalar(h, xr, g, b, ALU.mult, ALU.add))
        if plain is None:
            self.split_later(f, t0, tn, h, value, i)
        else:
            self.h_done = self.h_plain[f] = value
        return value

    def layer_norm(self, which, layer=None, m=None, plain=None):
        p, nc = self.p, self.nc
        t0, tn = CTX, LAT
        mean, r = self.mean[:, :], self.rstd[:, t0:t0 + tn]
        ready = self.coefficients(0, layer, m, which, 1) if m is not None else None
        self.add_sums()
        p.wait("act", self.sums.done)
        made = self.bank_free = p.act(nc.scalar.activation(mean, self.ps[:, 6, 0:tn], ACT.Copy, scale=1.0 / D))
        self.sums = Sums(self, LAT, True)
        for f in range(KD):
            x = self.x[:, f, t0:t0 + tn]
            p.wait("dve", made)
            self.x_tile[f] = p.dve(nc.vector.tensor_tensor(x, x, mean, ALU.subtract))
            self.sums.add(f, self.x_tile[f])
        rstd = self.reciprocal_root(r, self.ps[:, 6, 0:tn], D, LN_EPS, self.sums.done)
        self.sums = None
        p.wait("dve", rstd, ready)
        if m is not None:
            p.wait("pool", ready)
        for f in range(KD):
            x = self.x[:, f, t0:t0 + tn]
            xr = p.dve(nc.vector.tensor_tensor(x, x, r, ALU.mult))
            if m is None:
                p.wait("dve", xr)
                self.x_tile[f] = p.dve(nc.vector.tensor_scalar(x, x, self.col("ln_g", which * KD + f),
                                                               self.col("ln_b", which * KD + f), ALU.mult, ALU.add))
            else:
                value = self.modulated(f, t0, tn, x, 1, xr, plain)
                p.wait("pool", value)
                self.x_tile[f] = p.pool(nc.gpsimd.tensor_scalar(x, x, self.coef[:, 2, 1, f:f + 1], self.coef[:, 3, 1, f:f + 1],
                                                                ALU.mult, ALU.add))
        self.split_rest()
        self.rstd_free = xr
        self.x_done = self.coef_read = self.x_tile[KD - 1]

    def modulate_first(self):
        p, nc = self.p, self.nc
        g, b = self.coef[:, 0, 1, :], self.coef[:, 1, 1, :]
        p.wait("dve", self.mods_made)
        p.dve(nc.vector.tensor_copy(g, self.mods1[:, 0, KD:2 * KD]))
        ready = p.dve(nc.vector.tensor_copy(b, self.mods1[:, 0, 0:KD]))
        for f in range(KD):
            x = self.x[:, f, LATS]
            value = self.modulated(f, CTX, LAT, x, 1, ready)
            p.wait("pool", value)
            self.x_tile[f] = p.pool(nc.gpsimd.tensor_scalar(x, x, ALPHA, None, ALU.mult))
        self.split_rest()
        self.x_done = self.coef_read = self.x_tile[KD - 1]

    def rms_modulate(self, layer, m, gain, tokens):
        p, nc = self.p, self.nc
        for _, _, bank in segments(tokens):
            ready = self.coefficients(1, layer, m, gain, bank)
        self.add_sums()
        roots = {}
        for t0, tn, bank in segments(tokens):
            roots[bank] = self.reciprocal_root(self.rstd[:, t0:t0 + tn], self.ps[:, 6 + (bank if tokens == TALL else 0), 0:tn],
                                               D, EPS, self.sums.done)
        self.sums = None
        for f in range(KD):
            for t0, tn, bank in segments(tokens):
                x = self.x[:, f, t0:t0 + tn]
                i = self.next_tmp()
                xr = self.tmp[i][:, 0:tn]
                p.wait("dve", roots[bank], ready, *self.tmp_free[i])
                scaled = p.dve(nc.vector.tensor_tensor(xr, x, self.rstd[:, t0:t0 + tn], ALU.mult))
                p.wait("dve", scaled)
                value = p.dve(nc.vector.tensor_scalar(xr, xr, self.coef[:, 0, bank, f:f + 1], self.coef[:, 1, bank, f:f + 1],
                                                      ALU.mult, ALU.add))
                self.split_later(f, t0, tn, xr, value, i)
        self.split_rest()
        self.rstd_free = self.coef_read = self.h_done

    def ffn(self, block, layer, tokens, sums, hosting=None):
        p, nc = self.p, self.nc
        with ExitStack() as ctx:
            sb = lambda name, shape, dt=F32: ctx.enter_context(nc.sbuf_tensor(f"{name}_{block}{layer}", shape, dt))
            t_first = TALL - tokens
            g_hi, g_lo = sb("g_hi", [P, FG, tokens], F32R), sb("g_lo", [P, FG, tokens], F32R)
            conv = [sb("conv_u", [P, TALL]), sb("conv_v", [P, TALL])]
            act = sb("silu_u", [P, TALL])
            g = sb("gated", [P, TALL])
            self.job_space = Space(self, ctx, f"{block}{layer}") if hosting else None
            cw, cb, parts = ("fcw", "fcb", 1) if block == 0 else ("cw2", "cb2", 2)
            base_w, base_b = SMALL[cw][0], SMALL[cb][0]
            down_done = self.h_done
            for half in range(2):
                up = Stream(self, f"up{block}{layer}", half * 2 * FG, 2 * FG, self.h_hi, self.h_lo, tokens)
                if hosting:
                    up.host(hosting.pop(0)(self.job_space))

                def taps(j, part, tap):
                    width = parts * 3 * FT
                    at = base_w + layer * width + (part * 3 + tap) * FT + half * FG
                    return self.small[:, at + j:at + j + 1] if isinstance(j, int) else self.small[:, bass.ds(j + at, 1)]

                def bias(j, part):
                    at = base_b + layer * parts * FT + part * FT + half * FG
                    return self.small[:, at + j:at + j + 1] if isinstance(j, int) else self.small[:, bass.ds(j + at, 1)]

                def convolve(j, part, ps, product, kept):
                    out = conv[part]
                    shifts = ((2, 0), (1, 1), (0, 2)) if block == 0 else ((1, 0), (0, 1), (-1, 2))
                    p.wait("act", product, kept)
                    for t0, tn, bank in segments(tokens):
                        centre = next(tap for d, tap in shifts if d == 0)
                        first = p.act(nc.scalar.activation(out[:, t0:t0 + tn], ps[:, bank, 0:tn], ACT.Identity,
                                                           scale=taps(j, part, centre), bias=bias(j, part)))
                    last = first
                    for d, tap in shifts:
                        if d == 0:
                            continue
                        p.wait("dve", last)
                        for t0, tn, bank in segments(tokens):
                            lo, hi = max(d, 0), tn + min(d, 0)
                            o = out[:, t0 + lo:t0 + hi]
                            last = p.dve(nc.vector.scalar_tensor_tensor(o, ps[:, bank, lo - d:hi - d], taps(j, part, tap),
                                                                        o, ALU.mult, ALU.add))
                    return last

                tall = slice(t_first, TALL)

                def consume(n, s, ps, product):
                    if isinstance(n, int):
                        is_u, j = n % 2 == 0, n // 2
                    else:
                        is_u, j = s == consume.s0, consume.pair
                    if is_u:
                        made = convolve(j, 0, ps, product, up.kept.get("silu"))
                        p.wait("act", made, up.kept.get("gated"))
                        up.kept["silu"] = p.act(nc.scalar.activation(act[:, tall], conv[0][:, tall], ACT.Silu))
                        return (made,)
                    where = j if isinstance(j, int) else bass.ds(j, 1)
                    hi, lo = g_hi[:, where, :], g_lo[:, where, :]
                    if not isinstance(j, int):
                        hi, lo = hi.rearrange("p o t -> p (o t)"), lo.rearrange("p o t -> p (o t)")
                    if block == 1:
                        made = convolve(j, 1, ps, product, up.kept.get("gated"))
                        p.wait("dve", made, up.kept["silu"], up.kept.get("low"))
                        gated = p.dve(nc.vector.tensor_tensor(g[:, tall], act[:, tall], conv[1][:, tall], ALU.mult))
                        read = made
                    else:
                        p.wait("dve", product, up.kept["silu"], up.kept.get("low"))
                        read = gated = p.dve(nc.vector.tensor_tensor(g[:, tall], act[:, tall], ps[:, 1, 0:LAT], ALU.mult))
                    up.kept["gated"] = gated
                    p.wait("act", gated, down_done)
                    high = p.act(nc.scalar.activation(hi, g[:, tall], ACT.Copy))
                    p.wait("dve", high)
                    low = up.kept["low"] = p.dve(nc.vector.tensor_tensor(lo, g[:, tall], hi.bitcast(F32), ALU.subtract))
                    self.g_ready = [*self.g_ready[1:], low]
                    return (read,)

                consume.s0 = self.tile % 2
                self.g_ready = [None, None]
                self.run_pairs(up, consume, block, tokens)
                if half == 1:
                    self.sums = sums
                ready = [self.g_ready[0]] * (FG - 1) + [self.g_ready[1]]
                down = Stream(self, f"down{block}{layer}", half * KD, KD, g_hi, g_lo, tokens, ready)
                if hosting:
                    down.host(hosting.pop(0)(self.job_space))
                down.run(self.residual(block, layer, 5, tokens))
                down_done = self.free_hl[1 - self.tile % 2]
                if half == 1 and hosting:
                    hosting.pop(0)()

    def run_pairs(self, up, consume, block, tokens):
        n_seg = len(segments(tokens))
        conv = n_seg * (1 if block == 0 else 2)
        orig = up.step

        def step(n, s, c):
            if not isinstance(n, int):
                consume.pair = self.p.loop.index + 1
            orig(n, s, c)

        up.step = step
        up.run(consume, act=conv + 2, dve=2 * conv + 2)

    def keep(self, dst, tokens, scale=1.0, func=ACT.Copy):
        t_first = TALL - tokens

        def consume(n, s, ps, product):
            p, nc = self.p, self.nc
            p.wait("act", product, self.z_free if isinstance(n, int) else None)
            for t0, tn, bank in segments(tokens):
                at = dst[:, n if isinstance(n, int) else bass.ds(n, 1), t0 - t_first:t0 - t_first + tn]
                if not isinstance(n, int):
                    at = at.rearrange("p o t -> p (o t)")
                self.z_done = p.act(nc.scalar.activation(at, ps[:, bank, 0:tn], func, scale=scale))
            return (self.z_done,)
        return consume

    def straight(self, name, first, count, tokens, consume, **strides):
        Stream(self, name, first, count, self.h_hi, self.h_lo, tokens).run(consume, **strides)

    def decayed_products(self, steps, att, masks, q, k, combs, diagonal, units, made, zeroed, scale=1.0,
                         beside=(None, None)):
        p, nc = self.p, self.nc
        W = combs[0].shape[1]
        reads = [None, None]

        def prepare(i):
            b, level, backward, mask = steps[i]
            comb = combs[i % 2]
            half = 1 << level
            v = lambda a: a.rearrange("p (n c) -> p n c", c=2 * half)
            bb, cc, qq, kk = v(b), v(comb), v(q), v(k)
            left, right = slice(0, half), slice(half, 2 * half)
            shape = [P, W // (2 * half), half]
            middle = half if backward else half - 1
            mid = bb[:, :, middle:middle + 1].to_broadcast(shape)
            p.wait("dve", made, reads[i % 2])
            p.dve(nc.vector.tensor_tensor(cc[:, :, left], mid, bb[:, :, left], ALU.subtract))
            ready = p.dve(nc.vector.tensor_tensor(cc[:, :, right], bb[:, :, right], mid, ALU.subtract))
            p.wait("act", ready)
            decays = p.act(nc.scalar.activation(comb, comb, ACT.Exp, scale=scale))
            p.wait("dve", decays)
            for side, factor in ((left, qq), (right, kk)) if backward else ((left, kk), (right, qq)):
                ready = p.dve(nc.vector.tensor_tensor(cc[:, :, side], cc[:, :, side], factor[:, :, side], ALU.mult))
            return comb, comb, mask, ready

        now = (*diagonal, made)
        for i in range(len(steps) + 1):
            following = prepare(i) if i < len(steps) else None
            if i == 0:
                p.wait("dve", zeroed)
            lhs, rhs, mask, ready = now
            reads[(i - 1) % 2] = self.products_to(att, lhs, rhs, units, ready, masks[:, mask, :])
            if i == beside[0]:
                made = beside[1]()
            now = following
        return reads

    def load_masks(self, masks, name, att, after):
        p, nc = self.p, self.nc
        n = masks.shape[1]
        wide = att[:, 0:n, :].bitcast(I32)
        loaded = self.load(wide, self.ins[name], after)
        p.wait("pool", loaded)
        packed = p.pool(nc.gpsimd.tensor_copy(masks[:, :, :], wide))
        p.wait("pool", packed)
        return packed, p.pool(nc.gpsimd.memset(att[:, :, :], 0.0))

    def products_to(self, att, lhs, rhs, units, made, mask):
        p, nc = self.p, self.nc
        last = None
        for b0 in range(0, len(units), 8):
            pair = (b0 // 8) % 2
            group = units[b0:b0 + 8]
            p.wait("pe", made, self.att_free[pair])
            for i, (rows, cols) in enumerate(group):
                out = self.ps[:, 4 + 2 * pair + i // 4, (i % 4) * P:(i % 4 + 1) * P]
                last = nc.tensor.matmul(out, lhs[rows, cols], rhs[rows, cols], start=True, stop=True)
            last = p.pe(last)
            p.wait("dve", last)
            n = len(group)
            got = self.ps[:, 4 + 2 * pair:6 + 2 * pair, :].rearrange("p b (i t) -> p (b i) t", t=P)[:, 0:n, :]
            self.att_free[pair] = self.att_done = p.dve(nc.vector.copy_predicated(
                att[:, b0:b0 + n, :], mask.unsqueeze(1).to_broadcast([P, n, P]), got))
        return last

    def even_mixer1(self):
        p, nc, ins = self.p, self.nc, self.ins
        self.z_free = None
        NC = LAT // CHUNK
        with ExitStack() as ctx:
            sb = lambda name, shape, dt=F32: ctx.enter_context(nc.sbuf_tensor(name, shape, dt))
            z = sb("z1", [P, 22, LAT])
            v = sb("v1", [P, NC, 5 * P])
            with ExitStack() as inner:
                st = Stream(self, "in1", 0, 22, self.h_hi, self.h_lo, LAT)
                st.host(Modulations(Space(self, inner, "in1"), 0, 0, START_JOBS, JOBS - START_JOBS, [0]))
                keep = self.keep(z, LAT)

                def consume(n, s, ps, product):
                    kept = keep(n, s, ps, product)
                    if isinstance(n, int) and n in (19, 20):
                        self.rotary_table(n - 19)
                    return kept

                st.run(consume, act=2)
                self.att_free[0] = max((st.jobs.kept[f"taken{s}"] for s in range(2)), key=lambda t: t.value)
            for f in range(5):
                units = [(slice(0, P), slice(t * P, (t + 1) * P)) for t in range(NC)]
                self.transposes(v[:, :, f * P:(f + 1) * P], z[:, 17 + f, :], units, self.z_done)
            self.kept, self.z_done = self.z_done, self.evicted
            self.columns_of(0, 0, [0], 2 * KD, NMOD)
            self.att_free[1] = self.columns_read
            zk = z[:, 16:17, :]
            self.rotation = self.rstd[:, 0:3 * P].rearrange("p (i c) -> p i c", i=3)
            p.wait("sp", self.rstd_free)
            self.rotation_loaded = p.done("turn", nc.sync.dma_start(self.rotation, ins["rot1"]), 16)
            z_done = self.z_done
            self.hgrn(ins, z, v, z_done)
            self.window_attention(ins, z, zk, v, z_done)
            self.sums = Sums(self, LAT, False)
            self.straight("out1", 0, KD, LAT, self.residual(0, 0, 2, LAT), dve=2)

    def hgrn(self, ins, z, v, z_done):
        p, nc = self.p, self.nc
        H, NC = 4, LAT // CHUNK
        W = H * LAT
        with ExitStack() as ctx:
            sb = lambda name, shape, dt=F32: ctx.enter_context(nc.sbuf_tensor(name, shape, dt))
            flat = lambda a, i: a[:, i:i + H, :].rearrange("p h t -> p (h t)")
            q, f, gate = flat(z, 0), flat(z, 4), flat(z, 8)
            k = sb("hk", [P, W])
            b = sb("hb", [P, W])
            comb = sb("hcomb", [P, W])
            att = sb("hatt", [P, H * NC, P])
            kd_t = flat(z, 18).rearrange("p (n c) -> p n c", c=P)
            state = f.rearrange("p (h c v) -> p h c v", h=H, c=NC)
            reset = self.mean
            masks = sb("hmasks", [P, LEVELS + 1, P], U8)
            lb = sb("hlb", [P, 4 * H])
            loaded = self.load(reset[:, :], ins["reset1"], self.angles_read)
            loaded, zeroed = self.load_masks(masks, "masks1", att, None)
            raw, e, prob, one_less = (lb[:, i * H:(i + 1) * H] for i in range(4))
            p.wait("dve", self.consts)
            made = p.dve(nc.vector.tensor_tensor(e, self.col("lb_raw", 0, H), self.col("lb_raw", 0, H), ALU.subtract))
            p.wait("act", made)
            made = p.act(nc.scalar.activation(e, e, ACT.Exp))
            p.wait("dve", made)
            made = p.dve(nc.vector.reciprocal(raw, e))
            p.wait("dve", made)
            made = p.dve(nc.vector.tensor_tensor(prob, e, raw, ALU.mult))
            p.wait("dve", made)
            made = p.dve(nc.vector.tensor_tensor(raw, prob, prob, ALU.subtract))
            p.wait("dve", made)
            lower = p.dve(nc.vector.tensor_scalar(one_less, raw, -1.0, 1.0, ALU.mult, ALU.add))
            p.wait("dve", self.kept)
            made = p.dve(nc.vector.tensor_scalar(f, f, -1.0, 40.0, ALU.mult, ALU.min))
            p.wait("act", made, *self.modulations_done)
            made = p.act(nc.scalar.activation(k[:, :], f, ACT.Exp))
            p.wait("act", made)
            made = p.act(nc.scalar.activation(f, k[:, :], ACT.Ln, bias=1.0))
            p.wait("act", made)
            made = p.act(nc.scalar.activation(f, f, ACT.Exp, scale=-1.0))
            p.wait("dve", made, lower)
            made = p.dve(nc.vector.tensor_tensor(k[:, :], k[:, :], f, ALU.mult))
            p.wait("dve", made)
            for h in range(H):
                at = slice(h * LAT, (h + 1) * LAT)
                p.dve(nc.vector.tensor_scalar(k[:, at], k[:, at], one_less[:, h:h + 1], None, ALU.mult))
                gates = p.dve(nc.vector.tensor_scalar(f[:, at], f[:, at], one_less[:, h:h + 1], raw[:, h:h + 1],
                                                      ALU.mult, ALU.add))
            p.wait("act", gates)
            logs = p.act(nc.scalar.activation(f, f, ACT.Ln))
            silu = p.act(nc.scalar.activation(gate, gate, ACT.Silu))
            p.wait("dve", logs, loaded)
            for h in range(H):
                at = slice(h * LAT, (h + 1) * LAT)
                summed = p.dve(nc.vector.tensor_tensor_scan(b[:, at], reset[:, :], f[:, at], 0.0, ALU.mult, ALU.add))
            units = [(slice(0, P), slice(h * LAT + c * CHUNK, h * LAT + (c + 1) * CHUNK))
                     for h in range(H) for c in range(NC)]
            reads = self.decayed_products([(b[:, :], level, False, level) for level in range(LEVELS)], att, masks, q, k[:, :],
                                          [comb[:, :], flat(z, 18)], (k, q, LEVELS), units, summed, zeroed)
            v3 = lambda a: a.rearrange("p (n c) -> p n c", c=CHUNK)
            ends = v3(b[:, :])[:, :, CHUNK - 1:CHUNK]
            p.wait("dve", *reads, summed)
            made = p.dve(nc.vector.tensor_tensor(v3(comb[:, :]), ends.to_broadcast([P, H * NC, CHUNK]), v3(b[:, :]), ALU.subtract))
            p.wait("act", made)
            made = p.act(nc.scalar.activation(comb[:, :], comb[:, :], ACT.Exp))
            p.wait("dve", made)
            made = p.dve(nc.vector.tensor_tensor(comb[:, :], comb[:, :], k[:, :], ALU.mult))
            kd_read = self.transposes(kd_t, comb, units, made)
            p.wait("act", self.att_done, *reads)
            qd = k
            p.wait("act", made)
            e2 = p.act(nc.scalar.activation(qd[:, :], b[:, :], ACT.Exp))
            ends_e = reset
            made_e = p.act(nc.scalar.activation(ends_e[:, 0:H * NC].unsqueeze(2), ends, ACT.Exp))
            p.wait("dve", e2)
            q_done = p.dve(nc.vector.tensor_tensor(qd[:, :], qd[:, :], q, ALU.mult))
            p.wait("pe", self.evicted, self.att_free[0], self.att_free[1])
            p.wait("dve", made_e)
            zero = p.dve(nc.vector.memset(state[:, :, 0, :], 0.0))
            for c in range(NC - 1):
                for h in range(H):
                    last = nc.tensor.matmul(self.ps[:, 4 + c, h * P:(h + 1) * P], kd_t[:, h * NC + c, :],
                                            v[:, c, (1 + h) * P:(2 + h) * P], start=True, stop=True)
                got = p.pe(last)
                p.wait("dve", got, zero)
                for h in range(H):
                    zero_next = p.dve(nc.vector.scalar_tensor_tensor(
                        state[:, h, c + 1, :], state[:, h, c, :], ends_e[:, h * NC + c:h * NC + c + 1],
                        self.ps[:, 4 + c, h * P:(h + 1) * P], ALU.mult, ALU.add))
                zero = zero_next
            p.wait("pe", self.att_done, q_done, zero)
            outs = []
            for h in range(H):
                for c in range(NC):
                    out = self.ps[:, 4 + h, c * P:(c + 1) * P]
                    nc.tensor.matmul(out, v[:, c, (1 + h) * P:(2 + h) * P], att[:, h * NC + c, :], start=True, stop=False)
                    last = nc.tensor.matmul(out, state[:, h, c, :], qd[:, h * LAT + c * CHUNK:h * LAT + (c + 1) * CHUNK],
                                            start=False, stop=True)
                outs.append(p.pe(last))
            squares, summed = flat(z, 18), []
            heads = [slice(h * LAT, (h + 1) * LAT) for h in range(H)]
            for h, at in enumerate(heads):
                p.wait("act", outs[h], kd_read, zero)
                copied = p.act(nc.scalar.activation(comb[:, at], self.ps[:, 4 + h, :], ACT.Copy))
                p.wait("act", copied)
                squared = p.act(nc.scalar.activation(squares[:, at], comb[:, at], ACT.Square))
                p.wait("pe", squared)
                summed.append(p.pe(nc.tensor.matmul(self.ps[:, 4 + h, :], self.ones[:, :], squares[:, at], start=True, stop=True)))
            for h, at in enumerate(heads):
                p.wait("act", summed[h])
                logs = p.act(nc.scalar.activation(b[:, at], self.ps[:, 4 + h, :], ACT.Ln, scale=1.0 / P,
                                                  bias=self.col(EPS_COL[RMS_EPS])))
            p.wait("act", logs)
            roots = p.act(nc.scalar.activation(b[:, :], b[:, :], ACT.Exp, scale=-0.5))
            for h, at in enumerate(heads):
                o = comb[:, at]
                p.wait("dve", roots, silu)
                made = p.dve(nc.vector.scalar_tensor_tensor(o, o, self.col("norm_g"), b[:, at], ALU.mult, ALU.mult))
                p.wait("dve", made)
                made = p.dve(nc.vector.tensor_tensor(o, o, gate[:, at], ALU.mult))
                self.h_done = self.split(h, CTX, LAT, o, made)
            self.att_free = [self.h_done, self.h_done]

    def transposes(self, dst, src, units, made):
        p, nc = self.p, self.nc
        for b0 in range(0, len(units), 8):
            pair = (b0 // 8) % 2
            group = units[b0:b0 + 8]
            p.wait("pe", made, self.att_free[pair])
            rows_n = group[0][0].stop - group[0][0].start
            for i, (rows, cols) in enumerate(group):
                last = nc.tensor.matmul(self.ps[:, 4 + 2 * pair + i // 4, (i % 4) * P:(i % 4) * P + rows_n], src[rows, cols],
                                        self.ident[rows, rows], is_transpose=True, start=True, stop=True)
            last = p.pe(last)
            p.wait("act", last)
            n = len(group)
            got = self.ps[:, 4 + 2 * pair:6 + 2 * pair, :].rearrange("p b (i t) -> p (b i) t", t=P)[:, 0:n, 0:rows_n]
            self.att_free[pair] = self.evicted = p.act(nc.scalar.activation(dst[:, b0:b0 + n, 0:rows_n], got, ACT.Copy))
        return last

    def window_attention(self, ins, z, zk, v, z_done):
        p, nc = self.p, self.nc
        NB, QT, NQ = LAT // P, 4, 8
        with ExitStack() as ctx:
            sb = lambda name, shape, dt=F32: ctx.enter_context(nc.sbuf_tensor(name, shape, dt))
            turned = sb("turned1", [P, LAT])
            sin, cos = self.tmp[0][:, :], self.tmp[1][:, :]
            rot = self.rotation
            kk = sb("kk1", [P, 2, LAT])
            mask = sb("wmask", [P, 2 * P])
            s = [sb("scores1", [P, NQ, 2 * P]), z[:, 0:4, :].rearrange("p h (i k) -> p (h i) k", k=2 * P)]
            pt = [sb("probs1t", [P, 2 * NQ, P]), z[:, 4:8, :].rearrange("p h (i k) -> p (h i) k", k=P)]
            m, rs, es = sb("wm", [P, NQ]), sb("wrs", [P, NQ]), sb("wes", [P, NQ])
            o = z[:, 8:12, :]
            loaded = self.load(mask[:, :], ins["wmask"], self.h_done)
            rotated, roped = [], None
            for j in range(QT + 1):
                x = z[:, 12 + j, :] if j < QT else zk[:, 0, :]
                bank = j % 2
                p.wait("pe", self.rotation_loaded, z_done, *((rotated[j - 2],) if j > 1 else self.free_ps[j]))
                got = p.pe(nc.tensor.matmul(self.ps[:, bank, :], rot[:, 0, :], x, start=True, stop=True))
                p.wait("dve", got, self.tables, roped, self.h_done)
                made = p.dve(nc.vector.tensor_tensor(turned[:, :], self.ps[:, bank, :], sin, ALU.mult))
                rotated.append(made)
                made2 = p.dve(nc.vector.tensor_tensor(x, x, cos, ALU.mult))
                p.wait("dve", made2, made)
                roped = p.dve(nc.vector.tensor_tensor(x, x, turned[:, :], ALU.add))
            self.tmp_free = [[roped], [roped]]
            for g in range(2):
                p.wait("pe", roped, *rotated, self.h_done)
                got = p.pe(nc.tensor.matmul(self.ps[:, 4 + g, :], rot[:, 1 + g, :], zk[:, 0, :], start=True, stop=True))
                p.wait("act", got)
                keys = p.act(nc.scalar.activation(kk[:, g, :], self.ps[:, 4 + g, :], ACT.Copy))
            order = HEAD_ORDER
            banks = [self.ps[:, 4:8, :], self.ps[:, 0:4, :]]
            self.rstd_free = keys
            free = [(keys,), (keys, *self.free_ps[0], *self.free_ps[1])]
            free_s, free_pt = [self.h_done, self.h_done], [self.h_done, self.h_done]

            def scores(n):
                ps, sn = banks[n % 2], s[n % 2][:, :, 0:min(n + 1, 2) * P]
                k0, nk = max(n - 1, 0) * P, sn.shape[2]
                p.wait("pe", roped, *free[n % 2])
                for i, h in enumerate(order):
                    rows = slice((h % 2) * 64, (h % 2) * 64 + 64)
                    last = nc.tensor.matmul(ps[:, i // 2, (i % 2) * 256:(i % 2) * 256 + nk],
                                            z[rows, 12 + h // 2, n * P:(n + 1) * P], kk[rows, h // 4, k0:k0 + nk],
                                            start=True, stop=True)
                return p.pe(last)

            def softmax(n, scored):
                ps, sn = banks[n % 2], s[n % 2][:, :, 0:min(n + 1, 2) * P]
                nk = sn.shape[2]
                m0 = 2 * P - nk
                got = ps.rearrange("p b (i k) -> p (b i) k", k=256)[:, :, 0:nk]
                p.wait("dve", scored, free_s[n % 2], loaded)
                made = p.dve(nc.vector.scalar_tensor_tensor(sn, got, 64 ** -0.5,
                             mask[:, m0:2 * P].unsqueeze(1).to_broadcast([P, NQ, nk]), ALU.mult, ALU.add))
                p.wait("dve", made)
                made = p.dve(nc.vector.tensor_reduce(m[:, :], sn, AX.X, ALU.max))
                p.wait("dve", made)
                made = p.dve(nc.vector.tensor_tensor(m[:, :], m[:, :], self.col("sinks", 0, NQ), ALU.max))
                p.wait("dve", made)
                p.dve(nc.vector.tensor_tensor(es[:, :], self.col("sinks", 0, NQ), m[:, :], ALU.subtract))
                made = p.dve(nc.vector.tensor_tensor(sn, sn, m[:, :].unsqueeze(2).to_broadcast([P, NQ, nk]), ALU.subtract))
                p.wait("act", made)
                p.act(nc.scalar.activation(es[:, :], es[:, :], ACT.Exp))
                made = p.act(nc.scalar.activation(sn, sn, ACT.Exp))
                p.wait("dve", made)
                made = p.dve(nc.vector.tensor_reduce(rs[:, :], sn, AX.X, ALU.add))
                p.wait("dve", made)
                made = p.dve(nc.vector.tensor_tensor(rs[:, :], rs[:, :], es[:, :], ALU.add))
                p.wait("dve", made)
                made = p.dve(nc.vector.reciprocal(rs[:, :], rs[:, :]))
                p.wait("dve", made)
                return p.dve(nc.vector.tensor_tensor(sn, sn, rs[:, :].unsqueeze(2).to_broadcast([P, NQ, nk]), ALU.mult))

            probs = softmax(0, scores(0))
            for n in range(NB):
                ready = probs
                if n + 1 < NB:
                    scored = scores(n + 1)
                ps, sn, pn = banks[n % 2], s[n % 2], pt[n % 2]
                nkb = min(n + 1, 2)
                p.wait("pe", ready)
                for i in range(NQ):
                    for j in range(nkb):
                        u = i * nkb + j
                        last = nc.tensor.matmul(ps[:, u // 4, (u % 4) * P:(u % 4 + 1) * P], sn[:, i, j * P:(j + 1) * P],
                                                self.ident[:, :], is_transpose=True, start=True, stop=True)
                free_s[n % 2] = p.pe(last)
                nu = NQ * nkb
                p.wait("act", free_s[n % 2], free_pt[n % 2])
                moved = p.act(nc.scalar.activation(pn[:, 0:nu, :], ps[:, 0:nu // 4, :].rearrange("p b (i t) -> p (b i) t", t=P),
                                                   ACT.Copy))
                p.wait("pe", moved)
                for i, h in enumerate(order):
                    rows = slice((h % 2) * 64, (h % 2) * 64 + 64)
                    for j in range(nkb):
                        last = nc.tensor.matmul(ps[rows, 0, (h // 2) * P:(h // 2 + 1) * P],
                                                v[:, max(n - 1, 0) + j, (h // 4) * 64:(h // 4) * 64 + 64], pn[:, i * nkb + j, :],
                                                start=j == 0, stop=j == nkb - 1)
                mixed = free_pt[n % 2] = p.pe(last)
                p.wait("act", mixed)
                mixed_out = p.act(nc.scalar.activation(o[:, :, n * P:(n + 1) * P], ps[:, 0, :].rearrange("p (i t) -> p i t", t=P),
                                                       ACT.Copy))
                free[n % 2] = (mixed_out,)
                if n + 1 < NB:
                    probs = softmax(n + 1, scored)
            self.free_ps = [[mixed_out], [mixed_out]]
            free = mixed_out
            for f in range(QT):
                self.h_done = self.split(4 + f, CTX, LAT, o[:, f, :], free)
            self.att_free = [self.h_done, self.h_done]

    def pool_mixer(self, layer, which):
        p, nc, ins = self.p, self.nc, self.ins
        with ExitStack() as ctx:
            sb = lambda name, shape, dt=F32: ctx.enter_context(nc.sbuf_tensor(name, shape, dt))
            h, recip = sb("pool_h", [P, KD, LAT]), sb("pool_recip", [P, 4, WINDOW])
            gate, wins = sb("pool_gate", [P, KD]), [sb(f"pool_win{i}", [P, LAT])[:, :] for i in range(8)]
            loaded = self.load(recip[:, :, :], ins["recip"], self.x_done)
            wins_free = [None, None]
            self.layer_norm(which, layer, 0, plain=h)
            p.wait("dve", self.mods_made)
            gated = p.dve(nc.vector.tensor_tensor(gate[:, :], self.mods1[:, layer, 2 * KD:3 * KD], self.col("pool_scale", 0, KD), ALU.mult))
            p.wait("dve", loaded, gated)
            self.sums = Sums(self, LAT, False)
            p.wait("pool", loaded)
            def window(f, buffers):
                name, engine = ("pool", nc.gpsimd) if f >= 6 else ("dve", nc.vector)
                p.wait(name, self.h_plain[f])
                src, made = h[:, f, :], wins_free[f % 2] if f < 6 else None
                for d in range(f // 2 + 1):
                    w, dst = 1 << d, buffers[d % 2]
                    p.wait(name, made)
                    p.done(name, engine.tensor_tensor(dst[:, w:], src[:, w:], src[:, 0:LAT - w], ALU.add))
                    made = p.done(name, engine.tensor_copy(dst[:, 0:w], src[:, 0:w]))
                    src = dst
                p.wait(name, made)
                made = p.done(name, engine.tensor_tensor(src[:, 0:WINDOW], src[:, 0:WINDOW], recip[:, f // 2, :], ALU.mult))
                return src, made

            wide = [window(f, wins[4 + 2 * (f % 2):6 + 2 * (f % 2)]) for f in (6, 7)]
            for f in range(KD):
                src, made = wide[f - 6] if f >= 6 else window(f, wins[2 * (f % 2):2 * (f % 2) + 2])
                p.wait("dve", made)
                made = p.dve(nc.vector.scalar_tensor_tensor(src, src, 1.0 / (2 << (f // 2)), h[:, f, :], ALU.mult, ALU.subtract))
                self.h_done = wins_free[f % 2] = self.split(f, CTX, LAT, src, made)
            for g in range(4):
                at = slice(2 * g, 2 * g + 2)
                Stream(self, "pool", 2 * g, 2, self.h_hi[:, at, :], self.h_lo[:, at, :], LAT, self.h_ready[at]).run(
                              self.shifted(self.residual(0, layer, 2, LAT, gate=lambda n: gate[:, n:n + 1]), 2 * g))

    def shifted(self, consume, by):
        return lambda n, s, ps, product: consume(n + by, s, ps, product)

    def even_mixer2(self):
        p, nc, ins = self.p, self.nc, self.ins
        T = TALL
        with ExitStack() as ctx:
            sb = lambda name, shape, dt=F32: ctx.enter_context(nc.sbuf_tensor(name, shape, dt))
            v = sb("v2", [P, T // P, 4 * P])
            z = sb("z2", [P, 9, T])
            with ExitStack() as inner:
                more = inner.enter_context(nc.sbuf_tensor("z2more", [P, 8, T], F32))
                self.z_free = self.h_done
                self.straight("in2", 0, 9, T, self.keep(z, T), act=4)
                self.straight("in2", 9, 8, T, self.keep(more, T), act=4)
                z_done = self.z_done
                for f in range(4):
                    units = [(slice(0, P), slice(t * P, (t + 1) * P)) for t in range(T // P)]
                    self.transposes(v[:, :, f * P:(f + 1) * P], more[:, f, :], units, z_done)
                self.z_free = self.evicted
                self.fourier(inner, more, z_done)
            self.gla(z, v)
            self.sums = Sums(self, T, True)
            self.straight("out2", 0, KD, T, self.residual(1, 0, 2, T), dve=4)

    def fourier(self, ctx, more, z_done):
        p, nc, ins = self.p, self.nc, self.ins
        sb = lambda name, shape, dt=F32: ctx.enter_context(nc.sbuf_tensor(name, shape, dt))
        feat = sb("dft_f", [P, 2 * P])
        lat, con = sb("dft_lat", [P, 2, LAT // P, LAT]), sb("dft_ctx", [P, 2, CTX // P, CTX])
        a = more[:, 0:2, :].rearrange("p k t -> p (k t)").rearrange("p (t c) -> p t c", c=2 * P)
        f, u = more[:, 2, :], more[:, 4:8, :]
        self.gate_weights = self.tmp[0][0:16, :].rearrange("p (f c) -> p f c", c=P)
        p.wait("sp", *self.tmp_free[0])
        self.gate_loaded = p.done("turn", nc.sync.dma_start(self.gate_weights, ins["w_gate"]), 16)
        self.load(feat[:, :], ins["dft_f"], self.z_free)
        self.load(lat[:, :, :, :], ins["dft_lat"])
        loaded = self.load(con[:, :, :, :], ins["dft_ctx"])
        done = None
        for g in range(4):
            p.wait("pe", loaded, z_done, done, self.att_free[0], self.att_free[1])
            for t in range(TALL // P):
                last = nc.tensor.matmul(self.ps[:, 4 + t // 2, (t % 2) * 256:(t % 2) * 256 + 256],
                                        u[:, g, t * P:(t + 1) * P], feat[:, :], start=True, stop=True)
            got = p.pe(last)
            p.wait("act", got, done)
            rows = p.act(nc.scalar.activation(a, self.ps[:, 4:7, :].rearrange("p b (i c) -> p (b i) c", c=2 * P), ACT.Copy))
            p.wait("pe", rows)
            for t0, tn, bank in segments(TALL):
                basis = con if bank == 0 else lat
                nt = tn // P
                for part in range(2):
                    for t in range(nt):
                        last = nc.tensor.matmul(self.ps[:, 4 + bank, 0:tn], a[:, t0 // P + t, part * P:(part + 1) * P],
                                                basis[:, part, t, :], start=part == 0 and t == 0,
                                                stop=part == 1 and t == nt - 1)
            got = p.pe(last)
            p.wait("act", got, done)
            p.act(nc.scalar.activation(f[:, 0:CTX], self.ps[:, 4, 0:CTX], ACT.Copy))
            made = p.act(nc.scalar.activation(f[:, CTX:TALL], self.ps[:, 5, 0:LAT], ACT.Copy))
            done = self.split(g, 0, TALL, f, made)
        self.h_done = done
        self.att_free = [done, done]

    def gla(self, z, v):
        p, nc, ins = self.p, self.nc, self.ins
        T, H, NC = TALL, 4, TALL // CHUNK
        W = 2 * T
        with ExitStack() as ctx:
            sb = lambda name, shape, dt=F32: ctx.enter_context(nc.sbuf_tensor(name, shape, dt))
            flat = lambda i, n: z[:, i:i + n, :].rearrange("p h t -> p (h t)")
            q, k = flat(0, 2), flat(2, 2)
            b = [sb(f"gb{d}", [P, W]) for d in range(2)]
            comb = sb("gcomb", [P, W])
            att = sb("gatt", [P, H * NC, P])
            kd_t = [sb(f"gkdt{d}", [P, 2 * NC, P]) for d in range(2)]
            masks = sb("gmasks", [P, 2 * LEVELS + 1, P], U8)
            reset = sb("greset", [P, T])
            wg, wg_loaded = self.gate_weights, self.gate_loaded
            ends = sb("gends", [P, 2, 2 * NC])
            start = self.h_done
            self.load(reset[:, :], ins["reset2"], start)
            loaded, zeroed = self.load_masks(masks, "masks2", att, start)
            p.wait("dve", start)
            p.dve(nc.vector.tensor_scalar(q, q, 0.125, None, ALU.mult))
            logas = [comb[:, :], kd_t[0][:, :, :].rearrange("p n c -> p (n c)")]

            def gates(d):
                loga, e, b0 = logas[d], b[d][:, :], 4 - 4 * d
                p.wait("pe", wg_loaded, self.h_done, *self.free_ps[0], *self.free_ps[1])
                for f in range(2):
                    for t0, tn, bank in segments(T):
                        last = nc.tensor.matmul(self.ps[:, b0 + 2 * f + bank, 0:tn], wg[:, 2 * d + f, :],
                                                z[0:16, 8, t0:t0 + tn], start=True, stop=True)
                got = p.pe(last)
                p.wait("act", got)
                for f in range(2):
                    for t0, tn, bank in segments(T):
                        x = p.act(nc.scalar.activation(loga[:, f * T + t0:f * T + t0 + tn], self.ps[:, b0 + 2 * f + bank, 0:tn],
                                                       ACT.Identity, bias=self.col("bgate", 2 * d + f)))
                if d == 1:
                    self.tmp_free[0], self.free_ps = [got], [[x], [x]]
                p.wait("dve", x)
                made = p.dve(nc.vector.scalar_tensor_tensor(e, loga, -1.0, loga, ALU.mult, ALU.min))
                p.wait("act", made)
                made = p.act(nc.scalar.activation(e, e, ACT.Exp))
                p.wait("act", made)
                made = p.act(nc.scalar.activation(e, e, ACT.Ln, bias=1.0))
                p.wait("dve", made)
                made = p.dve(nc.vector.scalar_tensor_tensor(loga, loga, 0.0, e, ALU.min, ALU.subtract))
                p.wait("dve", made, loaded)
                for f in range(2):
                    at = slice(f * T, (f + 1) * T)
                    made = p.dve(nc.vector.tensor_tensor_scan(e[:, at], reset[:, :], loga[:, at], 0.0, ALU.mult, ALU.add))
                if d == 1:
                    p.wait("dve", made)
                    n3 = lambda a: a.rearrange("p (n c) -> p n c", c=CHUNK)
                    made = p.dve(nc.vector.tensor_tensor(e, e, loga, ALU.subtract))
                    total = ends[:, 1, :].unsqueeze(2)
                    p.wait("dve", made)
                    made = p.dve(nc.vector.tensor_tensor(total, n3(e)[:, :, CHUNK - 1:CHUNK], n3(loga)[:, :, CHUNK - 1:CHUNK], ALU.add))
                return made

            forward = gates(0)
            units = [(slice((h % 2) * 64, (h % 2) * 64 + 64), slice((h // 2) * T + c * CHUNK, (h // 2) * T + (c + 1) * CHUNK))
                     for h in (0, 2, 1, 3) for c in range(NC)]
            p.wait("dve", forward)
            made = p.dve(nc.vector.tensor_scalar(comb[:, :], k, 2.0, None, ALU.mult))
            steps = [(b[d][:, :], level, d == 1, d * LEVELS + level) for d in range(2) for level in range(LEVELS)]
            turned = kd_t[1][:, :, :].rearrange("p n c -> p (n c)")
            reads = self.decayed_products(steps, att, masks, q, k, [turned, comb[:, :]], (comb, q, 2 * LEVELS), units, made, zeroed, 1.0 / 16.0,
                                          beside=(2, lambda: gates(1)))
            silu = p.act(nc.scalar.activation(flat(4, H), flat(4, H), ACT.Silu))
            v3 = lambda a: a.rearrange("p (n c) -> p n c", c=CHUNK)
            full = [(slice(0, P), slice(f * T + c * CHUNK, f * T + (c + 1) * CHUNK)) for f in range(2) for c in range(NC)]
            e0, e1 = b[0][:, :], b[1][:, :]
            p.wait("dve", *reads, self.att_done)
            kept = p.dve(nc.vector.tensor_copy(ends[:, 0, :].unsqueeze(2), v3(e0)[:, :, CHUNK - 1:CHUNK]))
            p.wait("dve", kept)
            made = p.dve(nc.vector.tensor_tensor(v3(comb[:, :]), ends[:, 0, :].unsqueeze(2).to_broadcast([P, 2 * NC, CHUNK]), v3(e0), ALU.subtract))
            p.wait("act", made)
            made = p.act(nc.scalar.activation(comb[:, :], comb[:, :], ACT.Exp, scale=1.0 / 16.0))
            p.wait("dve", made)
            made = p.dve(nc.vector.tensor_tensor(comb[:, :], comb[:, :], k, ALU.mult))
            read = self.transposes(kd_t[0], comb, full, made)
            p.wait("act", read)
            made = p.act(nc.scalar.activation(comb[:, :], e1, ACT.Exp, scale=1.0 / 16.0))
            p.wait("dve", made)
            made = p.dve(nc.vector.tensor_tensor(comb[:, :], comb[:, :], k, ALU.mult))
            read = self.transposes(kd_t[1], comb, full, made)
            p.wait("act", kept)
            f_done = p.act(nc.scalar.activation(e0, e0, ACT.Exp, scale=1.0 / 16.0))
            p.wait("dve", made, f_done)
            p.dve(nc.vector.tensor_tensor(e0, e0, q, ALU.mult))
            made = p.dve(nc.vector.tensor_tensor(v3(e1), ends[:, 1, :].unsqueeze(2).to_broadcast([P, 2 * NC, CHUNK]), v3(e1), ALU.subtract))
            p.wait("act", made)
            made = p.act(nc.scalar.activation(e1, e1, ACT.Exp, scale=1.0 / 16.0))
            ends_e = p.act(nc.scalar.activation(ends[:, :, :], ends[:, :, :], ACT.Exp, scale=1.0 / 16.0))
            p.wait("dve", made)
            q_done = p.dve(nc.vector.tensor_tensor(e1, e1, q, ALU.mult))
            state = flat(0, 4).rearrange("p (d n v) -> p d n v", d=2, v=P)
            lat0 = CTX // CHUNK
            orders = [list(range(NC)), list(range(lat0 - 1, -1, -1)) + list(range(NC - 1, lat0 - 1, -1))]
            p.wait("pool", q_done)
            for d in range(2):
                for f in range(2):
                    init = p.pool(nc.gpsimd.memset(state[:, d, f * NC + orders[d][0], :], 0.0))
            p.wait("dve", ends_e, init)
            stepped = [self.evicted, self.evicted]
            for n in range(NC - 1):
                for d in range(2):
                    c, nxt = orders[d][n], orders[d][n + 1]
                    bank = 4 + 2 * d + n % 2
                    p.wait("pe", *stepped, self.att_free[0], self.att_free[1])
                    for h in range(H):
                        rows = slice((h % 2) * 64, (h % 2) * 64 + 64)
                        last = nc.tensor.matmul(self.ps[rows, bank, (h // 2) * P:(h // 2 + 1) * P],
                                                kd_t[d][:, (h // 2) * NC + c, rows], v[:, c, h * P:(h + 1) * P], start=True, stop=True)
                    got = p.pe(last)
                    p.wait("dve", got, stepped[d])
                    for f in range(2):
                        stepped[d] = p.dve(nc.vector.scalar_tensor_tensor(
                            state[:, d, f * NC + nxt, :], state[:, d, f * NC + c, :], ends[:, d, f * NC + c:f * NC + c + 1],
                            self.ps[:, bank, f * P:(f + 1) * P], ALU.mult, ALU.add))
            p.wait("pe", self.att_done, q_done, *stepped)
            free_o = [None, None]
            for h in range(H):
                rows = slice((h % 2) * 64, (h % 2) * 64 + 64)
                b0 = 4 + 2 * (h % 2)
                p.wait("pe", free_o[h % 2])
                for t0, tn, bank in segments(T):
                    for c in range(t0 // P, (t0 + tn) // P):
                        out = self.ps[:, b0 + bank, c * P - t0:(c + 1) * P - t0]
                        nc.tensor.matmul(out, v[:, c, h * P:(h + 1) * P], att[:, ((h % 2) * 2 + h // 2) * NC + c, :], start=True, stop=False)
                        cols = slice((h // 2) * T + c * CHUNK, (h // 2) * T + (c + 1) * CHUNK)
                        nc.tensor.matmul(out, state[rows, 0, (h // 2) * NC + c, :], e0[rows, cols], start=False, stop=False)
                        last = nc.tensor.matmul(out, state[rows, 1, (h // 2) * NC + c, :], e1[rows, cols], start=False, stop=True)
                got = p.pe(last)
                o = comb[:, (h % 2) * T:(h % 2 + 1) * T]
                p.wait("act", got, read, free_o[h % 2])
                for t0, tn, bank in segments(T):
                    copied = p.act(nc.scalar.activation(o[:, t0:t0 + tn], self.ps[:, b0 + bank, 0:tn], ACT.Copy))
                p.wait("act", copied)
                for t0, tn, bank in segments(T):
                    i = self.next_tmp()
                    p.wait("act", *self.tmp_free[i])
                    squared = p.act(nc.scalar.activation(self.tmp[i][:, 0:tn], o[:, t0:t0 + tn], ACT.Square))
                    p.wait("pe", squared)
                    summed = p.pe(nc.tensor.matmul(self.ps[:, b0 + bank, 0:tn], self.ones[:, :], self.tmp[i][:, 0:tn],
                                                   start=True, stop=True))
                    self.tmp_free[i] = [summed]
                p.wait("act", summed, self.rstd_free)
                for t0, tn, bank in segments(T):
                    logs = p.act(nc.scalar.activation(self.rstd[:, t0:t0 + tn], self.ps[:, b0 + bank, 0:tn], ACT.Ln,
                                                      scale=1.0 / P, bias=self.col(EPS_COL[EPS])))
                p.wait("act", logs)
                roots = p.act(nc.scalar.activation(self.rstd[:, :], self.rstd[:, :], ACT.Exp, scale=-0.5))
                p.wait("dve", roots, silu)
                made = self.rstd_free = p.dve(nc.vector.scalar_tensor_tensor(o, o, self.col("ggla", h), self.rstd[:, :], ALU.mult, ALU.mult))
                p.wait("dve", made)
                made = p.dve(nc.vector.tensor_tensor(o, o, z[:, 4 + h, :], ALU.mult))
                self.h_done = self.split(4 + h, 0, T, o, made)
                free_o[h % 2] = self.h_done
            self.att_free = [self.h_done, self.h_done]

    def attention(self):
        p, nc, ins = self.p, self.nc, self.ins
        T, NH, NKV, NT = TALL, 8, 2, LAT // P
        NS = T // P
        with ExitStack() as ctx:
            sb = lambda name, shape, dt=F32: ctx.enter_context(nc.sbuf_tensor(name, shape, dt))
            q, k = sb("aq", [P, NH, LAT]), sb("ak", [P, NKV, T])
            v = sb("av", [P, NS, NKV * P])
            cos, sin, rot = sb("acos", [P, LAT]), sb("asin", [P, LAT]), sb("arot", [P, P])
            s, pt = sb("ascores", [P, 2, NT, T]), sb("aprobs", [P, NS, LAT])
            nm, rs = sb("anm", [P, 2 * NT]), sb("ars", [P, 2 * NT])
            turned = sb("aturn", [P, LAT])
            o = sb("ao", [P, 2, LAT])
            self.z_free = self.h_done
            self.load(cos[:, :], ins["cos2"], self.h_done)
            self.load(sin[:, :], ins["sin2"])
            loaded = self.load(rot[:, :], ins["rot2"])
            self.straight("qkv", 0, 8, LAT, self.keep(q, LAT), act=2)
            self.straight("qkv", 8, 2, T, self.keep(k, T), act=4)
            vf = s[:, 0, 0:2, :]
            self.straight("qkv", 10, 2, T, self.keep(vf, T))
            z_done = self.z_done
            for f in range(2):
                units = [(slice(0, P), slice(t * P, (t + 1) * P)) for t in range(NS)]
                self.transposes(v[:, :, f * P:(f + 1) * P], vf[:, f, :], units, z_done)
            z_done = self.evicted
            h_read = self.free_hl[1 - self.tile % 2]
            parts = [(k[:, j, t0:t0 + tn], self.col("gk")) for j in range(NKV) for t0, tn, _ in segments(T)]
            parts += [(q[:, h, :], self.col("gq")) for h in range(NH)]
            places = [pt[:, :, :].rearrange("p j t -> p (j t)"), s[:, 1, :, :].rearrange("p t k -> p (t k)")]
            roots, rooted, logs, summed = [], [], [z_done] * 4, []
            for i in range(len(parts) + 1):
                if i < len(parts):
                    x, tmp_i = parts[i][0], self.next_tmp()
                    tn = x.shape[1]
                    t = self.tmp[tmp_i][:, 0:tn]
                    p.wait("act", z_done, *self.tmp_free[tmp_i])
                    squared = p.act(nc.scalar.activation(t, x, ACT.Square))
                    p.wait("pe", squared, logs[i % 4])
                    summed.append(p.pe(nc.tensor.matmul(self.ps[:, 4 + i % 4, 0:tn], self.ones[:, :], t, start=True, stop=True)))
                    self.tmp_free[tmp_i] = [summed[i]]
                if i == 0:
                    continue
                i -= 1
                tn = parts[i][0].shape[1]
                root = places[i // 6][:, (i % 6) * LAT:(i % 6) * LAT + tn]
                p.wait("act", summed[i])
                logs[i % 4] = p.act(nc.scalar.activation(root, self.ps[:, 4 + i % 4, 0:tn], ACT.Ln, scale=1.0 / P, bias=self.col("eps6")))
                roots.append(root)
                if i % 6 == 5:
                    p.wait("act", logs[i % 4])
                    for root in roots[-6:]:
                        rooted.append(p.act(nc.scalar.activation(root, root, ACT.Exp, scale=-0.5)))
            rotated = [rooted[-1], rooted[-1]]
            roped = None

            def normalize(i):
                x, gain = parts[i]
                p.wait("dve", rooted[i])
                return p.dve(nc.vector.scalar_tensor_tensor(x, x, gain, roots[i], ALU.mult, ALU.mult))

            def rotate(i, b):
                nonlocal roped
                x = parts[i][0]
                p.wait("pe", normed[i], loaded, rotated[b], free_o[b])
                got = p.pe(nc.tensor.matmul(self.ps[:, 6 + b, :], rot[:, :], x, start=True, stop=True))
                p.wait("dve", got, loaded, roped)
                rotated[b] = p.dve(nc.vector.tensor_tensor(turned[:, :], self.ps[:, 6 + b, :], sin[:, :], ALU.mult))
                own = p.dve(nc.vector.tensor_tensor(x, x, cos[:, :], ALU.mult))
                p.wait("dve", rotated[b], own)
                roped = p.dve(nc.vector.tensor_tensor(x, x, turned[:, :], ALU.add))
                return roped

            free_s, free_pt, free_o = [None, None], None, [None, None]
            free_bank, free_t = [z_done, z_done], [logs[0], logs[1]]
            first = len(parts) - NH
            normed = [normalize(i) for i in range(len(parts))]
            for i in range(1, first, 2):
                keys = rotate(i, i // 2)
            queries = [rotate(first + h, h) for h in range(2)] + [None] * (NH - 2)
            probs = [None, None]

            def scores(h, t):
                sl, bank = h % 2, 2 * (t % 2)
                p.wait("pe", keys, queries[h], free_bank[t % 2], *self.free_ps[t % 2])
                for i in range(2):
                    last = nc.tensor.matmul(self.ps[:, bank + i, 0:T // 2], q[:, h, t * P:(t + 1) * P],
                                            k[:, h // 4, i * (T // 2):(i + 1) * (T // 2)], start=True, stop=True)
                scored = p.pe(last)
                got = self.ps[:, bank:bank + 2, 0:T // 2]
                sc = s[:, sl, t, :]
                at = slice(sl * NT + t, sl * NT + t + 1)
                p.wait("dve", scored, free_s[sl])
                made = p.dve(nc.vector.tensor_reduce(nm[:, at], got, AX.XY, ALU.max))
                p.wait("dve", made)
                made = p.dve(nc.vector.tensor_scalar(nm[:, at], nm[:, at], -(P ** -0.5), None, ALU.mult))
                p.wait("act", made)
                made = free_bank[t % 2] = p.act(nc.scalar.activation(sc.rearrange("p (i k) -> p i k", i=2), got, ACT.Exp,
                                                scale=P ** -0.5, bias=nm[:, at], accum_out=rs[:, at]))
                p.wait("dve", made)
                made = p.dve(nc.vector.reciprocal(rs[:, at], rs[:, at]))
                p.wait("dve", made)
                probs[sl] = p.dve(nc.vector.tensor_scalar(sc, sc, rs[:, at], None, ALU.mult))

            for t in range(NT):
                scores(0, t)
            for h in range(NH):
                sl = h % 2
                ready = probs[sl]
                for j in range(NS):
                    p.wait("pe", ready, free_t[j % 2])
                    for t in range(NT):
                        last = nc.tensor.matmul(self.ps[:, 4 + j % 2, t * P:(t + 1) * P], s[:, sl, t, j * P:(j + 1) * P],
                                                self.ident[:, :], is_transpose=True, start=True, stop=True)
                    got = p.pe(last)
                    if j % 2:
                        p.wait("dve", got, free_pt)
                        free_t[1] = p.dve(nc.vector.tensor_copy(pt[:, j, :], self.ps[:, 5, :]))
                    else:
                        p.wait("act", got, free_pt, normed[-1])
                        free_t[0] = p.act(nc.scalar.activation(pt[:, j, :], self.ps[:, 4, :], ACT.Copy))
                    if h + 1 < NH and j < NT:
                        scores(h + 1, j)
                free_s[sl] = got
                if h + 2 < NH:
                    queries[h + 2] = rotate(first + h + 2, sl)
                p.wait("pe", free_t[0], free_t[1], free_o[sl], rotated[sl])
                for j in range(NS):
                    last = nc.tensor.matmul(self.ps[:, 6 + sl, :], v[:, j, (h // 4) * P:(h // 4 + 1) * P], pt[:, j, :],
                                            start=j == 0, stop=j == NS - 1)
                mixed = free_pt = p.pe(last)
                p.wait("act", mixed, free_o[sl], h_read)
                copied = p.act(nc.scalar.activation(o[:, sl, :], self.ps[:, 6 + sl, :], ACT.Copy))
                free_o[sl] = self.h_done = self.split(h, CTX, LAT, o[:, sl, :], copied)
            self.att_free = [self.h_done, self.h_done]
            self.free_ps = [[self.h_done], [self.h_done]]
            self.sums = Sums(self, LAT, True)
            self.straight("attout", 0, KD, LAT, self.residual(1, 1, 2, LAT), dve=2)

    def final_norm(self):
        p, nc = self.p, self.nc
        self.add_sums()
        rstd = self.reciprocal_root(self.rstd[:, LATS], self.ps[:, 6, 0:LAT], D, EPS, self.sums.done)
        p.wait("dve", rstd)
        for f in range(KD):
            x = self.x[:, f, LATS]
            made = p.dve(nc.vector.scalar_tensor_tensor(x, x, self.col("gfin", f), self.rstd[:, LATS], ALU.mult, ALU.mult))
            p.wait("sp", made)
            stored = p.done("store", nc.sync.dma_start(self.out[:, f, :], x), 16)
        p.wait("sp", stored)


def build(nc, ins, out):
    with ExitStack() as ctx:
        k = Stages(nc, ctx, ins, out)
        k.att_free, k.z_free = [None, None], None
        k.constants()
        k.condition_start()
        k.first_tiles()
        k.x_tile = [k.consts] * KD
        k.x_done = k.consts
        k.modulate_first()
        k.even_mixer1()
        k.layer_norm(0, 0, 3)
        half = JOBS // 2
        k.ffn(0, 0, LAT, Sums(k, LAT, False), [
            lambda space: Modulations(space, 0, 1, 0, half, [0]),
            lambda space: Modulations(space, 1, 0, 0, KD, [1, 2]),
            lambda space: Modulations(space, 0, 1, half, half, [0]),
            lambda space: Modulations(space, 1, 0, KD, KD, [1, 2]),
            lambda: k.columns_of(0, 1, [0], 0, NMOD)])
        k.pool_mixer(1, 1)
        k.layer_norm(2, 1, 3)
        k.ffn(0, 1, LAT, Sums(k, LAT, False), [
            lambda space: Modulations(space, 1, 1, 0, half, [1, 2]),
            lambda space: Modulations(space, 1, 0, 2 * KD, KD, [1, 2]),
            lambda space: Modulations(space, 1, 1, half, half, [2]),
            lambda space: Modulations(space, 1, 0, 3 * KD, KD, [1, 2]),
            lambda: (k.columns_of(1, 0, [1, 2], 0, NMOD), k.columns_of(1, 1, [1, 2], 0, 2 * KD),
                     k.columns_of(1, 1, [2], 2 * KD, NMOD))])
        k.layer_norm(3)
        k.sums = Sums(k, TALL, True)
        for f in range(KD):
            k.sums.add(f, k.x_tile[f])
        k.rms_modulate(0, 0, "gmix", TALL)
        k.even_mixer2()
        k.rms_modulate(0, 3, "gffn", TALL)
        k.ffn(1, 0, TALL, Sums(k, TALL, True))
        k.rms_modulate(1, 0, "gmix", TALL)
        k.attention()
        k.rms_modulate(1, 3, "gffn", LAT)
        k.ffn(1, 1, LAT, Sums(k, LAT, True))
        k.final_norm()


def shape_constants():
    c = {"ident": np.eye(P, dtype=np.float32)}
    s, t = np.meshgrid(np.arange(P), np.arange(P), indexing="ij")

    def level_masks(first, second):
        return [((s >> (l + 1)) == (t >> (l + 1))) & (((s >> l) & 1) == first) & (((t >> l) & 1) == second)
                for l in range(LEVELS)]

    fwd, bwd = level_masks(0, 1), level_masks(1, 0)
    pack = lambda ms: np.ascontiguousarray(np.stack(ms, 1).astype(np.int32))
    c["masks1"], c["masks2"] = pack(fwd + [s == t]), pack(fwd + bwd + [s == t])
    for name, n in (("reset1", LAT), ("reset2", TALL)):
        c[name] = np.ascontiguousarray(np.broadcast_to((np.arange(n) % CHUNK != 0).astype(np.float32), (P, n)))
    rel = np.arange(P)[:, None] + P - np.arange(2 * P)[None, :]
    c["wmask"] = np.where((rel >= 0) & (rel < P), 0.0, NEG).astype(np.float32)
    rot1 = np.zeros((P, 3, P), np.float32)
    for head in (0, 64):
        for i in range(8):
            rot1[head + 8 + i, 0, head + i] = -1.0
            rot1[head + i, 0, head + 8 + i] = 1.0
    for g in range(2):
        for i in range(64):
            rot1[g * 64 + i, 1 + g, i] = rot1[g * 64 + i, 1 + g, 64 + i] = 1.0
    c["rot1"] = rot1
    rot2 = np.zeros((P, P), np.float32)
    for i in range(64):
        rot2[64 + i, i], rot2[i, 64 + i] = -1.0, 1.0
    c["rot2"] = rot2
    recip = np.stack([w / np.minimum(np.arange(WINDOW) + 1.0, w) for w in (2, 4, 8, 16)])
    c["recip"] = np.ascontiguousarray(np.broadcast_to(recip.astype(np.float32), (P, 4, WINDOW)))
    def dft(n):
        a = 2.0 * np.pi * (np.outer(np.arange(n), np.arange(n)) % n) / n
        return np.cos(a), np.sin(a)
    c["dft_f"] = np.concatenate(dft(P), 1).astype(np.float32)
    for name, n in (("dft_lat", LAT), ("dft_ctx", CTX)):
        cn, sn = dft(n)
        m = np.stack([cn, -sn]) / np.sqrt(n * P)
        c[name] = np.ascontiguousarray(m.reshape(2, n // P, P, n).transpose(2, 0, 1, 3).astype(np.float32))
    inv = (10000.0 ** (-np.arange(0, 64, 2, dtype=np.float32) / 64)).astype(np.float32)
    r, col = np.meshgrid(np.arange(LAT // 64), np.arange(64), indexing="ij")
    ang = np.concatenate([r.reshape(-1, 1).astype(np.float32) * inv, col.reshape(-1, 1).astype(np.float32) * inv], -1)
    for name, fn in (("cos2", np.cos), ("sin2", np.sin)):
        c[name] = np.ascontiguousarray(np.concatenate([fn(ang), fn(ang)], 1).T.astype(np.float32))
    inv1 = (500000.0 ** (-np.arange(0, 16, 2, dtype=np.float32) / 16)).astype(np.float32)
    per = np.zeros(64, np.float32)
    per[0:8] = per[8:16] = inv1
    c["inv_freq"] = np.concatenate([per, per]).reshape(P, 1)
    return c


def tiles(w, pad=None):
    rows, cols = w.shape
    return w.reshape(rows // P, P, cols // P, P).transpose(2, 1, 0, 3).reshape(cols // P, P, (rows // P) * P)


def columns(a):
    return np.moveaxis(a.reshape(*a.shape[:-1], a.shape[-1] // P, P), -1, 0).reshape(P, -1)


def layout(inputs):
    g = {n: np.asarray(a) for n, a in inputs.items()}
    c = shape_constants()
    a = {n: v for n, v in c.items() if n != "inv_freq"}
    a["x"] = g["x"][0].T.reshape(KD, P, LAT).transpose(1, 0, 2)
    a["ctx"] = g["ctx_2"][0].T.reshape(KD, P, CTX).transpose(1, 0, 2)
    a["positions"] = g["positions"].reshape(1, LAT)
    parts = {
        "c1": columns(g["c"][0]), "c2": columns(g["c_2"][0]), "cc2": columns(g["c_ctx_2"]),
        "ada_b": columns(g["ada_b"]), "mod_b": columns(g["b_mod_2"]), "ln_g": columns(g["ln_g"]), "ln_b": columns(g["ln_b"]),
        "lb_raw": columns(g["hgrn_lb_raw"]), "norm_g": columns(g["hgrn_norm_g"]), "pool_scale": columns(g["pool_scale"]),
        "fcw": columns(g["ffn_conv_w"]), "fcb": columns(g["ffn_conv_b"]), "gmix": columns(g["g_norm_mix_2"]),
        "gffn": columns(g["g_norm_ffn_2"]), "gfin": columns(g["g_norm_final_2"]), "bgate": columns(g["b_gla_gate_2"]),
        "ggla": columns(g["g_gla_out_2"]), "gq": columns(g["g_q_2"]), "gk": columns(g["g_k_2"]),
        "cw2": columns(g["w_ffn_conv_2"].reshape(2, 3, 2, F_FF).transpose(0, 2, 1, 3)),
        "cb2": columns(g["b_ffn_conv_2"]), "inv_freq": c["inv_freq"],
        "eps5": np.full((P, 1), LN_EPS, np.float32), "eps6": np.full((P, 1), EPS, np.float32),
        "sinks": np.broadcast_to(g["attn_sinks"][:, HEAD_ORDER], (P, 8)),
    }
    a["small"] = np.concatenate([parts[n] for n in SMALL], 1)
    for name, w in (("ada_w", g["ada_w"]), ("w_mod", g["w_mod_2"])):
        t = w.reshape(2, KD, P, JOBS, JW).transpose(0, 3, 2, 1, 4).reshape(2 * JOBS, P, KD * JW)
        a[name] = np.concatenate([t, np.zeros((2, P, KD * JW), np.float32)])
    w = g["ab_w_in"][0]
    a["in1"] = tiles(np.concatenate([w[:, 0:1024], w[:, 1536:2048], w[:, 2048:2816], w[:, 1024:1536]], 1))
    a["out1"] = tiles(g["ab_w_out"][0])
    a["pool"] = np.concatenate([tiles(g["pool_w"][0, i]) for i in range(4)])
    for name, up, down in (("0", g["ffn_w_up"], g["ffn_w_down"]), ("1", g["w_ffn_up_2"], g["w_ffn_down_2"])):
        for layer in range(2):
            t = tiles(up[layer])
            a[f"up{name}{layer}"] = t.reshape(2, FT, P, D).transpose(1, 0, 2, 3).reshape(2 * FT, P, D)
            a[f"down{name}{layer}"] = np.concatenate([tiles(down[layer][h * FG * P:(h + 1) * FG * P]) for h in range(2)])
    w = g["w_even_in_2"][0]
    low = np.concatenate([w[:, 2048:2064], np.zeros((D, P - 16), np.float32)], 1)
    a["in2"] = tiles(np.concatenate([w[:, 512:1024], w[:, 1536:2048], low, w[:, 1024:1536], w[:, 0:512]], 1))
    a["out2"] = tiles(g["w_even_out_2"][0])
    a["w_gate"] = g["w_gla_gate_2"][0].transpose(1, 0, 2).reshape(16, 4, P)
    a["qkv"] = tiles(g["w_qkv_2"][0])
    a["attout"] = tiles(g["w_att_out_2"][0])
    return {n: np.ascontiguousarray(v) for n, v in a.items()}


def kernel(**inputs):
    import concourse.bacc as bacc
    from concourse.bass_utils import run_bass_kernel_spmd

    nc = bacc.Bacc("TRN2", target_bir_lowering=False, num_devices=1)
    arrays = layout(inputs)
    ins = {n: nc.dram_tensor(f"in_{n}", v.shape, mybir.dt.from_np(v.dtype), kind="ExternalInput").ap()
           for n, v in arrays.items()}
    out = nc.dram_tensor("out_y", (P, KD, LAT), F32, kind="ExternalOutput").ap()
    build(nc, ins, out)
    r = run_bass_kernel_spmd(nc, [{f"in_{n}": v for n, v in arrays.items()}], core_ids=[0])
    return np.ascontiguousarray(r.results[0]["out_y"].transpose(2, 1, 0).reshape(1, LAT, D))
```
